# Optimizing a Trainium2 kernel written in Bass

```python
import math
import jax
import jax.numpy as jnp
from jax import lax
import numpy as np

D_MODEL = 1024
BATCH = 1
SEQ = 1024
DEPTH = 2

GRID_W = 64
CTX_LEN = 256
HEAD_DIM = 64
A_HEADS = (3 * D_MODEL) // (8 * HEAD_DIM)
A_WIDTH = A_HEADS * HEAD_DIM
B_WIDTH = D_MODEL // 4
HYENA_ORDER = 2
C_HEADS = (3 * D_MODEL) // (8 * HEAD_DIM)
C_KV_HEADS = 2
C_WIDTH = C_HEADS * HEAD_DIM
C_KV_WIDTH = C_KV_HEADS * HEAD_DIM
MIX_WIDTH = A_WIDTH + B_WIDTH + C_WIDTH
SPLIT_SIZES = (A_WIDTH, A_WIDTH, A_WIDTH, A_WIDTH, (HYENA_ORDER + 1) * B_WIDTH, B_WIDTH, C_WIDTH, C_KV_WIDTH, C_KV_WIDTH, C_WIDTH)
IN_WIDTH = 4 * A_WIDTH + (HYENA_ORDER + 2) * B_WIDTH + 2 * C_WIDTH + 2 * C_KV_WIDTH
NA_KH = 8
NA_KW = 16
WINDOW = 128
C_BLOCK = 128
ROPE_BASE = 10000.0
HY_EMB = 33
HY_BANDS = (HY_EMB - 1) // 2
HY_FILTER_WIDTH = 64
HY_SHORT = 3
HY_FAST_DECAY = 0.3
HY_SLOW_DECAY = 1.5
HY_TARGET = 1e-2
RMS_EPS = 1e-6
NEG_INF = -1e30

kernel_name = 'hybrid_natten_hyena_swa_prefix_block'

def rmsnorm(x, g):
    xf = x.astype(jnp.float32)
    y = xf * lax.rsqrt(jnp.mean(xf * xf, axis=-1, keepdims=True) + RMS_EPS)
    return (y * g.astype(jnp.float32)).astype(x.dtype)

def split_proj(p):
    parts, start = [], 0
    for size in SPLIT_SIZES:
        parts.append(p[..., start:start + size])
        start += size
    return parts

def to_heads(t, n_heads):
    return t.reshape(t.shape[:-1] + (n_heads, HEAD_DIM))

def rope_1d(x, pos):
    half = x.shape[-1] // 2
    inv = ROPE_BASE ** (-jnp.arange(half, dtype=jnp.float32) / half)
    ang = pos.astype(jnp.float32)[:, None] * inv[None, :]
    cos = jnp.cos(ang)[:, None, :]
    sin = jnp.sin(ang)[:, None, :]
    xf = x.astype(jnp.float32)
    x1, x2 = xf[..., :half], xf[..., half:]
    return jnp.concatenate([x1 * cos - x2 * sin, x2 * cos + x1 * sin], axis=-1).astype(x.dtype)

def rope_2d(x, row, col):
    half = HEAD_DIM // 2
    return jnp.concatenate([rope_1d(x[..., :half], row), rope_1d(x[..., half:], col)], axis=-1)

def attend_context(q, k, v, sink):
    bsz, lq, nh, dh = q.shape
    nkv = k.shape[2]
    lk = k.shape[1]
    qg = q.reshape(bsz, lq, nkv, nh // nkv, dh)
    s = jnp.einsum('bqkgd,bmkd->bkgqm', qg, k).astype(jnp.float32) * (dh ** -0.5)
    if sink is not None:
        s_sink = jnp.broadcast_to(sink.astype(jnp.float32).reshape(1, nkv, nh // nkv, 1, 1), s.shape[:-1] + (1,))
        s = jnp.concatenate([s, s_sink], axis=-1)
    p = jax.nn.softmax(s, axis=-1)[..., :lk].astype(v.dtype)
    o = jnp.einsum('bkgqm,bmkd->bqkgd', p, v)
    return o.reshape(bsz, lq, nh * dh)

def neighbourhood_attention(q, k, v, k_ctx, v_ctx, rpb):
    bsz, seq, nh, dh = q.shape
    rows = seq // GRID_W
    kh = min(NA_KH, rows)
    kw = NA_KW
    scale = dh ** -0.5
    qg = q.reshape(bsz, rows, GRID_W, nh, dh)
    kg = k.reshape(bsz, rows, GRID_W, nh, dh)
    vg = v.reshape(bsz, rows, GRID_W, nh, dh)
    col = jnp.arange(GRID_W)
    c0 = jnp.clip(col - kw // 2, 0, GRID_W - kw)
    col_idx = c0[:, None] + jnp.arange(kw)[None, :]
    rel_col = col_idx - col[:, None] + (NA_KW - 1)
    bias_cols = rpb[:, :, rel_col]

    def row_block(r):
        r0 = jnp.clip(r - kh // 2, 0, rows - kh)
        q_r = lax.dynamic_index_in_dim(qg, r, axis=1, keepdims=False)
        k_r = lax.dynamic_slice_in_dim(kg, r0, kh, axis=1)[:, :, col_idx]
        v_r = lax.dynamic_slice_in_dim(vg, r0, kh, axis=1)[:, :, col_idx]
        rel_row = r0 + jnp.arange(kh) - r + (NA_KH - 1)
        bias = bias_cols[:, rel_row].transpose(0, 2, 1, 3)
        s_nb = jnp.einsum('bjhd,bajkhd->bhjak', q_r, k_r).astype(jnp.float32) * scale + bias[None].astype(jnp.float32)
        s_nb = s_nb.reshape(bsz, nh, GRID_W, kh * kw)
        s_cx = jnp.einsum('bjhd,bmhd->bhjm', q_r, k_ctx).astype(jnp.float32) * scale
        p = jax.nn.softmax(jnp.concatenate([s_nb, s_cx], axis=-1), axis=-1).astype(v.dtype)
        p_nb = p[..., :kh * kw].reshape(bsz, nh, GRID_W, kh, kw)
        p_cx = p[..., kh * kw:]
        return jnp.einsum('bhjak,bajkhd->bjhd', p_nb, v_r) + jnp.einsum('bhjm,bmhd->bjhd', p_cx, v_ctx)

    out = lax.map(row_block, jnp.arange(rows))
    return jnp.moveaxis(out, 0, 1).reshape(bsz, seq, nh * dh)

def window_attention(q, k, v, k_ctx, v_ctx, sink):
    bsz, seq, nh, dh = q.shape
    nkv = k.shape[2]
    g = nh // nkv
    ctx_len = k_ctx.shape[1]
    nblk = seq // C_BLOCK
    span = C_BLOCK + 2 * WINDOW
    scale = dh ** -0.5
    kp = jnp.pad(k, ((0, 0), (WINDOW, WINDOW), (0, 0), (0, 0)))
    vp = jnp.pad(v, ((0, 0), (WINDOW, WINDOW), (0, 0), (0, 0)))
    qb = q.reshape(bsz, nblk, C_BLOCK, nkv, g, dh)
    sink_l = sink.astype(jnp.float32).reshape(1, nkv, g, 1, 1)
    qi = jnp.arange(C_BLOCK)
    mi = jnp.arange(span)

    def block(n):
        start = n * C_BLOCK
        q_n = lax.dynamic_index_in_dim(qb, n, axis=1, keepdims=False)
        k_n = lax.dynamic_slice_in_dim(kp, start, span, axis=1)
        v_n = lax.dynamic_slice_in_dim(vp, start, span, axis=1)
        q_pos = start + qi
        k_pos = start - WINDOW + mi
        valid = (jnp.abs(q_pos[:, None] - k_pos[None, :]) <= WINDOW) & (k_pos >= 0)[None, :] & (k_pos < seq)[None, :]
        s_w = jnp.einsum('bqkgd,bmkd->bkgqm', q_n, k_n).astype(jnp.float32) * scale
        s_w = jnp.where(valid, s_w, NEG_INF)
        s_c = jnp.einsum('bqkgd,bmkd->bkgqm', q_n, k_ctx).astype(jnp.float32) * scale
        s_s = jnp.broadcast_to(sink_l, (bsz, nkv, g, C_BLOCK, 1))
        p = jax.nn.softmax(jnp.concatenate([s_w, s_c, s_s], axis=-1), axis=-1).astype(v.dtype)
        o = jnp.einsum('bkgqm,bmkd->bqkgd', p[..., :span], v_n) + jnp.einsum('bkgqm,bmkd->bqkgd', p[..., span:span + ctx_len], v_ctx)
        return o.reshape(bsz, C_BLOCK, nh * dh)

    out = lax.map(block, jnp.arange(nblk))
    return jnp.moveaxis(out, 0, 1).reshape(bsz, seq, nh * dh)

def hyena_filter_spectrum(L, w1, b1, fr1, w2, b2, fr2, w3):
    f32 = jnp.float32
    t = jnp.linspace(0.0, 1.0, L, dtype=f32)[:, None]
    w = (2.0 * math.pi / L) * jnp.arange(L, dtype=f32)[:, None]
    f = jnp.linspace(1e-4, HY_BANDS - 1, HY_BANDS, dtype=f32)[None, :]
    z = jnp.concatenate([t, jnp.cos(f * w), -jnp.sin(f * w)], axis=-1)
    h = jnp.sin(fr1.astype(f32) * (z @ w1.astype(f32) + b1.astype(f32)))
    h = jnp.sin(fr2.astype(f32) * (h @ w2.astype(f32) + b2.astype(f32)))
    h = (h @ w3.astype(f32)).reshape(L, 2, HYENA_ORDER, B_WIDTH)
    max_decay = math.log(HY_TARGET) / HY_FAST_DECAY
    min_decay = math.log(HY_TARGET) / HY_SLOW_DECAY
    deltas = jnp.abs(jnp.linspace(min_decay, max_decay, B_WIDTH, dtype=f32))
    h = h * jnp.exp(-t * deltas[None, :])[:, None, None, :]
    kern = jnp.concatenate([h[:, 0], jnp.zeros((1, HYENA_ORDER, B_WIDTH), f32), h[1:, 1][::-1]], axis=0)
    kern = kern * lax.rsqrt(jnp.sum(kern * kern, axis=0, keepdims=True) + 1e-6)
    return jnp.fft.rfft(kern, axis=0)

def long_conv(u, spec, d):
    L = u.shape[1]
    uf = u.astype(jnp.float32)
    y = jnp.fft.irfft(jnp.fft.rfft(uf, n=2 * L, axis=1) * spec[None], n=2 * L, axis=1)[:, :L]
    return (y + uf * d.astype(jnp.float32)).astype(u.dtype)

def short_conv(u, w, b):
    up = jnp.pad(u, ((0, 0), (1, 1), (0, 0)))
    return up[:, :-2] * w[0] + up[:, 1:-1] * w[1] + up[:, 2:] * w[2] + b

def hyena_mixer(proj, conv_w, conv_b, spec, d_skip):
    u = short_conv(proj, conv_w, conv_b)
    z, x1, x2 = jnp.split(u, HYENA_ORDER + 1, axis=-1)
    for o, gate in enumerate((x1, x2)):
        z = gate * long_conv(z, spec[:, o], d_skip[o])
    return z

def setup_inputs(seed: int = 0) -> dict:
    key = jax.random.key(seed)
    ks = jax.random.split(key, 22)
    f32 = jnp.float32

    def nrm(k, shape, s):
        return s * jax.random.normal(k, shape, f32)

    return {
        'x': nrm(ks[0], (BATCH, SEQ, D_MODEL), 1.0),
        'c': nrm(ks[1], (BATCH, D_MODEL), 1.0),
        'ctx': nrm(ks[2], (BATCH, CTX_LEN, D_MODEL), 1.0),
        'c_ctx': nrm(ks[3], (D_MODEL,), 1.0),
        'norm_g': 1.0 + nrm(ks[4], (DEPTH, D_MODEL), 0.02),
        'w_ada': nrm(ks[5], (DEPTH, D_MODEL, 3 * D_MODEL), 0.5 * D_MODEL ** -0.5),
        'b_ada': nrm(ks[6], (DEPTH, 3 * D_MODEL), 0.01),
        'w_in': nrm(ks[7], (DEPTH, D_MODEL, IN_WIDTH), D_MODEL ** -0.5),
        'w_out': nrm(ks[8], (DEPTH, MIX_WIDTH, D_MODEL), MIX_WIDTH ** -0.5),
        'na_rpb': nrm(ks[9], (DEPTH, A_HEADS, 2 * NA_KH - 1, 2 * NA_KW - 1), 0.1),
        'hy_conv_w': nrm(ks[10], (DEPTH, HY_SHORT, (HYENA_ORDER + 1) * B_WIDTH), HY_SHORT ** -0.5),
        'hy_conv_b': nrm(ks[11], (DEPTH, (HYENA_ORDER + 1) * B_WIDTH), 0.01),
        'hy_w1': nrm(ks[12], (DEPTH, HY_EMB, HY_FILTER_WIDTH), 1.0),
        'hy_b1': nrm(ks[13], (DEPTH, HY_FILTER_WIDTH), 0.1),
        'hy_freq1': 1.0 + nrm(ks[14], (DEPTH, HY_FILTER_WIDTH), 0.01),
        'hy_w2': nrm(ks[15], (DEPTH, HY_FILTER_WIDTH, HY_FILTER_WIDTH), HY_FILTER_WIDTH ** -0.5),
        'hy_b2': nrm(ks[16], (DEPTH, HY_FILTER_WIDTH), 0.1),
        'hy_freq2': 1.0 + nrm(ks[17], (DEPTH, HY_FILTER_WIDTH), 0.01),
        'hy_w3': nrm(ks[18], (DEPTH, HY_FILTER_WIDTH, 2 * HYENA_ORDER * B_WIDTH), HY_FILTER_WIDTH ** -0.5),
        'hy_d': nrm(ks[19], (DEPTH, HYENA_ORDER, B_WIDTH), 0.3),
        'sink': nrm(ks[20], (DEPTH, C_HEADS), 1.0),
        'final_g': 1.0 + nrm(ks[21], (D_MODEL,), 0.02),
    }

def reference(x, c, ctx, c_ctx, norm_g, w_ada, b_ada, w_in, w_out, na_rpb, hy_conv_w, hy_conv_b, hy_w1, hy_b1, hy_freq1, hy_w2, hy_b2, hy_freq2, hy_w3, hy_d, sink, final_g):
    seq = x.shape[1]
    ctx_len = ctx.shape[1]
    pos = jnp.arange(seq)
    row, col = pos // GRID_W, pos % GRID_W
    cx = ctx
    for l in range(DEPTH):
        last = l == DEPTH - 1
        shift, scale, gate = jnp.split(jax.nn.silu(c) @ w_ada[l] + b_ada[l], 3, axis=-1)
        shift_c, scale_c, gate_c = jnp.split(jax.nn.silu(c_ctx) @ w_ada[l] + b_ada[l], 3, axis=-1)
        h = rmsnorm(x, norm_g[l]) * (1.0 + scale[:, None]) + shift[:, None]
        hc = rmsnorm(cx, norm_g[l]) * (1.0 + scale_c) + shift_c
        qa, ka, va, ga, pb, gb, qc, kc, vc, gc = split_proj(h @ w_in[l])
        cqa, cka, cva, cga, cpb, cgb, cqc, ckc, cvc, cgc = split_proj(hc @ w_in[l])
        filt = (hy_w1[l], hy_b1[l], hy_freq1[l], hy_w2[l], hy_b2[l], hy_freq2[l], hy_w3[l])
        ka_ctx, va_ctx = to_heads(cka, A_HEADS), to_heads(cva, A_HEADS)
        kc_ctx, vc_ctx = to_heads(ckc, C_KV_HEADS), to_heads(cvc, C_KV_HEADS)
        y_a = neighbourhood_attention(to_heads(qa, A_HEADS), to_heads(ka, A_HEADS), to_heads(va, A_HEADS), ka_ctx, va_ctx, na_rpb[l])
        y_b = hyena_mixer(pb, hy_conv_w[l], hy_conv_b[l], hyena_filter_spectrum(seq, *filt), hy_d[l])
        y_c = window_attention(rope_2d(to_heads(qc, C_HEADS), row, col), rope_2d(to_heads(kc, C_KV_HEADS), row, col), to_heads(vc, C_KV_HEADS), kc_ctx, vc_ctx, sink[l])
        y = jnp.concatenate([y_a * jax.nn.silu(ga), y_b * jax.nn.silu(gb), y_c * jax.nn.silu(gc)], axis=-1) @ w_out[l]
        x_next = x + gate[:, None] * y
        if not last:
            yc_a = attend_context(to_heads(cqa, A_HEADS), ka_ctx, va_ctx, None)
            yc_b = hyena_mixer(cpb, hy_conv_w[l], hy_conv_b[l], hyena_filter_spectrum(ctx_len, *filt), hy_d[l])
            yc_c = attend_context(to_heads(cqc, C_HEADS), kc_ctx, vc_ctx, sink[l])
            yc = jnp.concatenate([yc_a * jax.nn.silu(cga), yc_b * jax.nn.silu(cgb), yc_c * jax.nn.silu(cgc)], axis=-1) @ w_out[l]
            cx = cx + gate_c * yc
        x = x_next
    return rmsnorm(x, final_g)


_drawn_inputs = setup_inputs


def setup_inputs(seed=0):
    import zlib

    import numpy as np

    out = dict(_drawn_inputs(seed))
    spreads = {}
    factors = {'ctx': 3.101,
     'norm_g': 4.897,
     'b_ada': 3.219,
     'na_rpb': 53.8,
     'hy_conv_b': 5.076,
     'hy_freq1': 2.859,
     'hy_freq2': 8.0,
     'sink': 8.0,
     'final_g': 7.619}
    for name, (base, spread) in spreads.items():
        noise = np.random.default_rng([zlib.crc32(name.encode()), seed]).standard_normal(out[name].shape)
        drawn = base * np.exp(spread * noise) if base else spread * noise
        out[name] = jnp.asarray(drawn.astype(out[name].dtype))
    for name, factor in factors.items():
        out[name] = (out[name] * factor).astype(out[name].dtype)
    return out
```

```python
import math
from contextlib import ExitStack

import numpy as np

import concourse.bass as bass
from concourse import mybir

F32 = mybir.dt.float32
ALU = mybir.AluOpType
ACT = mybir.ActivationFunctionType

P = 128
D = 1024
KC = D // P
SEQ, CTX = 1024, 256
TOK = SEQ + CTX
NT, NTC = SEQ // P, CTX // P
DEPTH = 2
GRID = 64
CH = 256
HD = 64
QSCALE = HD ** -0.5
EPS = 1e-6
NEG = -1e30
LOWEST = -3.0e38

N_ADA, N_PB, N_Q, N_K, N_V, N_G, N_OUT = 24, 6, 6, 4, 4, 8, 8
RING = 4
STREAM = [(0, "ada", N_ADA), (0, "pb", N_PB), (0, "g", N_G), (1, "ada", N_ADA), (0, "q", N_Q), (0, "k", N_K),
          (0, "v", N_V), (0, "out", N_OUT), (1, "pb", N_PB), (1, "g", N_G), (1, "q", N_Q), (1, "k", N_K),
          (1, "v", N_V), (1, "out", N_OUT)]
N_STREAM = sum(n for _, _, n in STREAM)
STREAM_AT = {(l, name): sum(n for _, _, n in STREAM[:i]) for i, (l, name, n) in enumerate(STREAM)}
assert N_STREAM % RING == 0 and all(a % 2 == 0 for a in STREAM_AT.values())

MIX_B, MIX_A, MIX_C = 0, 2, 5
C_HEAD_ORDER = (0, 3, 1, 4, 2, 5)

SLOT_R = (0, 8, 4, 2, 6, 1, 3, 7, 5)
NS_MAIN, NS_CTX = 9, 3
DFT_START = [0, 2, 4, 7, 10, 13, 16, 19, 22]
N_DFT = 25
SQ5, C1, S1 = math.sqrt(0.5), math.cos(math.pi / 8), math.sin(math.pi / 8)

TWO_PI_A, TWO_PI_B = 6.28125, 0.0019340515136718750
TWO_PI_C = 2 * math.pi - TWO_PI_A - TWO_PI_B
ROUND = 12582912.0


def dft_tables():
    p = np.arange(P, dtype=np.float64)
    fwd, inv = [], []
    for slot, r in enumerate(SLOT_R):
        theta = 2 * np.pi * (p[:, None] * r / 2048 + p[:, None] * p[None, :] / P)
        c, s = np.cos(theta), np.sin(theta)
        g = (1.0 if r in (0, 8) else 2.0) / 2048
        fwd += [c, -s] if slot < 2 else [c, s, -s]
        inv += [g * c.T, -g * s.T] if slot < 2 else [g * c.T, g * s.T, -g * s.T]
    pack = lambda m: np.stack(m, 1).astype(np.float32)
    return pack(fwd), pack(inv)


def rope_tables():
    pos = np.arange(SEQ)
    row, col = pos // GRID, pos % GRID
    inv = 10000.0 ** (-np.arange(16) / 16.0)
    cos, sin = np.zeros((P, SEQ)), np.zeros((P, SEQ))
    for d in range(P):
        e = d % HD
        ang = (row if e < 32 else col) * inv[e % 16]
        cos[d] = np.cos(ang)
        sin[d] = np.sin(ang) * (-1 if e % 32 < 16 else 1)
    return cos.astype(np.float32), sin.astype(np.float32)


def attention_masks():
    c = np.arange(GRID)
    c0 = np.clip(c - 8, 0, GRID - 16)
    ok = (c[None, :] >= c0[:, None]) & (c[None, :] < c0[:, None] + 16)
    cols = np.where(ok, 0, NEG)
    cols = np.concatenate([cols, cols]).astype(np.float32)
    rows = np.zeros((P, 10, GRID), np.float32)
    for par in range(2):
        for i in range(10):
            dr = i - 4 - par
            if not -4 <= dr <= 3:
                rows[64 * par:64 * par + 64, i] = NEG
    q, k = np.arange(P)[:, None], np.arange(3 * P)[None, :] - P
    window = np.where(np.abs(q - k) <= 128, 0, NEG).astype(np.float32)
    return cols, rows.reshape(P, 640), window


def filter_tables(L):
    t = np.linspace(0.0, 1.0, L, dtype=np.float32)
    w = (np.float32(2.0 * math.pi / L) * np.arange(L, dtype=np.float32)).astype(np.float32)
    f = np.linspace(1e-4, 15, 16, dtype=np.float32)
    a = (f[:, None] * w[None, :]).astype(np.float32).astype(np.float64)
    z = np.concatenate([t[None].astype(np.float64), np.cos(a), -np.sin(a)], 0)
    back = (L - np.arange(L)) % L
    feats = np.concatenate([z, z[:, back]], 0).astype(np.float32)
    lo, hi = math.log(1e-2) / 1.5, math.log(1e-2) / 0.3
    deltas = np.abs(np.linspace(lo, hi, CH, dtype=np.float32)).astype(np.float64)
    dec = np.exp(-t.astype(np.float64)[:, None] * deltas[None])
    late = dec[back]
    late[0] = 0.0
    both = np.concatenate([dec, late], 0).reshape(2 * L // P, P, CH)
    return feats, both.transpose(1, 0, 2).astype(np.float32)


def build(nc, A):
    ctx = ExitStack()
    with ctx:
        def sb(name, shape):
            return ctx.enter_context(nc.sbuf_tensor(name, shape, F32))

        act_t = sb("act_t", [P, KC, TOK])
        mix = sb("mix", [P, KC, TOK])
        ring = sb("ring", [P, RING, KC, P])
        R_SIZE = 26000
        region = sb("region", [P, R_SIZE])
        ident = sb("ident", [P, P])
        ones = sb("ones", [P, P])
        condT = sb("condT", [P, KC, 2])
        silu_c = sb("silu_c", [P, KC, 2])
        norm_g = sb("norm_g", [P, DEPTH + 1, KC])
        b_ada = sb("b_ada", [P, DEPTH, N_ADA])
        ada = sb("ada", [P, DEPTH, N_ADA, 2])
        mod_a = sb("mod_a", [P, KC, 2])
        conv_w = sb("conv_w", [P, DEPTH, N_PB, 4])
        f_small = sb("f_small", [P, DEPTH, 4])
        sink = sb("sink", [P, DEPTH, 6])
        ps = ctx.enter_context(nc.psum_tensor("ps", [P, 8, 512], F32))

        def view(start, *shape):
            n = int(np.prod(shape))
            assert start + n <= R_SIZE, (start, shape)
            v = region[:, start:start + n]
            if len(shape) == 2:
                v = v.rearrange("p (a b) -> p a b", b=shape[1])
            if len(shape) == 3:
                v = v.rearrange("p (a b c) -> p a b c", b=shape[1], c=shape[2])
            return v

        sq = view(0, 3, 512)
        rstd = view(1536, TOK)
        spec = view(0, NS_MAIN, 2, CH)
        khat = view(4608, NS_MAIN, 2, CH)
        decay = view(4608, 2 * NT, CH)
        z_tm = view(9216, NT + NTC, CH)
        x1_tm = view(11776, NT + NTC, CH)
        dft_f = view(14336, N_DFT, P)
        dft_i = view(17536, N_DFT, P)
        PAD = TOK + 4
        pc_in = view(20736, 2, PAD)
        pc_out = view(20736 + 2 * PAD, 2, PAD)
        hid = view(20736, SEQ)
        w3f = view(21760, 2 * CH)
        w3r = view(22272, 2 * CH)
        k_rt = view(22784, CH)
        k_s = view(23040, CH)
        prod = view(23296, 2, 2, 2 * CH)
        w12 = view(25344, 2, P)
        mlp = [view(1024 * i, SEQ) for i in range(3)]
        feats = view(3072, SEQ)
        d_row = view(25600, CH)
        g_st = sb("g_st", [P, 2, 512])
        room = mix[:, 2:8, :].rearrange("p a b -> p (a b)").rearrange("p (u c) -> p u c", c=CH)
        k_fm = view(0, N_K, TOK)
        v_tm = view(5120, NT + NTC, 512)
        t_raw = view(10240, 6, 14, GRID)
        rope_cs = view(10240, 2, SEQ)
        rope_t = view(12288, 2, SEQ)
        t_edge = view(15616, 2, 896)
        t_inner = view(17408, 2, 640)
        s_sb = view(18688, 2, 896)
        p_sb = view(20480, 2, 896)
        pt_sb = view(22272, 2, 896)
        q_st = view(24064, 2, 2, P)
        o_sb = view(24576, 2, P)
        m_cols = view(24832, GRID)
        m_rows = view(24896, 640)
        m_win = view(25536, 3 * P)
        stat = view(25920, 32)
        g_in = view(15616, 2, TOK)
        x_in = view(0, 2, TOK)
        fin = view(2560, 2, SEQ)

        def sem(name):
            return ctx.enter_context(nc.semaphore(name))

        L2 = range(DEPTH)

        def per_layer(name):
            return [sem(f"{name}{l}") for l in L2]

        consts_in, consts_set, x_loaded, silu_ready = sem("consts_in"), sem("consts_set"), sem("x_loaded"), sem("silu_ready")
        slot_in = [sem(f"slot_in{s}") for s in range(RING)]
        block_done = sem("block_done")
        block_taken = sem("block_taken")
        sq_ready = [sem(f"sq_ready{l}") for l in range(DEPTH + 1)]
        sq_used = [sem(f"sq_used{l}") for l in range(DEPTH + 1)]
        ms_ready, std_ready = sem("ms_ready"), sem("std_ready")
        ada_ready, scaled, h_ready = sem("ada_ready"), per_layer("scaled"), per_layer("h_ready")
        pads_set, dft_in, pc_ready, conv_ready = sem("pads_set"), per_layer("dft_in"), per_layer("pc_ready"), per_layer("conv_ready")
        tp_ready, tp_taken = per_layer("tp_ready"), per_layer("tp_taken")
        fl_in, dec_in, drow_in = per_layer("fl_in"), per_layer("dec_in"), per_layer("drow_in")
        mlp_mm, arg_ready, hid_ready = per_layer("mlp_mm"), per_layer("arg_ready"), per_layer("hid_ready")
        tap_mm, tap_ready, tsq_ready, tsq_used = (per_layer(x) for x in ("tap_mm", "tap_ready", "tsq_ready", "tsq_used"))
        en_ready, rt_ready = per_layer("en_ready"), per_layer("rt_ready")
        bf_ready, x_mm, x_taken, prod_ready = (per_layer(x) for x in ("bf_ready", "x_mm", "x_taken", "prod_ready"))
        y_part, w_mm, w_taken = (per_layer(x) for x in ("y_part", "w_mm", "w_taken"))
        yt_ready, yt_mm, yt_taken, hyena_done = (per_layer(x) for x in ("yt_ready", "yt_mm", "yt_taken", "hyena_done"))
        v_mm, v_taken, rope_in, rope_done = (per_layer(x) for x in ("v_mm", "v_taken", "rope_in", "rope_done"))
        masks_in, traw_in, qst_zero = per_layer("masks_in"), per_layer("traw_in"), sem("qst_zero")
        qst_ready, s_ready, neg_ready, p_ready = sem("qst_ready"), sem("s_ready"), sem("neg_ready"), sem("p_ready")
        es_ready, pt_ready, pt_dve, pt_act = sem("es_ready"), sem("pt_ready"), sem("pt_dve"), sem("pt_act")
        o_ready, on_ready, ot_ready, ot_taken = sem("o_ready"), sem("on_ready"), sem("ot_ready"), sem("ot_taken")
        unit_step = sem("unit_step")
        g_mm, g_taken, mix_gated = (per_layer(x) for x in ("g_mm", "g_taken", "mix_gated"))
        g_stored = [[sem(f"g_stored{l}_{b}") for b in range(2)] for l in L2]
        g_in_in = [[sem(f"g_in_in{l}_{b}") for b in range(2)] for l in L2]
        xin_in = [[sem(f"xin_in{l}_{b}") for b in range(2)] for l in L2]
        x_stored, fin_ready = sem("x_stored"), sem("fin_ready")
        fin_out = [sem(f"fin_out{b}") for b in range(2)]
        vec_step = sem("vec_step")

        stat_h = view(R_SIZE - 8, 8)

        def back_tiles(isctx):
            return [(b, NT, NTC) for b in range(2)] if isctx else [(b, t, 4) for b in range(2) for t in (0, 4)]

        class Steps:
            def __init__(self, eng):
                self.eng, self.open, self.at = eng, {}, {}

            def __call__(self, ins, sem=None):
                s = vec_step if sem is None else sem
                self.at[s.name] = self.at.get(s.name, 0) + 1
                ins.then_inc(s, 1)
                self.open[s.name] = (s, self.at[s.name])

            def join(self):
                for s, n in self.open.values():
                    self.eng.wait_ge(s, n)
                self.open = {}

        def ntok(l):
            return TOK if l == 0 else SEQ

        def groups(n):
            return [(t, min(512, n - t)) for t in range(0, n, 512)]

        TAKEN = N_PB + N_Q + N_K + N_OUT

        def taken_before(l, stage):
            return l * TAKEN + dict(pb=0, q=N_PB, k=N_PB + N_Q, out=TAKEN - N_OUT, end=TAKEN)[stage]

        def gate_parts(l):
            return [(b, t, w) for b in range(N_G) for t, w in groups(ntok(l))]

        def done_at(l, stage):
            return STREAM_AT[l, stage]

        def fills(l, isctx):
            return (1, 0, 1, 2) if isctx else (2, 3, 1, 3) if l == 0 else (2, 3, 0, 3)

        def time_tiles(l):
            return [(0, 4), (4, 4), (8, 2)] if l == 0 else [(0, 4), (4, 4)]

        def sq_t(i):
            return room[:, 16 + 2 * (i % 2):18 + 2 * (i % 2)].rearrange("p a b -> p (a b)")

        def jobs(l):
            main = [(False, o, NS_MAIN, NT) for o in range(2)]
            return main + ([(True, o, NS_CTX, NTC) for o in range(2)] if l == 0 else [])

        def sections(l):
            edge = {0: 0, 1: 0, 6: 4, 7: 4}
            a = [(j, edge[j], 4) if j in edge else (j, j - 2, 5) for j in range(NT)]
            c = [(j, max(j - 1, 0), 2 if j in (0, NT - 1) else 3) for j in range(NT)]
            out = [("A", MIX_A, None, 0, a), ("C", MIX_C, N_K - 1, 384, c)]
            if l == 0:
                x = [(NT + j, 0, 0) for j in range(NTC)]
                out += [("XA", MIX_A, None, 0, x), ("XC", MIX_C, N_K - 1, 384, x)]
            return out

        def steps_of(name, n_units):
            tables = 2 if name == "A" else 0
            maxima = 2 if name in "AC" else 1
            sums = 2 if "C" in name else 1
            return tables + n_units * maxima + n_units // 2 * sums

        before, counted = {}, [0, 0, 0]
        for l in L2:
            for sec in sections(l):
                before[l, sec[0]] = tuple(counted)
                n_units = 2 * len(sec[4])
                counted[0] += 3 * n_units
                counted[1] += 3 * n_units * ("C" in sec[0])
                counted[2] += 3 * steps_of(sec[0], n_units)

        def chunks(sec, ji):
            _, first, n = sec[4][ji]
            return [(i * P, NT + i) for i in range(NTC)] + [(CTX + i * P, first + i) for i in range(n)]

        block = ctx.enter_context(nc.Block())

        @block.sync
        def _(sp):
            for s in range(RING):
                sp.dma_start(ring[:, s].rearrange("p k m -> p (k m)"), A["weights"][s]).then_inc(slot_in[s], 16)
            with sp.Fori(1, N_STREAM // RING) as i:
                for s in range(RING):
                    sp.wait_ge(block_done, i * RING + (s + 1 - RING))
                    sp.dma_start(ring[:, s].rearrange("p k m -> p (k m)"),
                                 A["weights"][bass.ds(i * RING + s, 1)].rearrange("a p f -> (a p) f")
                                 ).then_inc(slot_in[s], 16)

        @block.gpsimd
        def _(pool):
            g = nc.gpsimd
            for dst, src in ((ident[:], A["ident"]), (condT[:], A["cond"]), (norm_g[:], A["norm_g"]),
                             (b_ada[:], A["b_ada"]), (conv_w[:], A["conv_w"]), (f_small[:], A["f_small"]),
                             (sink[:], A["sink"])):
                pool.dma_start(dst, src).then_inc(consts_in, 16)
            pool.dma_start(act_t[:], A["x_blocks"].rearrange("m p t -> p m t")).then_inc(x_loaded, 16)
            g.memset(ones[:], 1.0).then_inc(consts_set, 1)
            for l in L2:
                if l:
                    pool.wait_ge(block_taken, taken_before(l, "pb"))
                for b in range(2):
                    g.memset(pc_in[:, b, 0:1], 0.0).then_inc(pads_set, 1)
                    g.memset(pc_in[:, b, SEQ + 1:SEQ + 3], 0.0).then_inc(pads_set, 1)
                    g.memset(pc_in[:, b, PAD - 1:PAD], 0.0).then_inc(pads_set, 1)
                pool.dma_start(dft_f, A["dft_f"]).then_inc(dft_in[l], 16)
                pool.dma_start(dft_i, A["dft_i"]).then_inc(dft_in[l], 16)
                pool.wait_ge(conv_ready[l], N_PB)
                pool.wait_ge(tp_ready[l], 4 * len(time_tiles(l)))
                pool.dma_start(w3f, A["w3"][l, 0]).then_inc(fl_in[l], 16)
                pool.dma_start(w3r, A["w3"][l, 1]).then_inc(fl_in[l], 16)
                pool.dma_start(w12, A["w12"][l]).then_inc(fl_in[l], 16)
                conv_n = x_n = 0
                for ji, (isctx, o, ns, nt) in enumerate(jobs(l)):
                    nm = "_ctx" if isctx else ""
                    if o == 0:
                        if isctx:
                            pool.wait_ge(yt_ready[l], 1)
                        pool.dma_start(feats[0:66, 0:nt * P], A["feats" + nm]).then_inc(fl_in[l], 16)
                    if ji:
                        pool.wait_ge(x_taken[l], x_n)
                    pool.dma_start(decay[:, 0:2 * nt], A["decay" + nm]).then_inc(dec_in[l], 16)
                    pool.dma_start(d_row[0:1], A["hy_d"][l, o:o + 1]).then_inc(drow_in[l], 16)
                    x_n += ns
                    for s in range(ns):
                        pr_a, pr_b = prod[:, conv_n % 2, 0], prod[:, conv_n % 2, 1]
                        x_n += 1
                        conv_n += 1
                        pool.wait_ge(prod_ready[l], conv_n)
                        pool.wait_ge(x_taken[l], x_n)
                        g.tensor_tensor(spec[:, s, 0], pr_a[:, 0:CH], pr_b[:, CH:], ALU.subtract).then_inc(y_part[l], 1)
                        g.tensor_tensor(spec[:, s, 1], pr_a[:, CH:], pr_b[:, 0:CH], ALU.add).then_inc(y_part[l], 1)
                pool.wait_ge(hyena_done[l], 1)
                pool.dma_start(rope_cs, A["rope"]).then_inc(rope_in[l], 16)
                for dst, src in ((m_cols, "m_cols"), (m_rows, "m_rows"), (m_win, "m_win")):
                    pool.dma_start(dst, A[src]).then_inc(masks_in[l], 16)
                g.memset(q_st.rearrange("p a b c -> p (a b c)"), 0.0).then_inc(qst_zero, 1)
                pool.wait_ge(rope_done[l], 1)
                for h in range(6):
                    for par in range(2):
                        pool.dma_start(t_raw[64 * par:64 * par + 64, h].rearrange("p a b -> p (a b)"),
                                       A["rpb"][l, h, :, 1 - par:15 - par].rearrange("p a b -> p (a b)")
                                       ).then_inc(traw_in[l], 16)
                pool.wait_ge(neg_ready, before[l, "C"][0])
                for b in range(2):
                    pool.wait_ge(g_stored[l][b], 16 * (len(gate_parts(l)) // 2))
                for m in range(N_G):
                    if m >= 2:
                        pool.wait_ge(mix_gated[l], m - 1)
                    pool.dma_start(g_in[:, m % 2, 0:ntok(l)], A["gates"][m, :, 0:ntok(l)]).then_inc(g_in_in[l][m % 2], 16)
                if l:
                    pool.wait_ge(x_stored, 16 * KC)
                pool.wait_ge(mix_gated[l], 1)
                for m in range(KC):
                    if m >= 2:
                        pool.wait_ge(block_taken, taken_before(l, "out") + m - 1)
                    pool.dma_start(x_in[:, m % 2], A["x_mid" if l else "x_blocks"][m]).then_inc(xin_in[l][m % 2], 16)
                    if l == 0 and m >= 1:
                        pool.wait_ge(block_taken, taken_before(l, "out") + m)
                        pool.dma_start(A["x_mid"][m - 1], act_t[:, m - 1]).then_inc(x_stored, 16)
                if l == 0:
                    pool.wait_ge(block_taken, taken_before(l, "end"))
                    pool.dma_start(A["x_mid"][KC - 1], act_t[:, KC - 1]).then_inc(x_stored, 16)
            for m in range(KC):
                pool.wait_ge(fin_ready, m + 1)
                pool.dma_start(A["out"][m], fin[:, m % 2]).then_inc(fin_out[m % 2], 16)
            for b in range(2):
                pool.wait_ge(fin_out[b], 16 * KC // 2)

        @block.tensor
        def _(pe):
            mm, tr = nc.tensor.matmul, nc.tensor.transpose
            at = [0]

            def over_blocks(n, emit):
                done = 0
                while done < n:
                    turns, base = (n - done) // RING, at[0] // RING
                    if at[0] % RING == 0 and turns >= 2:
                        with pe.Fori(0, turns) as i:
                            for s in range(RING):
                                pe.wait_ge(slot_in[s], (i + (base + 1)) * 16)
                                emit(i * RING + (done + s), s)
                        done += turns * RING
                        at[0] += turns * RING
                    else:
                        s = at[0] % RING
                        pe.wait_ge(slot_in[s], 16 * (base + 1))
                        emit(done, s)
                        done += 1
                        at[0] += 1

            def project(src, n, first_taken):
                def emit(idx, s):
                    if first_taken or not isinstance(idx, int) or idx >= 2:
                        pe.wait_ge(block_taken, idx + (first_taken - 1))
                    for k in range(KC):
                        for gi, (t, w) in enumerate(groups(n)):
                            last = mm(ps[:, 3 * (s % 2) + gi, 0:w], ring[:, s, k], src[:, k, t:t + w],
                                      start=(k == 0), stop=(k == KC - 1))
                    last.then_inc(block_done, 1)
                return emit

            def sum_of_squares(l, n):
                for gi, (t, w) in enumerate(groups(n)):
                    for k in range(KC):
                        pe.wait_ge(sq_ready[l], gi * KC + k + 1)
                        mm(ps[:, gi, 0:w], ones[:], sq[:, (gi * KC + k) % 3, 0:w],
                           start=(k == 0), stop=(k == KC - 1)).then_inc(sq_used[l], 1)

            def transform(mats, slot, bank, inverse):
                m0, out = DFT_START[slot], ps[:, bank]
                if slot < 2 and not inverse:
                    mm(out[:, 0:CH], mats[:, m0], spec[:, slot, 0], start=True, stop=True)
                    return mm(out[:, CH:], mats[:, m0 + 1], spec[:, slot, 0], start=True, stop=True)
                if slot < 2:
                    mm(out[:, 0:CH], mats[:, m0], spec[:, slot, 0], start=True, stop=False)
                    return mm(out[:, 0:CH], mats[:, m0 + 1], spec[:, slot, 1], start=False, stop=True)
                plus, minus = (m0 + 2, m0 + 1) if inverse else (m0 + 1, m0 + 2)
                mm(out, mats[:, m0], spec[:, slot].rearrange("p a c -> p (a c)"), start=True, stop=False,
                   skip_group_check=True)
                mm(out[:, 0:CH], mats[:, plus], spec[:, slot, 1], start=False, stop=False, skip_group_check=True)
                return mm(out[:, CH:], mats[:, minus], spec[:, slot, 0], start=False, stop=True, skip_group_check=True)

            def hyena(l, fill):
                net = taps = bf = xn = wn = 0
                for ji, (isctx, o, ns, nt) in enumerate(jobs(l)):
                    if o == 0:
                        pe.wait_ge(fl_in[l], 16 * (4 + isctx))
                        pe.wait_ge(block_taken, taken_before(l, "q"))
                        for gi, (t, w) in enumerate(groups(nt * P)):
                            last = mm(ps[:, gi, 0:w], w12[0:66, 0], feats[0:66, t:t + w], start=True, stop=True)
                        last.then_inc(mlp_mm[l], 1)
                        pe.wait_ge(hid_ready[l], net + 1)
                        for gi, (t, w) in enumerate(groups(nt * P)):
                            last = mm(ps[:, 2 + gi, 0:w], w12[:, 1], mlp[2][:, t:t + w], start=True, stop=True)
                        last.then_inc(mlp_mm[l], 1)
                        net += 2
                        pe.wait_ge(hid_ready[l], net)
                    if isctx and o == 0:
                        pe.wait_ge(yt_taken[l], 4)
                    for i in range(nt):
                        if taps >= 2:
                            pe.wait_ge(tap_ready[l], taps - 1)
                        for e in range(2):
                            t = 2 * i + e
                            last = mm(ps[:, 4 + taps % 2, e * CH:(e + 1) * CH], hid[:, (t % nt) * P:(t % nt + 1) * P],
                                      (w3f if t < nt else w3r)[:, o * CH:(o + 1) * CH], start=True, stop=True)
                        last.then_inc(tap_mm[l], 1)
                        taps += 1
                    for i in range(nt):
                        pe.wait_ge(tsq_ready[l], taps - nt + i + 1)
                        mm(ps[:, 1], ones[:], sq_t(i), start=(i == 0), stop=(i == nt - 1)).then_inc(tsq_used[l], 1)
                    if ji == 0:
                        pe.wait_ge(dft_in[l], 32)
                    at_taps, at_signal, at_slot, at_end = fills(l, isctx)
                    fill(at_taps)
                    for signal in range(2):
                        if signal:
                            fill(at_signal)
                        for s in range(ns + signal):
                            if s < ns:
                                pe.wait_ge(bf_ready[l], bf + s + 1)
                                if xn >= 2:
                                    pe.wait_ge(x_taken[l], xn - 1)
                                transform(dft_f, s, xn % 2, False).then_inc(x_mm[l], 1)
                                xn += 1
                            if signal and s >= 1:
                                pe.wait_ge(y_part[l], 2 * (wn + 1))
                                if wn >= 2:
                                    pe.wait_ge(w_taken[l], wn - 1)
                                transform(dft_i, s - 1, 2 + wn % 2, True).then_inc(w_mm[l], 1)
                                wn += 1
                                if s in (3, 6):
                                    fill(at_slot)
                        bf += ns
                    fill(at_end)
                    if o == 1:
                        pe.wait_ge(yt_ready[l], 1 + isctx)
                        for gi, (b, t0, w) in enumerate(back_tiles(isctx)):
                            if gi >= 2 or isctx:
                                pe.wait_ge(yt_taken[l], 4 * isctx + gi - 1 if gi >= 2 else 4)
                            for e in range(w):
                                last = tr(ps[:, 4 + gi % 2, e * P:(e + 1) * P], z_tm[:, t0 + e, b * P:(b + 1) * P], ident[:])
                            last.then_inc(yt_mm[l], 1)

            def attention(l, sec):
                name, _, kb, vcol, tiles = sec
                base, _, _ = before[l, name]
                nu = 2 * len(tiles)
                with pe.Fori(0, 3) as pr:
                    u0 = pr * nu + base

                    def keys(t0, n):
                        if kb is None:
                            return k_fm[:, bass.ds(pr, 1), t0:t0 + n].rearrange("p a b -> p (a b)")
                        return k_fm[:, kb, t0:t0 + n]

                    def scores(k):
                        ji, par = divmod(k, 2)
                        _, first, n = tiles[ji]
                        if par == 0:
                            pe.wait_ge(qst_ready, u0 + (k + 2))
                        if k >= 2:
                            pe.wait_ge(neg_ready, u0 + (k - 1))
                        bank, q = 2 * (k % 2), q_st[:, ji % 2, par]
                        if n:
                            w = min(n, 4) * P
                            mm(ps[:, bank, 0:w], q, keys(first * P, w), start=True, stop=True)
                        if n > 4:
                            mm(ps[:, bank + 1, 0:P], q, keys((first + 4) * P, P), start=True, stop=True)
                        mm(ps[:, bank + 1, P:P + CTX], q, keys(SEQ, CTX), start=True, stop=True).then_inc(s_ready, 1)

                    def transpose_p(k):
                        pe.wait_ge(p_ready, u0 + (k + 1))
                        if k >= 1:
                            pe.wait_ge(pt_dve, u0 + k)
                            pe.wait_ge(pt_act, u0 + k)
                        cs = chunks(sec, k // 2)
                        half = (len(cs) + 1) // 2
                        for c, (col, _) in enumerate(cs):
                            bank, at_col = (4, c) if c < half else (5, c - half)
                            last = tr(ps[:, bank, at_col * P:(at_col + 1) * P], p_sb[:, k % 2, col:col + P], ident[:])
                        last.then_inc(pt_ready, 1)

                    def times_v(k):
                        ji, par = divmod(k, 2)
                        pe.wait_ge(pt_dve, u0 + (k + 1))
                        pe.wait_ge(pt_act, u0 + (k + 1))
                        if par == 0 and ji >= 2:
                            pe.wait_ge(ot_taken, half_of(u0) + (ji - 1))
                        cs = chunks(sec, ji)
                        for c, (_, t) in enumerate(cs):
                            v = v_tm[:, t, bass.ds(pr * P + par * HD, HD)] if kb is None else \
                                v_tm[:, t, vcol + par * HD:vcol + (par + 1) * HD]
                            last = mm(ps[:, 6 + ji % 2, par * HD:(par + 1) * HD], pt_sb[:, k % 2, c * P:(c + 1) * P], v,
                                      start=(c == 0), stop=(c == len(cs) - 1))
                        last.then_inc(o_ready, 1)

                    def half_of(_):
                        return pr * (nu // 2) + base // 2

                    def transpose_o(w):
                        pe.wait_ge(on_ready, u0 + (2 * w + 2))
                        tr(ps[:, 6 + w % 2, P:2 * P], o_sb[:, w % 2], ident[:]).then_inc(ot_ready, 1)

                    scores(0)
                    scores(1)
                    for k in range(nu):
                        transpose_p(k)
                        if k + 2 < nu:
                            scores(k + 2)
                        times_v(k)
                        if k >= 2 and k % 2 == 0:
                            transpose_o(k // 2 - 1)
                    transpose_o(nu // 2 - 1)

            def ada_block(idx, s):
                out = ps[:, 7, bass.ds(idx * 2, 2)] if not isinstance(idx, int) else ps[:, 7, 2 * idx:2 * idx + 2]
                for k in range(KC):
                    last = mm(out, ring[:, s, k], silu_c[:, k], start=(k == 0), stop=(k == KC - 1))
                last.then_inc(block_done, 1)

            def gate_filler(l):
                parts, done = gate_parts(l), [0]

                def fill(n):
                    for _ in range(min(n, len(parts) - done[0])):
                        c = done[0]
                        b, t, w = parts[c]
                        s = at[0] % RING
                        if t == 0:
                            pe.wait_ge(slot_in[s], 16 * (at[0] // RING + 1))
                        if c >= 2:
                            pe.wait_ge(g_taken[l], c - 1)
                        for k in range(KC):
                            last = mm(ps[:, 6 + c % 2, 0:w], ring[:, s, k], act_t[:, k, t:t + w],
                                      start=(k == 0), stop=(k == KC - 1))
                        done[0] += 1
                        if t + w == ntok(l):
                            last.then_inc(block_done, 1)
                            at[0] += 1
                        else:
                            last.then_inc(g_mm[l], 1)
                return fill

            pe.wait_ge(consts_in, 16 * 7)
            pe.wait_ge(consts_set, 1)
            pe.wait_ge(silu_ready, 1)
            for l in L2:
                n = ntok(l)

                if l:
                    pe.wait_ge(block_taken, taken_before(l, "pb"))
                else:
                    over_blocks(N_ADA, ada_block)
                sum_of_squares(l, TOK)

                pe.wait_ge(h_ready[l], 2 * KC)

                def to_time(b):
                    pe.wait_ge(conv_ready[l], b + 1)
                    for gi, (t0, w) in enumerate(time_tiles(l)):
                        c = b * len(time_tiles(l)) + gi
                        if c >= 2:
                            pe.wait_ge(tp_taken[l], c - 1)
                        for t in range(t0, t0 + w):
                            col = 1 + t * P + (2 if t >= NT else 0)
                            last = tr(ps[:, 6 + c % 2, (t - t0) * P:(t - t0 + 1) * P], pc_out[:, b % 2, col:col + P], ident[:])
                        last.then_inc(tp_ready[l], 1)

                emit = project(act_t, n, taken_before(l, "pb"))

                def pb_block(idx, s):
                    emit(idx, s)
                    if 1 <= idx <= 4:
                        to_time(idx - 1)
                for b in range(N_PB):
                    s = at[0] % RING
                    pe.wait_ge(slot_in[s], 16 * (at[0] // RING + 1))
                    pb_block(b, s)
                    at[0] += 1
                pe.wait_ge(tp_taken[l], 4 * len(time_tiles(l)))
                fill = gate_filler(l)
                hyena(l, fill)
                fill(len(gate_parts(l)))
                if l == 0:
                    pe.wait_ge(g_taken[l], len(gate_parts(l)))
                    over_blocks(N_ADA, ada_block)
                    v_banks_free = ada_ready, DEPTH
                else:
                    v_banks_free = g_taken[l], len(gate_parts(l))

                pe.wait_ge(hyena_done[l], 1)
                over_blocks(N_Q, project(act_t, n, taken_before(l, "q")))
                over_blocks(N_K, project(act_t, TOK, taken_before(l, "k")))
                slots = [(at[0] + i) % RING for i in range(N_V)]
                for i, s in enumerate(slots):
                    pe.wait_ge(slot_in[s], 16 * ((at[0] + i) // RING + 1))
                pe.wait_ge(*v_banks_free)
                for t in range(NT + NTC):
                    if t >= 2:
                        pe.wait_ge(v_taken[l], t - 1)
                    for k in range(KC):
                        w = ring[:, slots[k // 2]].rearrange("p k m -> p (k m)")[:, (k % 2) * 512:(k % 2) * 512 + 512]
                        last = mm(ps[:, 6 + t % 2], act_t[:, k, t * P:(t + 1) * P], w, start=(k == 0), stop=(k == KC - 1))
                        if t == NT + NTC - 1 and k % 2:
                            last.then_inc(block_done, 1)
                    if t < NT + NTC - 1:
                        last.then_inc(v_mm[l], 1)
                at[0] += N_V

                pe.wait_ge(v_taken[l], NT + NTC)
                pe.wait_ge(rope_done[l], 1)
                pe.wait_ge(qst_zero, l + 1)
                for sec in sections(l):
                    attention(l, sec)

                pe.wait_ge(mix_gated[l], N_G)
                over_blocks(N_OUT, project(mix, n, taken_before(l, "out")))
            pe.wait_ge(block_taken, DEPTH * TAKEN)
            sum_of_squares(DEPTH, SEQ)

        @block.scalar
        def _(act):
            fn = nc.scalar.activation

            def squares(l, n):
                for gi, (t, w) in enumerate(groups(n)):
                    for k in range(KC):
                        i = gi * KC + k
                        if i >= 3:
                            act.wait_ge(sq_used[l], i - 2)
                        fn(sq[:, i % 3, 0:w], act_t[:, k, t:t + w], ACT.Square).then_inc(sq_ready[l], 1)
                act.wait_ge(ms_ready, l + 1)
                fn(rstd[:, 0:n], rstd[:, 0:n], ACT.Sqrt).then_inc(std_ready, 1)

            def attention(l, sec):
                name, _, kb, _, tiles = sec
                base, sinks, _ = before[l, name]
                nu = 2 * len(tiles)
                with act.Fori(0, 3) as pr:
                    u0 = pr * nu + base

                    def exps(k):
                        n = CTX + tiles[k // 2][2] * P
                        act.wait_ge(neg_ready, u0 + (k + 1))
                        if k >= 2:
                            act.wait_ge(pt_ready, u0 + (k - 1))
                        fn(p_sb[:, k % 2, 0:n], s_sb[:, k % 2, 0:n], ACT.Exp, bias=stat[:, k % 2:k % 2 + 1],
                           accum_out=stat[:, 8 + k % 4:9 + k % 4]).then_inc(p_ready, 1)
                        if "C" in name:
                            fn(stat[:, 12 + k % 4:13 + k % 4], sink[:, l, bass.ds(pr * 2 + k % 2, 1)], ACT.Exp,
                               bias=stat[:, k % 2:k % 2 + 1]).then_inc(es_ready, 1)

                    def take_pt(k):
                        cs = len(chunks(sec, k // 2))
                        half = (cs + 1) // 2
                        act.wait_ge(pt_ready, u0 + (k + 1))
                        if k >= 2:
                            act.wait_ge(o_ready, u0 + (k - 1))
                        fn(pt_sb[:, k % 2, half * P:cs * P], ps[:, 5, 0:(cs - half) * P], ACT.Copy).then_inc(pt_act, 1)

                    exps(0)
                    for k in range(nu):
                        take_pt(k)
                        if k + 1 < nu:
                            exps(k + 1)

            def gate_filler(l):
                parts, done = gate_parts(l), [0]

                def fill(n):
                    for _ in range(min(n, len(parts) - done[0])):
                        c = done[0]
                        b, t, w = parts[c]
                        if t + w == ntok(l):
                            act.wait_ge(block_done, done_at(l, "g") + b + 1)
                        else:
                            act.wait_ge(g_mm[l], c - b + 1)
                        if c >= 2:
                            act.wait_ge(g_stored[l][c % 2], 16 * (c // 2))
                        elif l:
                            act.wait_ge(g_stored[0][c], 16 * (len(gate_parts(0)) // 2))
                        fn(g_st[:, c % 2, 0:w], ps[:, 6 + c % 2, 0:w], ACT.Silu).then_inc(g_taken[l], 1)
                        act.wait_ge(g_taken[l], c + 1)
                        if l and c == 0:
                            act.wait_ge(mix_gated[0], N_G)
                        act.dma_start(A["gates"][b, :, t:t + w], g_st[:, c % 2, 0:w]).then_inc(g_stored[l][c % 2], 16)
                        done[0] += 1
                return fill

            act.wait_ge(consts_in, 16 * 7)
            fn(silu_c[:], condT[:], ACT.Silu).then_inc(silu_ready, 1)
            act.wait_ge(x_loaded, 16)
            for l in L2:
                n = ntok(l)
                if l:
                    act.wait_ge(block_taken, taken_before(l, "pb"))
                squares(l, TOK)
                act.wait_ge(ada_ready, l + 1)
                for k in range(KC):
                    for c, (t0, t1) in enumerate(((0, SEQ), (SEQ, TOK))):
                        act.wait_ge(scaled[l], 2 * k + c + 1)
                        fn(act_t[:, k, t0:t1], act_t[:, k, t0:t1], ACT.Identity,
                           bias=ada[:, l, k, c:c + 1]).then_inc(h_ready[l], 1)

                act.wait_ge(pads_set, 6 * (l + 1))

                def pad_block(b):
                    act.wait_ge(block_done, done_at(l, "pb") + b + 1)
                    if b >= 2:
                        act.wait_ge(conv_ready[l], b - 1)
                    src = ps[:, 3 * (b % 2):3 * (b % 2) + 3].rearrange("p a b -> p (a b)")
                    fn(pc_in[:, b % 2, 1:1 + SEQ], src[:, 0:SEQ], ACT.Copy).then_inc(pc_ready[l], 1)
                    if l == 0:
                        fn(pc_in[:, b % 2, SEQ + 3:SEQ + 3 + CTX], src[:, SEQ:TOK], ACT.Copy).then_inc(pc_ready[l], 1)

                def take_tiles(b):
                    dst = z_tm if b < 2 else x1_tm
                    for gi, (t0, w) in enumerate(time_tiles(l)):
                        c = b * len(time_tiles(l)) + gi
                        act.wait_ge(tp_ready[l], c + 1)
                        fn(dst[:, t0:t0 + w, (b % 2) * P:(b % 2 + 1) * P],
                           ps[:, 6 + c % 2, 0:w * P].rearrange("p (a b) -> p a b", b=P), ACT.Copy).then_inc(tp_taken[l], 1)

                pad_block(0)
                for b in range(1, N_PB):
                    pad_block(b)
                    if b <= 4:
                        take_tiles(b - 1)

                taps = net = wn = 0
                fill = gate_filler(l)
                for ji, (isctx, o, ns, nt) in enumerate(jobs(l)):
                    at_taps, at_signal, at_slot, at_end = fills(l, isctx)
                    if o == 0:
                        for layer in range(2):
                            act.wait_ge(arg_ready[l], net + 1)
                            dst = mlp[2] if layer == 0 else hid
                            fn(dst[:, 0:nt * P], mlp[0][:, 0:nt * P], ACT.Sin).then_inc(hid_ready[l], 1)
                            net += 1
                    for i in range(nt):
                        act.wait_ge(tap_ready[l], taps + i + 1)
                        if i >= 2:
                            act.wait_ge(tsq_used[l], taps + i - 1)
                        fn(sq_t(i), room[:, 2 * i:2 * i + 2].rearrange("p a b -> p (a b)"), ACT.Square).then_inc(tsq_ready[l], 1)
                    taps += nt
                    act.wait_ge(en_ready[l], ji + 1)
                    fn(k_rt, k_rt, ACT.Sqrt).then_inc(rt_ready[l], 1)
                    fill(at_taps)
                    fill(at_signal)
                    for s in range(ns):
                        act.wait_ge(w_mm[l], wn + 1)
                        w = CH if s < 2 else 2 * CH
                        fn(spec[:, s].rearrange("p a c -> p (a c)")[:, 0:w], ps[:, 2 + wn % 2, 0:w], ACT.Copy
                           ).then_inc(w_taken[l], 1)
                        wn += 1
                        if s in (2, 5):
                            fill(at_slot)
                    fill(at_end)
                fill(len(gate_parts(l)))

                for t in range(NT + NTC):
                    if t < NT + NTC - 1:
                        act.wait_ge(v_mm[l], t + 1)
                    else:
                        act.wait_ge(block_done, done_at(l, "v") + N_V)
                    fn(v_tm[:, t], ps[:, 6 + t % 2], ACT.Copy).then_inc(v_taken[l], 1)

                for sec in sections(l):
                    attention(l, sec)

            act.wait_ge(block_taken, DEPTH * TAKEN)
            squares(DEPTH, SEQ)

        @block.vector
        def _(dve):
            v = nc.vector
            step = Steps(dve)

            def tt(out, a, op, b, sem=None):
                step(v.tensor_tensor(out, a, b, op), sem)

            def stt(out, a, c, op, b, sem=None):
                step(v.scalar_tensor_tensor(out=out, in0=a, scalar=c, in1=b, op0=ALU.mult, op1=op), sem)

            def mul(out, a, c, sem=None):
                step(v.tensor_scalar(out, a, c, None, ALU.mult), sem)

            add, sub, mult = ALU.add, ALU.subtract, ALU.mult

            def norm(l, n):
                dve.wait_ge(sq_used[l], KC * len(groups(n)))
                src = ps[:, 0:3].rearrange("p a b -> p (a b)")
                step(v.tensor_scalar(rstd[:, 0:n], src[:, 0:n], 1.0 / D, EPS, mult, add), ms_ready)
                dve.wait_ge(std_ready, l + 1)
                step(v.reciprocal(rstd[:, 0:n], rstd[:, 0:n]))
                step.join()

            def reduce_arg(n, bank, b, f):
                src = ps[:, bank:bank + 2].rearrange("p a b -> p (a b)")[:, 0:n]
                a, k = mlp[0][:, 0:n], mlp[1][:, 0:n]
                step(v.tensor_scalar(a, src, b, f, add, mult))
                step.join()
                step(v.tensor_scalar(k, a, 1.0 / (2 * math.pi), ROUND, mult, add))
                step.join()
                step(v.tensor_scalar(k, k, ROUND, None, sub))
                for part in (TWO_PI_A, TWO_PI_B, TWO_PI_C):
                    step.join()
                    stt(a, k, -part, add, a)
                step.join()

            def even(src, z):
                tb, tc, te, td = room[:, 0:4], room[:, 4:8], room[:, 24:26], room[:, 26:28]
                tt(tb, src[:, 0:4], add, src[:, 4:8])
                tt(tc, src[:, 0:4], sub, src[:, 4:8])
                step.join()
                tt(te, tb[:, 0:2], add, tb[:, 2:4])
                tt(z[:, 2, 0], tb[:, 0], sub, tb[:, 2])
                tt(td[:, 0], tc[:, 1], sub, tc[:, 3])
                tt(td[:, 1], tc[:, 1], add, tc[:, 3])
                step.join()
                tt(z[:, 0, 0], te[:, 0], add, te[:, 1], bf)
                tt(z[:, 1, 0], te[:, 0], sub, te[:, 1], bf)
                tt(z[:, 2, 1], tb[:, 3], sub, tb[:, 1], bf)
                stt(z[:, 3, 0], td[:, 0], SQ5, add, tc[:, 0])
                stt(z[:, 3, 1], td[:, 1], -SQ5, sub, tc[:, 2], bf)
                stt(z[:, 4, 0], td[:, 0], -SQ5, add, tc[:, 0])
                stt(z[:, 4, 1], td[:, 1], -SQ5, add, tc[:, 2], bf)
                step.join()

            def odd(src, z):
                tp, tm, te = room[:, 0:3], room[:, 3:6], room[:, 6:8]
                tf, to, tg = room[:, 24:26], room[:, 26:28], room[:, 28:30]
                tt(tp, src[:, 1:4], sub, src[:, 7:4:-1])
                tt(tm, src[:, 1:4], add, src[:, 7:4:-1])
                step.join()
                stt(te[:, 0], tp[:, 1], SQ5, add, src[:, 0])
                stt(te[:, 1], tp[:, 1], -SQ5, add, src[:, 0])
                stt(tf[:, 0], tm[:, 1], SQ5, add, src[:, 4])
                stt(tf[:, 1], tm[:, 1], SQ5, sub, src[:, 4])
                mul(to[:, 0], tp[:, 0], C1)
                mul(to[:, 1], tp[:, 0], S1)
                mul(tg[:, 0], tm[:, 0], -S1)
                mul(tg[:, 1], tm[:, 0], -C1)
                step.join()
                stt(to[:, 0], tp[:, 2], S1, add, to[:, 0])
                stt(to[:, 1], tp[:, 2], -C1, add, to[:, 1])
                stt(tg[:, 0], tm[:, 2], -C1, add, tg[:, 0])
                stt(tg[:, 1], tm[:, 2], S1, add, tg[:, 1])
                step.join()
                for i in range(2):
                    tt(z[:, 5 + i, 0], te[:, i], add, to[:, i])
                    tt(z[:, 5 + i, 1], tg[:, i], sub, tf[:, i], bf)
                for i in range(2):
                    tt(z[:, 7 + i, 0], te[:, i], sub, to[:, i])
                    tt(z[:, 7 + i, 1], tg[:, i], add, tf[:, i], bf)
                step.join()

            def few(kc, kn, z):
                tt(z[:, 0, 0], kc[:, 0], add, kc[:, 1], bf)
                tt(z[:, 1, 0], kc[:, 0], sub, kc[:, 1], bf)
                mul(z[:, 2, 0], kn[:, 0], 1.0)
                mul(z[:, 2, 1], kn[:, 1], -1.0, bf)
                step.join()

            def back(y):
                r = room
                tt(r[:, 0:4].rearrange("p (a b) c -> p a b c", b=2), spec[:, 5:7], add, spec[:, 7:9])
                tt(r[:, 4:8].rearrange("p (a b) c -> p a b c", b=2), spec[:, 5:7], sub, spec[:, 7:9])
                tt(r[:, 8], spec[:, 0, 0], add, spec[:, 1, 0])
                tt(r[:, 9], spec[:, 0, 0], sub, spec[:, 1, 0])
                tt(r[:, 10:12], spec[:, 3], add, spec[:, 4])
                tt(r[:, 12:14], spec[:, 3], sub, spec[:, 4])
                step.join()
                tt(r[:, 14], r[:, 8], add, spec[:, 2, 0])
                tt(r[:, 15], r[:, 9], sub, spec[:, 2, 1])
                tt(r[:, 16], r[:, 8], sub, spec[:, 2, 0])
                tt(r[:, 17], r[:, 9], add, spec[:, 2, 1])
                tt(r[:, 18], r[:, 12], sub, r[:, 11])
                tt(r[:, 19], r[:, 12], add, r[:, 11])
                step.join()
                e = r[:, 20:28]
                tt(e[:, 0], r[:, 14], add, r[:, 10])
                tt(e[:, 4], r[:, 14], sub, r[:, 10])
                tt(e[:, 2], r[:, 16], sub, r[:, 13])
                tt(e[:, 6], r[:, 16], add, r[:, 13])
                stt(e[:, 1], r[:, 18], SQ5, add, r[:, 15])
                stt(e[:, 5], r[:, 18], -SQ5, add, r[:, 15])
                stt(e[:, 3], r[:, 19], -SQ5, add, r[:, 17])
                stt(e[:, 7], r[:, 19], SQ5, add, r[:, 17])
                step.join()
                pp, qp, rp, tp_ = (r[:, i] for i in range(4))
                pm, qm, rm, tm = (r[:, i] for i in range(4, 8))
                tt(r[:, 8], pp, add, rp)
                tt(r[:, 9], tm, sub, qm)
                tt(r[:, 10], pp, sub, rp)
                tt(r[:, 11], qm, add, tm)
                mul(r[:, 12], pm, C1)
                mul(r[:, 13], pm, S1)
                mul(r[:, 14], qp, S1)
                mul(r[:, 15], qp, C1)
                step.join()
                stt(r[:, 12], rm, S1, add, r[:, 12])
                stt(r[:, 13], rm, -C1, add, r[:, 13])
                stt(r[:, 14], tp_, C1, add, r[:, 14])
                stt(r[:, 15], tp_, -S1, add, r[:, 15])
                tt(r[:, 16], r[:, 10], sub, r[:, 11])
                tt(r[:, 17], r[:, 10], add, r[:, 11])
                step.join()
                tt(r[:, 18], r[:, 12], sub, r[:, 14])
                tt(r[:, 19], r[:, 12], add, r[:, 14])
                tt(r[:, 28], r[:, 13], sub, r[:, 15])
                tt(r[:, 29], r[:, 13], add, r[:, 15])
                tt(y[:, 0], e[:, 0], add, r[:, 8])
                tt(y[:, 4], e[:, 4], add, r[:, 9])
                stt(y[:, 2], r[:, 16], SQ5, add, e[:, 2])
                stt(y[:, 6], r[:, 17], -SQ5, add, e[:, 6])
                step.join()
                tt(y[:, 1], e[:, 1], add, r[:, 18])
                tt(y[:, 7], e[:, 7], sub, r[:, 19])
                tt(y[:, 3], e[:, 3], add, r[:, 28])
                tt(y[:, 5], e[:, 5], sub, r[:, 29])
                step.join()

            def hyena(l):
                nonlocal bf
                bf = bf_ready[l]
                taps = net = xn = wn = conv_n = back_n = 0
                for ji, (isctx, o, ns, nt) in enumerate(jobs(l)):
                    if o == 0:
                        for layer in range(2):
                            dve.wait_ge(mlp_mm[l], net + 1)
                            if layer:
                                dve.wait_ge(hid_ready[l], net)
                            reduce_arg(nt * P, 2 * layer, f_small[:, l, 2 * layer:2 * layer + 1],
                                       f_small[:, l, 2 * layer + 1:2 * layer + 2])
                            a = mlp[0][:, 0:nt * P]
                            step(v.tensor_scalar(a, a, 3.1415925, -3.1415925, ALU.min, ALU.max), arg_ready[l])
                            step.join()
                            net += 1
                    dve.wait_ge(dec_in[l], 16 * (ji + 1))
                    for i in range(nt):
                        dve.wait_ge(tap_mm[l], taps + i + 1)
                        tt(room[:, 2 * i:2 * i + 2], ps[:, 4 + (taps + i) % 2].rearrange("p (a b) -> p a b", b=CH), mult,
                           decay[:, 2 * i:2 * i + 2], tap_ready[l])
                    taps += nt
                    dve.wait_ge(tsq_used[l], taps)
                    step(v.tensor_copy(k_rt, ps[:, 1, 0:CH]))
                    step.join()
                    tt(k_rt, k_rt, add, ps[:, 1, CH:2 * CH])
                    step.join()
                    step(v.tensor_scalar(k_rt, k_rt, 1e-6, None, add), en_ready[l])
                    dve.wait_ge(rt_ready[l], ji + 1)
                    dve.wait_ge(drow_in[l], 16 * (ji + 1))
                    step(v.reciprocal(k_s, k_rt))
                    tt(d_row[0:1], d_row[0:1], mult, k_rt[0:1])
                    step.join()
                    tt(room[0:1, 0], room[0:1, 0], add, d_row[0:1])
                    if isctx:
                        mul(k_s, k_s, 4.0)
                    step.join()
                    kc, kn = room[:, 16:16 + nt], room[:, nt:2 * nt]
                    tt(kc, room[:, 0:nt], add, room[:, nt:2 * nt])
                    step.join()
                    tt(kn, room[:, 0:nt], sub, room[:, nt:2 * nt])
                    step.join()
                    if isctx:
                        few(kc, kn, spec)
                    else:
                        even(kc, spec)
                        odd(kn, spec)
                    for s in range(ns):
                        dve.wait_ge(x_mm[l], xn + 1)
                        tt(khat[:, s], ps[:, xn % 2].rearrange("p (a b) -> p a b", b=CH), mult,
                           k_s.unsqueeze(1).broadcast_to([P, 2, CH]), x_taken[l])
                        xn += 1
                    step.join()
                    u = z_tm[:, NT:NT + NTC] if isctx else z_tm[:, 0:NT]
                    if ji == 0:
                        dve.wait_ge(tp_taken[l], 4 * len(time_tiles(l)))
                    if isctx:
                        few(u, u, spec)
                    else:
                        even(u, spec)
                        odd(u, spec)
                    for s in range(ns):
                        dve.wait_ge(x_mm[l], xn + 1)
                        if conv_n >= 2:
                            dve.wait_ge(y_part[l], 2 * (conv_n - 1))
                        x = ps[:, xn % 2].rearrange("p (a b) -> p a b", b=CH)
                        for part, sm in ((0, prod_ready[l]), (1, x_taken[l])):
                            tt(prod[:, conv_n % 2, part].rearrange("p (a b) -> p a b", b=CH), x, mult,
                               khat[:, s, part].unsqueeze(1).broadcast_to([P, 2, CH]), sm)
                        xn += 1
                        conv_n += 1
                    wn += ns
                    dve.wait_ge(w_taken[l], wn)
                    if isctx:
                        r = room
                        tt(r[:, 0], spec[:, 0, 0], add, spec[:, 1, 0])
                        tt(r[:, 1], spec[:, 0, 0], sub, spec[:, 1, 0])
                        step.join()
                        tt(u[:, 0], r[:, 0], add, spec[:, 2, 0])
                        tt(u[:, 1], r[:, 1], sub, spec[:, 2, 1])
                        step.join()
                    else:
                        back(u)
                    if o == 0:
                        x1 = x1_tm[:, NT:NT + NTC] if isctx else x1_tm[:, 0:NT]
                        tt(u, u, mult, x1)
                        step.join()
                    else:
                        step(v.memset(stat_h[:, 0:1], 0.0), yt_ready[l])
                        for gi, (b, t0, w) in enumerate(back_tiles(isctx)):
                            dve.wait_ge(yt_mm[l], back_n + 1)
                            dst = mix[:, b, t0 * P:(t0 + w) * P]
                            tt(dst, dst, mult, ps[:, 4 + gi % 2, 0:w * P], yt_taken[l])
                            back_n += 1
                step.join()
                step(v.memset(stat_h[:, 0:1], 0.0), hyena_done[l])
                step.join()

            def take_ada(l):
                dve.wait_ge(block_done, done_at(l, "ada") + N_ADA)
                tt(ada[:, l], ps[:, 7, 0:2 * N_ADA].rearrange("p (a b) -> p a b", b=2), add,
                   b_ada[:, l].unsqueeze(2).broadcast_to([P, N_ADA, 2]), ada_ready)
                step.join()

            def rope(l):
                dve.wait_ge(rope_in[l], 16)
                for blk in [mix[:, MIX_C + i, 0:SEQ] for i in range(3)] + [k_fm[:, N_K - 1, 0:SEQ]]:
                    step(v.stream_shuffle(rope_t[:, 0], blk, [i ^ 16 for i in range(32)]))
                    step.join()
                    tt(rope_t[:, 1], rope_t[:, 0], mult, rope_cs[:, 1])
                    tt(blk, blk, mult, rope_cs[:, 0])
                    step.join()
                    tt(blk, blk, add, rope_t[:, 1])
                    step.join()
                step(v.memset(stat[:, 31:32], 0.0), rope_done[l])
                step.join()

            def attention(l, sec):
                name, qb, kb, _, tiles = sec
                base, sinks, steps = before[l, name]
                nu = 2 * len(tiles)
                nw = nu // 2
                has_sink = "C" in name
                per = steps_of(name, nu)
                with dve.Fori(0, 3) as pr:
                    u0 = pr * nu + base
                    w0 = pr * nw + base // 2
                    own = [0]

                    def chain(ins):
                        ins.then_inc(unit_step, 1)
                        own[0] += 1

                    def join():
                        dve.wait_ge(unit_step, pr * per + (steps + own[0]))

                    def q_block(j):
                        return mix[:, bass.ds(pr + qb, 1), j * P:(j + 1) * P].rearrange("p a b -> p (a b)")

                    def stage_q(w):
                        if w >= 2:
                            dve.wait_ge(s_ready, u0 + (2 * w - 2))
                        j = tiles[w][0]
                        for par in range(2):
                            src = mix[64 * par:64 * par + 64, bass.ds(pr + qb, 1), j * P:(j + 1) * P]
                            v.tensor_scalar(q_st[64 * par:64 * par + 64, w % 2, par], src.rearrange("p a b -> p (a b)"),
                                            QSCALE, None, mult).then_inc(qst_ready, 1)

                    def softmax_in(k):
                        j, first, n = tiles[k // 2]
                        par = k % 2
                        dve.wait_ge(s_ready, u0 + (k + 1))
                        if k >= 2:
                            dve.wait_ge(p_ready, u0 + (k - 1))
                            if has_sink:
                                dve.wait_ge(es_ready, pr * nu + (sinks + k - 1))
                        bank = 2 * (k % 2)
                        lo = sink[:, l, bass.ds(pr * 2 + par, 1)] if has_sink else LOWEST
                        chain(v.tensor_scalar(s_sb[:, k % 2, 0:CTX], ps[:, bank + 1, P:P + CTX], 1.0, lo, mult, ALU.max,
                                              accum_out=stat[:, 2 + k % 2:3 + k % 2]))
                        c, m = stat[:, 2 + k % 2:3 + k % 2], stat[:, 4 + k % 2:5 + k % 2]
                        if n:
                            if name == "A":
                                bias = t_inner[:, par] if n == 5 else \
                                    t_edge[:, par, (2 * (first - j) + 6) * GRID:(2 * (first - j) + 6) * GRID + n * P]
                            else:
                                bias = m_win[:, (first - j + 1) * P:(first - j + 1 + n) * P]
                            src = ps[:, bank:bank + 2].rearrange("p a b -> p (a b)")[:, 0:n * P]
                            chain(v.tensor_tensor_reduce(out=s_sb[:, k % 2, CTX:CTX + n * P], in0=src, in1=bias, scale=1.0,
                                                         scalar=LOWEST, op0=add, op1=ALU.max, accum_out=m))
                            join()
                            v.tensor_scalar(stat[:, k % 2:k % 2 + 1], m, c, -1.0, ALU.max, mult).then_inc(neg_ready, 1)
                        else:
                            join()
                            v.tensor_scalar(stat[:, k % 2:k % 2 + 1], c, -1.0, None, mult).then_inc(neg_ready, 1)

                    def take_pt(k):
                        half = (len(chunks(sec, k // 2)) + 1) // 2
                        dve.wait_ge(pt_ready, u0 + (k + 1))
                        if k >= 2:
                            dve.wait_ge(o_ready, u0 + (k - 1))
                        v.tensor_copy(pt_sb[:, k % 2, 0:half * P], ps[:, 4, 0:half * P]).then_inc(pt_dve, 1)

                    def divide(w):
                        dve.wait_ge(o_ready, u0 + (2 * w + 2))
                        if w >= 2:
                            dve.wait_ge(ot_ready, w0 + (w - 1))
                        cols = slice(8 + (2 * w) % 4, 10 + (2 * w) % 4)
                        total = stat[:, cols]
                        if has_sink:
                            dve.wait_ge(es_ready, pr * nu + (sinks + 2 * w + 2))
                            chain(v.tensor_tensor(stat[:, 16:18], total, stat[:, cols.start + 4:cols.stop + 4], add))
                            total = stat[:, 16:18]
                            join()
                        chain(v.reciprocal(stat[:, 18:20], total))
                        join()
                        for par in range(2):
                            v.tensor_scalar(o_sb[:, w % 2, par * HD:(par + 1) * HD], ps[:, 6 + w % 2, par * HD:(par + 1) * HD],
                                            stat[:, 18 + par:19 + par], None, mult).then_inc(on_ready, 1)

                    def take_o(w):
                        dve.wait_ge(ot_ready, w0 + (w + 1))
                        v.tensor_scalar(q_block(tiles[w][0]), ps[:, 6 + w % 2, P:2 * P], 1.0, None, mult).then_inc(ot_taken, 1)

                    if name == "A":
                        raw = t_raw[:, bass.ds(pr * 2, 2)].rearrange("p h a b -> p (h a) b")
                        chain(v.tensor_tensor(t_edge.rearrange("p h (a b) -> p (h a) b", b=GRID), raw,
                                              m_cols.unsqueeze(1).broadcast_to([P, 28, GRID]), add))
                        join()
                        chain(v.tensor_tensor(t_inner, t_edge[:, :, 128:768], m_rows.unsqueeze(1).broadcast_to([P, 2, 640]), add))
                        join()
                    stage_q(0)
                    if nw > 1:
                        stage_q(1)
                    softmax_in(0)
                    for k in range(nu):
                        if k + 1 < nu:
                            softmax_in(k + 1)
                        take_pt(k)
                        if k % 2 and k // 2 + 2 < nw:
                            stage_q(k // 2 + 2)
                        if k >= 2 and k % 2 == 0:
                            divide(k // 2 - 1)
                        if k >= 3 and k % 2:
                            take_o(k // 2 - 1)
                    divide(nw - 1)
                    take_o(nw - 1)
                    assert own[0] == per, (name, own[0], per)

            bf = None
            for l in L2:
                n = ntok(l)
                if l == 0:
                    dve.wait_ge(consts_in, 16 * 7)
                    take_ada(0)
                step(v.scalar_tensor_tensor(out=mod_a[:], in0=ada[:, l, KC:2 * KC], scalar=1.0,
                                            in1=norm_g[:, l].unsqueeze(2).broadcast_to([P, KC, 2]), op0=add, op1=mult))
                norm(l, TOK)
                if l:
                    dve.wait_ge(x_stored, 16 * KC)
                for k in range(KC):
                    for c, (t0, t1) in enumerate(((0, SEQ), (SEQ, TOK))):
                        stt(act_t[:, k, t0:t1], act_t[:, k, t0:t1], mod_a[:, k, c:c + 1], mult, rstd[:, t0:t1], scaled[l])
                step.join()

                w = TOK + 2 if l == 0 else SEQ
                step.at[block_taken.name] = taken_before(l, "pb")
                for b in range(N_PB):
                    dve.wait_ge(pc_ready[l], (b + 1) * (2 if l == 0 else 1))
                    if b >= 2:
                        dve.wait_ge(tp_ready[l], len(time_tiles(l)) * min(b - 1, 4))
                    x, y = pc_in[:, b % 2], pc_out[:, b % 2]
                    cw = [conv_w[:, l, b, i:i + 1] for i in range(4)]
                    step(v.tensor_scalar(y[:, 1:1 + w], x[:, 1:1 + w], cw[1], cw[3], mult, add), block_taken)
                    step.join()
                    stt(y[:, 1:1 + w], x[:, 0:w], cw[0], add, y[:, 1:1 + w])
                    step.join()
                    if b < 4:
                        stt(y[:, 1:1 + w], x[:, 2:2 + w], cw[2], add, y[:, 1:1 + w], conv_ready[l])
                    else:
                        if l == 0:
                            stt(mix[:, b - 4, SEQ:TOK], x[:, SEQ + 4:SEQ + 4 + CTX], cw[2], add, y[:, SEQ + 3:SEQ + 3 + CTX])
                        stt(mix[:, b - 4, 0:SEQ], x[:, 2:2 + SEQ], cw[2], add, y[:, 1:1 + SEQ], conv_ready[l])
                    step.join()

                hyena(l)
                if l == 0:
                    take_ada(1)

                for dst, first, stage, count, width in ((mix, MIX_A, "q", N_Q, n), (k_fm, 0, "k", N_K, TOK)):
                    with dve.Fori(0, count // 2) as i:
                        for e in range(2):
                            dve.wait_ge(block_done, i * 2 + (done_at(l, stage) + e + 1))
                            src = ps[:, 3 * e:3 * e + 3].rearrange("p a b -> p (a b)")
                            v.tensor_scalar(dst[:, bass.ds(i * 2 + (first + e), 1), 0:width].rearrange("p a b -> p (a b)"),
                                            src[:, 0:width], 1.0, None, mult).then_inc(block_taken, 1)
                dve.wait_ge(block_taken, taken_before(l, "out"))
                rope(l)
                dve.wait_ge(masks_in[l], 16 * 3)
                dve.wait_ge(traw_in[l], 16 * 12)
                dve.wait_ge(qst_zero, l + 1)
                for sec in sections(l):
                    attention(l, sec)

                for m in range(N_G):
                    dve.wait_ge(g_in_in[l][m % 2], 16 * (m // 2 + 1))
                    tt(mix[:, m, 0:n], mix[:, m, 0:n], mult, g_in[:, m % 2, 0:n], mix_gated[l])
                step.join()
                for m in range(KC):
                    dve.wait_ge(block_done, done_at(l, "out") + m + 1)
                    dve.wait_ge(xin_in[l][m % 2], 16 * (m // 2 + 1))
                    src = ps[:, 3 * (m % 2):3 * (m % 2) + 3].rearrange("p a b -> p (a b)")
                    if l == 0:
                        stt(act_t[:, m, SEQ:TOK], src[:, SEQ:TOK], ada[:, l, 2 * KC + m, 1:2], add, x_in[:, m % 2, SEQ:TOK])
                    v.scalar_tensor_tensor(out=act_t[:, m, 0:SEQ], in0=src[:, 0:SEQ], scalar=ada[:, l, 2 * KC + m, 0:1],
                                           in1=x_in[:, m % 2, 0:SEQ], op0=mult, op1=add).then_inc(block_taken, 1)
                step.join()
            norm(DEPTH, SEQ)
            for m in range(KC):
                if m >= 2:
                    dve.wait_ge(fin_out[m % 2], 16 * (m // 2))
                stt(fin[:, m % 2], act_t[:, m, 0:SEQ], norm_g[:, DEPTH, m:m + 1], mult, rstd[:, 0:SEQ], fin_ready)


def lay_out(i):
    f = np.float32
    i = {k: np.asarray(v, f) for k, v in i.items()}
    o = {}
    blocks = lambda w, cols: [w[:, c].reshape(KC, P, P).transpose(1, 0, 2).reshape(P, KC * P) for c in cols]
    rng = lambda a, n: [np.arange(a + P * b, a + P * b + P) for b in range(n)]
    heads = lambda a: [np.concatenate([np.arange(a + HD * h, a + HD * h + HD) for h in C_HEAD_ORDER[p:p + 2]])
                       for p in (0, 2, 4)]
    per = []
    rows = np.concatenate(rng(384, 2) + rng(0, 3) + heads(640))
    for l, name, _ in STREAM:
        w = i["w_in"][l]
        if name == "v":
            wv = np.concatenate([w[:, 768:1152], w[:, 3072:3200]], 1).reshape(KC, P, 512).transpose(1, 0, 2)
            per += [wv[:, 2 * b:2 * b + 2].reshape(P, 1024) for b in range(N_V)]
        elif name == "ada":
            per += blocks(i["w_ada"][l], rng(0, N_ADA))
        elif name == "out":
            per += blocks(i["w_out"][l][rows], rng(0, 8))
        else:
            per += blocks(w, {"pb": rng(1536, 6), "q": rng(0, 3) + heads(2560), "k": rng(384, 3) + rng(2944, 1),
                              "g": rng(2304, 2) + rng(1152, 3) + heads(3200)}[name])
    o["weights"] = np.stack(per)
    col = lambda a, n: a.reshape(n, P).T
    x = np.concatenate([i["x"][0], i["ctx"][0]], 0).T
    o["x_blocks"] = x.reshape(KC, P, TOK)
    o["cond"] = np.stack([col(i["c"][0], KC), col(i["c_ctx"], KC)], 2)
    o["norm_g"] = np.stack([col(i["norm_g"][l], KC) for l in range(DEPTH)] + [col(i["final_g"], KC)], 1)
    o["b_ada"] = np.stack([col(i["b_ada"][l], N_ADA) for l in range(DEPTH)], 1)
    o["conv_w"] = np.stack([np.stack([col(i["hy_conv_w"][l, t], 6) for t in range(3)] + [col(i["hy_conv_b"][l], 6)], 2)
                            for l in range(DEPTH)], 1)
    two = lambda a: np.concatenate([a, a])
    o["f_small"] = np.stack([np.stack([two(i[n][l]) for n in ("hy_b1", "hy_freq1", "hy_b2", "hy_freq2")], 1)
                             for l in range(DEPTH)], 1)
    o["sink"] = np.broadcast_to(i["sink"][None][:, :, list(C_HEAD_ORDER)], (P, DEPTH, 6))
    w12 = np.zeros((DEPTH, P, 2, P), f)
    w3 = np.zeros((DEPTH, 2, P, 512), f)
    for l in range(DEPTH):
        for e in range(2):
            w12[l, 33 * e:33 * e + 33, 0, 64 * e:64 * e + 64] = i["hy_w1"][l]
            w12[l, 64 * e:64 * e + 64, 1, 64 * e:64 * e + 64] = i["hy_w2"][l]
            w3[l, e, 64 * e:64 * e + 64] = i["hy_w3"][l][:, 512 * e:512 * e + 512]
    o["w12"], o["w3"] = w12, w3
    o["hy_d"] = i["hy_d"]
    rel = np.arange(GRID)[None, :] - np.arange(GRID)[:, None] + 15
    padded = np.concatenate([i["na_rpb"], np.zeros(i["na_rpb"].shape[:3] + (1,), f)], 3)
    rel = np.where((rel < 0) | (rel > 30), 31, rel)
    o["rpb"] = padded[:, :, :, rel].transpose(0, 1, 3, 2, 4)
    o["ident"] = np.eye(P, dtype=f)
    o["dft_f"], o["dft_i"] = dft_tables()
    o["rope"] = np.stack(rope_tables(), 1)
    o["m_cols"], o["m_rows"], o["m_win"] = attention_masks()
    o["feats"], o["decay"] = filter_tables(SEQ)
    o["feats_ctx"], o["decay_ctx"] = filter_tables(CTX)
    return {k: np.ascontiguousarray(v, f) for k, v in o.items()}


def kernel(**inputs):
    import concourse.bacc as bacc
    from concourse.bass_utils import run_bass_kernel_spmd

    arrays = lay_out(inputs)
    nc = bacc.Bacc("TRN2", target_bir_lowering=False, num_devices=1)
    aps = {k: nc.dram_tensor(f"in_{k}", v.shape, F32, kind="ExternalInput").ap() for k, v in arrays.items()}
    aps["x_mid"] = nc.dram_tensor("x_mid", (KC, P, TOK), F32, kind="Internal").ap()
    aps["gates"] = nc.dram_tensor("gates", (N_G, P, TOK), F32, kind="Internal").ap()
    aps["out"] = nc.dram_tensor("out_fm", (KC, P, SEQ), F32, kind="ExternalOutput").ap()
    build(nc, aps)
    r = run_bass_kernel_spmd(nc, [{f"in_{k}": v for k, v in arrays.items()}], core_ids=[0])
    return np.ascontiguousarray(r.results[0]["out_fm"].reshape(D, SEQ).T)[None]
```

```python
import math
from contextlib import ExitStack

import numpy as np

import concourse.bass as bass
from concourse import mybir

F32, F32R = mybir.dt.float32, mybir.dt.float32r
ALU = mybir.AluOpType
ACT = mybir.ActivationFunctionType

P = 128
D = 1024
KC = D // P
SEQ, CTX = 1024, 256
TOK = SEQ + CTX
NT, NTC = SEQ // P, CTX // P
DEPTH = 2
GRID = 64
CH = 256
HD = 64
QSCALE = HD ** -0.5
EPS = 1e-6
NEG = -1e30
LOWEST = -3.0e38

N_ADA, N_PB, N_Q, N_K, N_V, N_G, N_OUT = 24, 6, 6, 4, 4, 8, 8
RING = 4
N_EARLY = 2 * KC
LATE = ([(0, "ada", b) for b in range(N_EARLY, N_ADA)] + [(1, "ada", b) for b in range(N_EARLY)],
        [(1, "ada", b) for b in range(N_EARLY, N_ADA)])
LATE_PER = (2, 1)
LATE_LAST = len(LATE[0]) - LATE_PER[0] * (N_Q + N_K)


def stream():
    stage = lambda l, name, n: [(l, name, b) for b in range(n)]
    out = []
    for l in range(DEPTH):
        late = list(LATE[l])
        out += stage(l, "pb", N_PB) + stage(l, "g", N_G)
        out += stage(l, "v", N_V)
        for block in stage(l, "k", N_K) + stage(l, "q", N_Q):
            out, late = out + [block] + late[:LATE_PER[l]], late[LATE_PER[l]:]
        out += late + stage(l, "out", N_OUT)
    return out


STREAM = stream()
STREAM_AT = {block: i for i, block in enumerate(STREAM)}
assert len(STREAM) % RING == 0 and all(i % 2 == 0 for (_, name, b), i in STREAM_AT.items() if b == 0 and name in ("pb", "out"))

MIX_B, MIX_A, MIX_C = 0, 2, 5
C_HEAD_ORDER = (0, 3, 1, 4, 2, 5)

SLOT_R = (0, 8, 4, 2, 6, 1, 3, 7, 5)
NS_MAIN, NS_CTX = 9, 3
DFT_START = [0, 2, 4, 7, 10, 13, 16, 19, 22]
N_DFT = 25
SQ5, C1, S1 = math.sqrt(0.5), math.cos(math.pi / 8), math.sin(math.pi / 8)

TWO_PI_A, TWO_PI_B = 6.28125, 0.0019340515136718750
TWO_PI_C = 2 * math.pi - TWO_PI_A - TWO_PI_B
ROUND = 12582912.0


def dft_tables():
    p = np.arange(P, dtype=np.float64)
    fwd, inv = [], []
    for slot, r in enumerate(SLOT_R):
        theta = 2 * np.pi * (p[:, None] * r / 2048 + p[:, None] * p[None, :] / P)
        c, s = np.cos(theta), np.sin(theta)
        g = (1.0 if r in (0, 8) else 2.0) / 2048
        fwd += [c, -s] if slot < 2 else [c, s, -s]
        inv += [g * c.T, -g * s.T] if slot < 2 else [g * c.T, g * s.T, -g * s.T]
    pack = lambda m: np.stack(m, 1).astype(np.float32)
    return pack(fwd), pack(inv)


def rope_tables():
    pos = np.arange(SEQ)
    row, col = pos // GRID, pos % GRID
    inv = 10000.0 ** (-np.arange(16) / 16.0)
    cos, sin = np.zeros((P, SEQ)), np.zeros((P, SEQ))
    for d in range(P):
        e = d % HD
        ang = (row if e < 32 else col) * inv[e % 16]
        cos[d] = np.cos(ang)
        sin[d] = np.sin(ang) * (-1 if e % 32 < 16 else 1)
    return cos.astype(np.float32), sin.astype(np.float32)


def attention_masks():
    c = np.arange(GRID)
    c0 = np.clip(c - 8, 0, GRID - 16)
    ok = (c[None, :] >= c0[:, None]) & (c[None, :] < c0[:, None] + 16)
    cols = np.where(ok, 0, NEG)
    cols = np.concatenate([cols, cols]).astype(np.float32)
    rows = np.zeros((P, 10, GRID), np.float32)
    for par in range(2):
        for i in range(10):
            dr = i - 4 - par
            if not -4 <= dr <= 3:
                rows[64 * par:64 * par + 64, i] = NEG
    q, k = np.arange(P)[:, None], np.arange(3 * P)[None, :] - P
    window = np.where(np.abs(q - k) <= 128, 0, NEG).astype(np.float32)
    return cols, rows.reshape(P, 640), window


def filter_tables(L):
    t = np.linspace(0.0, 1.0, L, dtype=np.float32)
    w = (np.float32(2.0 * math.pi / L) * np.arange(L, dtype=np.float32)).astype(np.float32)
    f = np.linspace(1e-4, 15, 16, dtype=np.float32)
    a = (f[:, None] * w[None, :]).astype(np.float32).astype(np.float64)
    z = np.concatenate([t[None].astype(np.float64), np.cos(a), -np.sin(a)], 0)
    back = (L - np.arange(L)) % L
    feats = np.concatenate([z, z[:, back]], 0).astype(np.float32)
    lo, hi = math.log(1e-2) / 1.5, math.log(1e-2) / 0.3
    deltas = np.abs(np.linspace(lo, hi, CH, dtype=np.float32)).astype(np.float64)
    dec = np.exp(-t.astype(np.float64)[:, None] * deltas[None])
    late = dec[back]
    late[0] = 0.0
    both = np.concatenate([dec, late], 0).reshape(2 * L // P, P, CH)
    return feats, both.transpose(1, 0, 2).astype(np.float32)


def build(nc, A):
    ctx = ExitStack()
    with ctx:
        def sb(name, shape):
            return ctx.enter_context(nc.sbuf_tensor(name, shape, F32))

        R_SIZE = 26000
        with ExitStack() as places:
            def sb_r(name, shape):
                return places.enter_context(nc.sbuf_tensor(name, shape, F32R))
            act_r, mix_r, ring_r = sb_r("act_r", [P, KC, TOK]), sb_r("mix_r", [P, KC, TOK]), sb_r("ring_r", [P, RING, KC, P])
            region_r, w_hi = sb_r("region_r", [P, R_SIZE]), sb_r("w_hi", [P, 2, KC, P])
        act_t = sb("act_t", [P, KC, TOK])
        mix = sb("mix", [P, KC, TOK])
        ring = sb("ring", [P, RING, KC, P])
        region = sb("region", [P, R_SIZE])
        g_st = sb("g_st", [P, 2, 512])
        w12 = sb("w12", [P, 2, P])
        sb("w_hi_rest", [P, 2 * KC * P - 2 * 512 - 2 * P])
        ident = sb("ident", [P, P])
        ones = sb("ones", [P, P])
        condT = sb("condT", [P, KC, 2])
        silu_c = sb("silu_c", [P, KC, 2])
        norm_g = sb("norm_g", [P, DEPTH + 1, KC])
        b_ada = sb("b_ada", [P, DEPTH, N_ADA])
        ada = sb("ada", [P, DEPTH, N_ADA, 2])
        mod_a = sb("mod_a", [P, KC, 2])
        conv_w = sb("conv_w", [P, DEPTH, N_PB, 4])
        f_small = sb("f_small", [P, DEPTH, 4])
        sink = sb("sink", [P, DEPTH, 6])
        ps = ctx.enter_context(nc.psum_tensor("ps", [P, 8, 512], F32))

        def view(start, *shape):
            n = int(np.prod(shape))
            assert start + n <= R_SIZE, (start, shape)
            v = region[:, start:start + n]
            if len(shape) == 2:
                v = v.rearrange("p (a b) -> p a b", b=shape[1])
            if len(shape) == 3:
                v = v.rearrange("p (a b c) -> p a b c", b=shape[1], c=shape[2])
            return v

        sq = view(9216, 2, TOK)
        sq_sum = view(11776, TOK)
        rstd = view(7424, TOK)
        spec = view(0, NS_MAIN, 2, CH)
        khat = view(4608, NS_MAIN, 2, CH)
        decay = view(4608, 2 * NT, CH)
        z_tm = view(9216, NT + NTC, CH)
        x1_tm = view(11776, NT + NTC, CH)
        dft_f = view(14336, N_DFT, P)
        dft_i = view(17536, N_DFT, P)
        PAD = TOK + 4
        pc_in = view(20736, 2, PAD)
        pc_out = view(20736 + 2 * PAD, 2, PAD)
        hid = view(20736, SEQ)
        w3f = view(21760, 2 * CH)
        w3r = view(22272, 2 * CH)
        k_rt = view(22784, CH)
        k_s = view(23040, CH)
        prod = view(23296, 2, 2, 2 * CH)
        mlp = [view(1024 * i, SEQ) for i in range(3)]
        feats = view(3072, SEQ)
        early_w = [mix[:].rearrange("p a b -> p (a b)")[:, 2048 * i:2048 * (i + 1)] if i < 5 else
                   view(3072 + 2048 * (i - 5), 2048) for i in range(KC)]
        d_row = view(25600, CH)
        room = mix[:, 2:8, :].rearrange("p a b -> p (a b)").rearrange("p (u c) -> p u c", c=CH)
        k_fm = view(0, N_K, TOK)
        v_tm = view(5120, NT + NTC, 512)
        t_raw = view(10240, 6, 14, GRID)
        rope_cs = view(10240, 2, SEQ)
        rope_t = view(12288, 2, SEQ)
        t_edge = view(15616, 2, 896)
        t_inner = view(17408, 2, 640)
        s_sb = view(18688, 2, 896)
        p_sb = view(20480, 2, 896)
        pt_sb = view(22272, 2, 896)
        q_st = view(24064, 2, 2, P)
        o_sb = view(24576, 2, P)
        m_cols = view(24832, GRID)
        m_rows = view(24896, 640)
        m_win = view(25536, 3 * P)
        stat = view(25920, 32)
        v_hi, v_lo = (region_r[:, at:at + N_V * KC * P].rearrange("p (k m) -> p k m", m=512) for at in (0, 10240))
        h_hi = region_r[:, 15616:15616 + KC * TOK].rearrange("p (k t) -> p k t", t=TOK)

        def mix_hi(k):
            at = 18176 + k * TOK if k < 6 else 5120 + (k - 6) * TOK
            return region_r[:, at:at + TOK]
        g_in = view(15616, 2, TOK)
        x_in = view(0, 2, TOK)
        fin = view(2560, 2, SEQ)

        def sem(name):
            return ctx.enter_context(nc.semaphore(name))

        L2 = range(DEPTH)

        def per_layer(name):
            return [sem(f"{name}{l}") for l in L2]

        consts_in, consts_set, cond_in, silu_ready = sem("consts_in"), sem("consts_set"), sem("cond_in"), sem("silu_ready")
        early_in, early_done = [sem(f"early_in{b}") for b in range(2)], sem("early_done")
        x_loaded = [sem(f"x_loaded{b}") for b in range(2)]
        slot_in = [sem(f"slot_in{s}") for s in range(RING)]
        block_done = sem("block_done")
        block_taken = sem("block_taken")
        sq_ready = [sem(f"sq_ready{l}") for l in range(DEPTH + 1)]
        sq_used = [sem(f"sq_used{l}") for l in range(DEPTH + 1)]
        ms_mm, ms_ready, std_ready = sem("ms_mm"), sem("ms_ready"), sem("std_ready")
        ada_ready, scaled, h_ready = sem("ada_ready"), per_layer("scaled"), per_layer("h_ready")
        pads_set, dft_in, pc_ready, conv_ready = sem("pads_set"), per_layer("dft_in"), per_layer("pc_ready"), per_layer("conv_ready")
        tp_ready, tp_taken = per_layer("tp_ready"), per_layer("tp_taken")
        net_in = per_layer("net_in")
        fl_in, dec_in, drow_in = per_layer("fl_in"), per_layer("dec_in"), per_layer("drow_in")
        mlp_mm, arg_ready, hid_ready = per_layer("mlp_mm"), per_layer("arg_ready"), per_layer("hid_ready")
        tap_mm, tap_ready, tsq_ready, tsq_used = (per_layer(x) for x in ("tap_mm", "tap_ready", "tsq_ready", "tsq_used"))
        en_ready, rt_ready = per_layer("en_ready"), per_layer("rt_ready")
        bf_ready, x_mm, x_taken, prod_ready = (per_layer(x) for x in ("bf_ready", "x_mm", "x_taken", "prod_ready"))
        y_part, w_mm, w_taken = (per_layer(x) for x in ("y_part", "w_mm", "w_taken"))
        yt_ready, yt_mm, yt_taken, hyena_done = (per_layer(x) for x in ("yt_ready", "yt_mm", "yt_taken", "hyena_done"))
        hi_made, lo_made = sem("hi_made"), sem("lo_made")
        v_hi_made, h_hi_made, h_split, mix_hi_made, mix_split = (
            per_layer(x) for x in ("v_hi_made", "h_hi_made", "h_split", "mix_hi_made", "mix_split"))
        v_mm, v_taken, rope_in, rope_done = (per_layer(x) for x in ("v_mm", "v_taken", "rope_in", "rope_done"))
        masks_in, traw_in, qst_zero = per_layer("masks_in"), per_layer("traw_in"), sem("qst_zero")
        qst_ready, s_ready, neg_ready, p_ready = sem("qst_ready"), sem("s_ready"), sem("neg_ready"), sem("p_ready")
        es_ready, pt_ready, pt_dve, pt_act = sem("es_ready"), sem("pt_ready"), sem("pt_dve"), sem("pt_act")
        o_ready, on_ready, ot_ready, ot_taken = sem("o_ready"), sem("on_ready"), sem("ot_ready"), sem("ot_taken")
        unit_step = sem("unit_step")
        g_mm, g_taken, mix_gated = (per_layer(x) for x in ("g_mm", "g_taken", "mix_gated"))
        g_stored = [[sem(f"g_stored{l}_{b}") for b in range(2)] for l in L2]
        g_in_in = [[sem(f"g_in_in{l}_{b}") for b in range(2)] for l in L2]
        xin_in = [[sem(f"xin_in{l}_{b}") for b in range(2)] for l in L2]
        x_stored, fin_ready = sem("x_stored"), sem("fin_ready")
        fin_out = [sem(f"fin_out{b}") for b in range(2)]
        vec_step = sem("vec_step")

        stat_h = view(R_SIZE - 8, 8)

        def back_tiles(isctx):
            return [(b, NT, NTC) for b in range(2)] if isctx else [(b, t, 4) for b in range(2) for t in (0, 4)]

        class Steps:
            def __init__(self, eng):
                self.eng, self.open, self.at = eng, {}, {}

            def __call__(self, ins, sem=None):
                s = vec_step if sem is None else sem
                self.at[s.name] = self.at.get(s.name, 0) + 1
                ins.then_inc(s, 1)
                self.open[s.name] = (s, self.at[s.name])

            def join(self):
                for s, n in self.open.values():
                    self.eng.wait_ge(s, n)
                self.open = {}

        def ntok(l):
            return TOK if l == 0 else SEQ

        def norm_parts(n):
            return [(0, SEQ), (SEQ, TOK)][:1 if n == SEQ else 2]

        def groups(n):
            return [(t, min(512, n - t)) for t in range(0, n, 512)]

        TAKEN = N_PB + N_Q + N_K + N_OUT

        def taken_before(l, stage):
            return l * TAKEN + dict(pb=0, k=N_PB, q=N_PB + N_K, out=TAKEN - N_OUT, end=TAKEN)[stage]

        SPLIT = [STREAM_AT[l, name, b] for l in L2 for name, n in (("k", N_K), ("q", N_Q), ("out", N_OUT)) for b in range(n)]

        def split_before(l, stage):
            return l * (N_K + N_Q + N_OUT) + (N_K + N_Q if stage == "out" else 0)

        def gate_parts(l):
            return [(b, t, w) for b in range(N_G) for t, w in groups(ntok(l))]

        def done_at(l, stage):
            return STREAM_AT[l, stage, 0]

        FILLS = [[(2, 2, 3, 0, 3), (0, 2, 3, 0, 3), (0, 1, 1, 1, 2), (0, 1, 1, 1, 2)], [(2, 2, 2, 0, 3), (0, 2, 2, 0, 4)]]

        def time_tiles(l):
            return [(0, 4), (4, 4), (8, 2)] if l == 0 else [(0, 4), (4, 4)]

        def sq_t(i):
            return room[:, 16 + 2 * (i % 2):18 + 2 * (i % 2)].rearrange("p a b -> p (a b)")

        def jobs(l):
            main = [(False, o, NS_MAIN, NT) for o in range(2)]
            return main + ([(True, o, NS_CTX, NTC) for o in range(2)] if l == 0 else [])

        def q_tiles(l):
            near = {0: 0, 1: 0, 6: 4, 7: 4}
            a = [(j, near[j], 4) if j in near else (j, j - 2, 5) for j in range(NT)]
            c = [(j, max(j - 1, 0), 2 if j in (0, NT - 1) else 3) for j in range(NT)]
            x = [(NT + j, 0, 0) for j in range(NTC)] if l == 0 else []
            return [(kind, *where, *tile) for kind, tiles in (("A", a), ("A", x), ("C", c), ("C", x)) for tile in tiles
                    for where in [(MIX_A, None, 0) if kind == "A" else (MIX_C, N_K - 1, 384)]]

        def steps_of(tiles):
            return 2 + sum(2 * (2 if n else 1) + (2 if kind == "C" else 1) for kind, _, _, _, _, _, n in tiles)

        def sinks_of(tiles, units):
            return sum(tiles[k // 2][0] == "C" for k in range(units))

        before = [(0, 0, 0)]
        for l in L2:
            tiles = q_tiles(l)
            u, c, st = before[-1]
            before.append((u + 6 * len(tiles), c + 3 * sinks_of(tiles, 2 * len(tiles)), st + 3 * steps_of(tiles)))

        def chunks(tile):
            first, n = tile[5:]
            return [(i * P, NT + i) for i in range(NTC)] + [(CTX + i * P, first + i) for i in range(n)]

        block = ctx.enter_context(nc.Block())

        @block.sync
        def _(sp):
            for k in range(KC):
                if k >= 2:
                    sp.wait_ge(early_in[k % 2], 16 * (k // 2))
                sp.dma_start(early_w[k], A["early"][k]).then_inc(early_in[k % 2], 16)
            for s in range(RING):
                sp.dma_start(ring[:, s].rearrange("p k m -> p (k m)"), A["weights"][s]).then_inc(slot_in[s], 16)
            with sp.Fori(1, len(STREAM) // RING) as i:
                for s in range(RING):
                    sp.wait_ge(block_done, i * RING + (s + 1 - RING))
                    sp.dma_start(ring[:, s].rearrange("p k m -> p (k m)"),
                                 A["weights"][bass.ds(i * RING + s, 1)].rearrange("a p f -> (a p) f")
                                 ).then_inc(slot_in[s], 16)

        @block.gpsimd
        def _(pool):
            g = nc.gpsimd
            g.memset(ones[:], 1.0).then_inc(consts_set, 1)
            for k in range(KC):
                if k >= 2:
                    pool.wait_ge(x_loaded[k % 2], 16 * (k // 2))
                pool.dma_start(act_t[:, k], A["x_blocks"][k]).then_inc(x_loaded[k % 2], 16)
            for dst, src in ((ident[:], A["ident"]), (norm_g[:], A["norm_g"]),
                             (b_ada[:], A["b_ada"]), (conv_w[:], A["conv_w"]), (f_small[:], A["f_small"]),
                             (sink[:], A["sink"])):
                pool.dma_start(dst, src).then_inc(consts_in, 16)
            for l in L2:
                if l:
                    pool.wait_ge(block_taken, taken_before(l, "pb"))
                else:
                    pool.wait_ge(early_done, KC)
                pool.dma_start(w12[:], A["w12"][l]).then_inc(net_in[l], 16)
                pool.dma_start(feats[0:66, 0:SEQ], A["feats"]).then_inc(net_in[l], 16)
                for b in range(2):
                    g.memset(pc_in[:, b, 0:1], 0.0).then_inc(pads_set, 1)
                    g.memset(pc_in[:, b, SEQ + 1:SEQ + 3], 0.0).then_inc(pads_set, 1)
                    g.memset(pc_in[:, b, PAD - 1:PAD], 0.0).then_inc(pads_set, 1)
                pool.dma_start(dft_f, A["dft_f"]).then_inc(dft_in[l], 16)
                pool.dma_start(dft_i, A["dft_i"]).then_inc(dft_in[l], 16)
                pool.wait_ge(conv_ready[l], N_PB)
                pool.wait_ge(tp_ready[l], 4 * len(time_tiles(l)))
                pool.dma_start(w3f, A["w3"][l, 0]).then_inc(fl_in[l], 16)
                pool.dma_start(w3r, A["w3"][l, 1]).then_inc(fl_in[l], 16)
                conv_n = x_n = 0
                for ji, (isctx, o, ns, nt) in enumerate(jobs(l)):
                    nm = "_ctx" if isctx else ""
                    if o == 0 and isctx:
                        pool.wait_ge(yt_ready[l], 1)
                        pool.dma_start(feats[0:66, 0:nt * P], A["feats_ctx"]).then_inc(net_in[l], 16)
                    if ji:
                        pool.wait_ge(x_taken[l], x_n)
                    pool.dma_start(decay[:, 0:2 * nt], A["decay" + nm]).then_inc(dec_in[l], 16)
                    pool.dma_start(d_row[0:1], A["hy_d"][l, o:o + 1]).then_inc(drow_in[l], 16)
                    x_n += ns
                    for s in range(ns):
                        pr_a, pr_b = prod[:, conv_n % 2, 0], prod[:, conv_n % 2, 1]
                        x_n += 1
                        conv_n += 1
                        pool.wait_ge(prod_ready[l], conv_n)
                        pool.wait_ge(x_taken[l], x_n)
                        g.tensor_tensor(spec[:, s, 0], pr_a[:, 0:CH], pr_b[:, CH:], ALU.subtract).then_inc(y_part[l], 1)
                        g.tensor_tensor(spec[:, s, 1], pr_a[:, CH:], pr_b[:, 0:CH], ALU.add).then_inc(y_part[l], 1)
                pool.wait_ge(hyena_done[l], 1)
                pool.wait_ge(v_taken[l], NT + NTC)
                pool.dma_start(rope_cs, A["rope"]).then_inc(rope_in[l], 16)
                pool.wait_ge(rope_done[l], 1)
                for h in range(6):
                    for par in range(2):
                        pool.dma_start(t_raw[64 * par:64 * par + 64, h].rearrange("p a b -> p (a b)"),
                                       A["rpb"][l, h, :, 1 - par:15 - par].rearrange("p a b -> p (a b)")
                                       ).then_inc(traw_in[l], 16)
                pool.wait_ge(block_done, STREAM_AT[l, "q", N_Q - 1] + 1)
                g.memset(q_st.rearrange("p a b c -> p (a b c)"), 0.0).then_inc(qst_zero, 1)
                for dst, src in ((m_cols, "m_cols"), (m_rows, "m_rows"), (m_win, "m_win")):
                    pool.dma_start(dst, A[src]).then_inc(masks_in[l], 16)
                pool.wait_ge(neg_ready, before[l][0] + 4 * len(q_tiles(l)) + 2 * NT)
                for b in range(2):
                    pool.wait_ge(g_stored[l][b], 16 * (len(gate_parts(l)) // 2))

                def load_gate(m):
                    pool.dma_start(g_in[:, m % 2, 0:ntok(l)], A["gates"][m, :, 0:ntok(l)]).then_inc(g_in_in[l][m % 2], 16)
                load_gate(0)
                load_gate(1)
                tiles_before, n_tiles = before[l][0] // 2, len(q_tiles(l))
                for m in range(N_G):
                    if m == 0:
                        pool.wait_ge(ot_taken, tiles_before + 3 * n_tiles - n_tiles // 2)
                    if m == N_G - 1:
                        pool.wait_ge(ot_taken, tiles_before + 3 * n_tiles)
                    pool.wait_ge(g_in_in[l][m % 2], 16 * (m // 2 + 1))
                    g.tensor_tensor(mix[:, m, 0:ntok(l)], mix[:, m, 0:ntok(l)], g_in[:, m % 2, 0:ntok(l)],
                                    ALU.mult).then_inc(mix_gated[l], 1)
                    if m + 2 < N_G:
                        pool.wait_ge(mix_gated[l], m + 1)
                        load_gate(m + 2)
                if l:
                    pool.wait_ge(x_stored, 16 * KC)
                for m in range(KC):
                    if m >= 2:
                        pool.wait_ge(block_taken, taken_before(l, "out") + m - 1)
                    pool.dma_start(x_in[:, m % 2], A["x_mid" if l else "x_blocks"][m]).then_inc(xin_in[l][m % 2], 16)
                    if l == 0 and m >= 1:
                        pool.wait_ge(block_taken, taken_before(l, "out") + m)
                        pool.dma_start(A["x_mid"][m - 1], act_t[:, m - 1]).then_inc(x_stored, 16)
                if l == 0:
                    pool.wait_ge(block_taken, taken_before(l, "end"))
                    pool.dma_start(A["x_mid"][KC - 1], act_t[:, KC - 1]).then_inc(x_stored, 16)
            for m in range(KC):
                pool.wait_ge(fin_ready, m + 1)
                pool.dma_start(A["out"][m], fin[:, m % 2]).then_inc(fin_out[m % 2], 16)
            for b in range(2):
                pool.wait_ge(fin_out[b], 16 * KC // 2)

        @block.tensor
        def _(pe):
            mm, tr = nc.tensor.matmul, nc.tensor.transpose
            at = [0]

            def over_blocks(n, emit):
                done = 0
                while done < n:
                    turns, base = (n - done) // RING, at[0] // RING
                    if at[0] % RING == 0 and turns >= 2:
                        with pe.Fori(0, turns) as i:
                            for s in range(RING):
                                pe.wait_ge(slot_in[s], (i + (base + 1)) * 16)
                                emit(i * RING + (done + s), s)
                        done += turns * RING
                        at[0] += turns * RING
                    else:
                        s = at[0] % RING
                        pe.wait_ge(slot_in[s], 16 * (base + 1))
                        emit(done, s)
                        done += 1
                        at[0] += 1

            def project_split(hi, lo, n, first_taken, first_split, src_ready):
                def emit(idx, s, parity=None):
                    parity = s % 2 if parity is None else parity
                    pe.wait_ge(block_taken, idx + (first_taken - 1))
                    pe.wait_ge(lo_made, idx + (first_split + 1))
                    for k in range(KC):
                        if idx == 0 if isinstance(idx, int) else s == 0:
                            pe.wait_ge(src_ready, k + 1)
                        gs = [(ps[:, 3 * parity + gi, 0:w], t, w) for gi, (t, w) in enumerate(groups(n))]
                        for out, t, w in gs:
                            mm(out, w_hi[:, parity, k], hi(k)[:, t:t + w], start=(k == 0), stop=False)
                            mm(out, w_hi[:, parity, k], lo[:, k, t:t + w], start=False, stop=False)
                        for out, t, w in gs:
                            last = mm(out, ring_r[:, s, k], hi(k)[:, t:t + w], start=False, stop=(k == KC - 1))
                    last.then_inc(block_done, 1)
                return emit

            def project(src, n, first_taken, src_ready=None, per_chunk=1):
                def emit(idx, s, parity=None):
                    parity = s % 2 if parity is None else parity
                    if first_taken or not isinstance(idx, int) or idx >= 2:
                        pe.wait_ge(block_taken, idx + (first_taken - 1))
                    for k in range(KC):
                        if src_ready is not None and (idx == 0 if isinstance(idx, int) else s == 0):
                            pe.wait_ge(src_ready, (k + 1) * per_chunk)
                        for gi, (t, w) in enumerate(groups(n)):
                            last = mm(ps[:, 3 * parity + gi, 0:w], ring[:, s, k], src[:, k, t:t + w],
                                      start=(k == 0), stop=(k == KC - 1))
                    last.then_inc(block_done, 1)
                return emit

            def sum_of_squares(l, n):
                pe.wait_ge(sq_used[l], KC - 1)
                for gi, (t, w) in enumerate(groups(n)):
                    last = mm(ps[:, gi, 0:w], ones[:], sq_sum[:, t:t + w], start=True, stop=True)
                last.then_inc(ms_mm, 1)

            def transform(mats, slot, bank, inverse):
                m0, out = DFT_START[slot], ps[:, bank]
                if slot < 2 and not inverse:
                    mm(out[:, 0:CH], mats[:, m0], spec[:, slot, 0], start=True, stop=True)
                    return mm(out[:, CH:], mats[:, m0 + 1], spec[:, slot, 0], start=True, stop=True)
                if slot < 2:
                    mm(out[:, 0:CH], mats[:, m0], spec[:, slot, 0], start=True, stop=False)
                    return mm(out[:, 0:CH], mats[:, m0 + 1], spec[:, slot, 1], start=False, stop=True)
                plus, minus = (m0 + 2, m0 + 1) if inverse else (m0 + 1, m0 + 2)
                mm(out, mats[:, m0], spec[:, slot].rearrange("p a c -> p (a c)"), start=True, stop=False,
                   skip_group_check=True)
                mm(out[:, 0:CH], mats[:, plus], spec[:, slot, 1], start=False, stop=False, skip_group_check=True)
                return mm(out[:, CH:], mats[:, minus], spec[:, slot, 0], start=False, stop=True, skip_group_check=True)

            def network(l, layer, isctx, bank, n):
                if layer == 0:
                    pe.wait_ge(net_in[l], 16 * (2 + isctx))
                else:
                    pe.wait_ge(hid_ready[l], 2 * isctx + 1)
                for gi, (t, w) in enumerate(groups(n)):
                    lhs, rhs = (w12[0:66, 0], feats[0:66, t:t + w]) if layer == 0 else (w12[:, 1], mlp[2][:, t:t + w])
                    last = mm(ps[:, bank + gi, 0:w], lhs, rhs, start=True, stop=True)
                last.then_inc(mlp_mm[l], 1)

            def hyena(l, fill):
                taps = bf = xn = wn = 0
                for ji, (isctx, o, ns, nt) in enumerate(jobs(l)):
                    at_start, at_taps, at_signal, at_slot, at_end = FILLS[l][ji]
                    fill(at_start)
                    if ji == 0:
                        pe.wait_ge(fl_in[l], 32)
                        pe.wait_ge(block_taken, taken_before(l, "k"))
                    if o == 0:
                        if isctx:
                            for layer in range(2):
                                network(l, layer, isctx, 2 * layer, nt * P)
                        pe.wait_ge(hid_ready[l], 2 * isctx + 2)
                    if isctx and o == 0:
                        pe.wait_ge(yt_taken[l], 4)
                    for i in range(nt):
                        if taps >= 2:
                            pe.wait_ge(tap_ready[l], taps - 1)
                        for e in range(2):
                            t = 2 * i + e
                            last = mm(ps[:, 4 + taps % 2, e * CH:(e + 1) * CH], hid[:, (t % nt) * P:(t % nt + 1) * P],
                                      (w3f if t < nt else w3r)[:, o * CH:(o + 1) * CH], start=True, stop=True)
                        last.then_inc(tap_mm[l], 1)
                        taps += 1
                    for i in range(nt):
                        pe.wait_ge(tsq_ready[l], taps - nt + i + 1)
                        mm(ps[:, 1], ones[:], sq_t(i), start=(i == 0), stop=(i == nt - 1)).then_inc(tsq_used[l], 1)
                    if ji == 0:
                        pe.wait_ge(dft_in[l], 32)
                    fill(at_taps)
                    for signal in range(2):
                        if signal:
                            fill(at_signal)
                        for s in range(ns + signal):
                            if s < ns:
                                pe.wait_ge(bf_ready[l], bf + s + 1)
                                if xn >= 2:
                                    pe.wait_ge(x_taken[l], xn - 1)
                                transform(dft_f, s, xn % 2, False).then_inc(x_mm[l], 1)
                                xn += 1
                            if signal and s >= 1:
                                pe.wait_ge(y_part[l], 2 * (wn + 1))
                                if wn >= 2:
                                    pe.wait_ge(w_taken[l], wn - 1)
                                transform(dft_i, s - 1, 2 + wn % 2, True).then_inc(w_mm[l], 1)
                                wn += 1
                                if s in (3, 6):
                                    fill(at_slot)
                        bf += ns
                    fill(at_end)
                    if o == 1:
                        pe.wait_ge(yt_ready[l], 1 + isctx)
                        for gi, (b, t0, w) in enumerate(back_tiles(isctx)):
                            if gi >= 2 or isctx:
                                pe.wait_ge(yt_taken[l], 4 * isctx + gi - 1 if gi >= 2 else 4)
                            for e in range(w):
                                last = tr(ps[:, 4 + gi % 2, e * P:(e + 1) * P], z_tm[:, t0 + e, b * P:(b + 1) * P], ident[:])
                            last.then_inc(yt_mm[l], 1)

            def attention(l):
                tiles = q_tiles(l)
                base, _, _ = before[l]
                nu = 2 * len(tiles)
                with pe.Fori(0, 3) as pr:
                    u0 = pr * nu + base
                    w0 = pr * (nu // 2) + base // 2

                    def keys(kb, t0, n):
                        if kb is None:
                            return k_fm[:, bass.ds(pr, 1), t0:t0 + n].rearrange("p a b -> p (a b)")
                        return k_fm[:, kb, t0:t0 + n]

                    def scores(k):
                        ji, par = divmod(k, 2)
                        _, _, kb, _, _, first, n = tiles[ji]
                        if par == 0:
                            pe.wait_ge(qst_ready, u0 + (k + 2))
                        if k >= 2:
                            pe.wait_ge(neg_ready, u0 + (k - 1))
                        bank, q = 2 * (k % 2), q_st[:, ji % 2, par]
                        if n:
                            w = min(n, 4) * P
                            mm(ps[:, bank, 0:w], q, keys(kb, first * P, w), start=True, stop=True)
                        if n > 4:
                            mm(ps[:, bank + 1, 0:P], q, keys(kb, (first + 4) * P, P), start=True, stop=True)
                        mm(ps[:, bank + 1, P:P + CTX], q, keys(kb, SEQ, CTX), start=True, stop=True).then_inc(s_ready, 1)

                    def transpose_p(k):
                        pe.wait_ge(p_ready, u0 + (k + 1))
                        if k >= 1:
                            pe.wait_ge(pt_dve, u0 + k)
                            pe.wait_ge(pt_act, u0 + k)
                        cs = chunks(tiles[k // 2])
                        half = (len(cs) + 1) // 2
                        for c, (col, _) in enumerate(cs):
                            bank, at_col = (4, c) if c < half else (5, c - half)
                            last = tr(ps[:, bank, at_col * P:(at_col + 1) * P], p_sb[:, k % 2, col:col + P], ident[:])
                        last.then_inc(pt_ready, 1)

                    def times_v(k):
                        ji, par = divmod(k, 2)
                        kb, vcol = tiles[ji][2:4]
                        pe.wait_ge(pt_dve, u0 + (k + 1))
                        pe.wait_ge(pt_act, u0 + (k + 1))
                        if par == 0 and ji >= 2:
                            pe.wait_ge(ot_taken, w0 + (ji - 1))
                        cs = chunks(tiles[ji])
                        for c, (_, t) in enumerate(cs):
                            v = v_tm[:, t, bass.ds(pr * P + par * HD, HD)] if kb is None else \
                                v_tm[:, t, vcol + par * HD:vcol + (par + 1) * HD]
                            last = mm(ps[:, 6 + ji % 2, par * HD:(par + 1) * HD], pt_sb[:, k % 2, c * P:(c + 1) * P], v,
                                      start=(c == 0), stop=(c == len(cs) - 1))
                        last.then_inc(o_ready, 1)

                    def transpose_o(w):
                        pe.wait_ge(on_ready, u0 + (2 * w + 2))
                        tr(ps[:, 6 + w % 2, P:2 * P], o_sb[:, w % 2], ident[:]).then_inc(ot_ready, 1)

                    scores(0)
                    scores(1)
                    for k in range(nu):
                        transpose_p(k)
                        if k + 2 < nu:
                            scores(k + 2)
                        times_v(k)
                        if k >= 2 and k % 2 == 0:
                            transpose_o(k // 2 - 1)
                    transpose_o(nu // 2 - 1)

            def ada_block(bank):
                def emit(idx, s):
                    out = ps[:, bank, 2 * idx:2 * idx + 2] if isinstance(idx, int) else ps[:, bank, bass.ds(idx * 2, 2)]
                    for k in range(KC):
                        last = mm(out, ring[:, s, k], silu_c[:, k], start=(k == 0), stop=(k == KC - 1))
                    last.then_inc(block_done, 1)
                return emit

            def with_late(first, count, late_per, ordinal, emit):
                body = RING // math.gcd(RING, 1 + late_per)
                start, each = at[0], 1 + late_per

                def one(i, p):
                    shift = lambda a, n: n if i is None else i * a + n
                    for e in range(each):
                        pos = start + p * each + e
                        s = pos % RING
                        pe.wait_ge(slot_in[s], shift(16 * body * each // RING, 16 * (pos // RING + 1)))
                        if e == 0:
                            emit(shift(body, first + p), s, (first + p) % 2)
                        else:
                            late(shift(body * late_per, ordinal + p * late_per + e - 1), s)
                turns = count // body
                if turns > 1:
                    with pe.Fori(0, turns) as i:
                        for p in range(body):
                            one(i, p)
                for p in range(body * turns if turns > 1 else 0, count):
                    one(None, p)
                at[0] += count * each

            late = ada_block(7)

            def gate_filler(l):
                parts, done = gate_parts(l), [0]

                def fill(n):
                    for _ in range(min(n, len(parts) - done[0])):
                        c = done[0]
                        b, t, w = parts[c]
                        s = at[0] % RING
                        if t == 0:
                            pe.wait_ge(slot_in[s], 16 * (at[0] // RING + 1))
                        if c >= 2:
                            pe.wait_ge(g_taken[l], c - 1)
                        for k in range(KC):
                            last = mm(ps[:, 6 + c % 2, 0:w], ring[:, s, k], act_t[:, k, t:t + w],
                                      start=(k == 0), stop=(k == KC - 1))
                        done[0] += 1
                        if t + w == ntok(l):
                            last.then_inc(block_done, 1)
                            at[0] += 1
                        else:
                            last.then_inc(g_mm[l], 1)
                return fill

            pe.wait_ge(consts_set, 1)
            pe.wait_ge(silu_ready, 1)
            for l in L2:
                n = ntok(l)

                if l == 0:
                    for part in range(KC):
                        pe.wait_ge(early_in[part % 2], 16 * (part // 2 + 1))
                        w = early_w[part].rearrange("p (b k m) -> p b k m", b=2, k=KC)
                        for b in range(2):
                            col = 2 * (2 * part + b)
                            for k in range(KC):
                                last = mm(ps[:, 5, col:col + 2], w[:, b, k], silu_c[:, k], start=(k == 0), stop=(k == KC - 1))
                        last.then_inc(early_done, 1)
                sum_of_squares(l, TOK)

                def to_time(b):
                    pe.wait_ge(conv_ready[l], b + 1)
                    for gi, (t0, w) in enumerate(time_tiles(l)):
                        c = b * len(time_tiles(l)) + gi
                        if c >= 2:
                            pe.wait_ge(tp_taken[l], c - 1)
                        for t in range(t0, t0 + w):
                            col = 1 + t * P + (2 if t >= NT else 0)
                            last = tr(ps[:, 6 + c % 2, (t - t0) * P:(t - t0 + 1) * P], pc_out[:, b % 2, col:col + P], ident[:])
                        last.then_inc(tp_ready[l], 1)

                if l == 0:
                    pe.wait_ge(consts_in, 16 * 6)
                if l == 0:
                    pe.wait_ge(ada_ready, 1)
                network(l, 0, False, 6, SEQ)
                emit = project(act_t, n, taken_before(l, "pb"), h_ready[l], 2)

                def pb_block(idx, s):
                    emit(idx, s)
                    if idx == 0:
                        network(l, 1, False, 6, SEQ)
                    if 1 <= idx <= 4:
                        to_time(idx - 1)
                for b in range(N_PB):
                    s = at[0] % RING
                    pe.wait_ge(slot_in[s], 16 * (at[0] // RING + 1))
                    pb_block(b, s)
                    at[0] += 1
                pe.wait_ge(tp_taken[l], 4 * len(time_tiles(l)))
                fill = gate_filler(l)
                hyena(l, fill)
                fill(len(gate_parts(l)))
                pe.wait_ge(g_taken[l], len(gate_parts(l)))

                for t in range(NT + NTC):
                    if t >= 2:
                        pe.wait_ge(v_taken[l], t - 1)
                    for k in range(KC):
                        if t == 0:
                            pe.wait_ge(h_split[l], k + 1)
                            pe.wait_ge(block_done, STREAM_AT[l, "v", k // 2] + 1)
                        cols = slice(t * P, (t + 1) * P)
                        out = ps[:, 6 + t % 2]
                        mm(out, h_hi[:, k, cols], v_hi[:, k], start=(k == 0), stop=False)
                        mm(out, h_hi[:, k, cols], v_lo[:, k], start=False, stop=False)
                        last = mm(out, act_r[:, k, cols], v_hi[:, k], start=False, stop=(k == KC - 1))
                    last.then_inc(v_mm[l], 1)
                at[0] += N_V

                pe.wait_ge(v_taken[l], NT + NTC)
                h = lambda n: project_split(lambda k: h_hi[:, k], act_r, n, taken_before(l, "k"), split_before(l, "k"), h_split[l])
                if l == 0:
                    with_late(0, N_K + N_Q, LATE_PER[l], 0, h(n))
                    over_blocks(LATE_LAST, lambda idx, s: late(len(LATE[0]) - LATE_LAST + idx, s))
                else:
                    with_late(0, N_K, LATE_PER[l], 0, h(TOK))
                    with_late(N_K, len(LATE[l]) - N_K, LATE_PER[l], N_K, h(n))
                    with_late(len(LATE[l]), N_Q + N_K - len(LATE[l]), 0, 0, h(n))
                pe.wait_ge(ada_ready, 3 + l)
                pe.wait_ge(rope_done[l], 1)
                pe.wait_ge(qst_zero, l + 1)
                attention(l)

                over_blocks(N_OUT, project_split(mix_hi, mix_r, n, taken_before(l, "out"), split_before(l, "out"), mix_split[l]))
            sum_of_squares(DEPTH, SEQ)

        @block.scalar
        def _(act):
            fn = nc.scalar.activation

            def square(l, n, k):
                if l == 0:
                    act.wait_ge(x_loaded[k % 2], 16 * (k // 2 + 1))
                else:
                    act.wait_ge(block_taken, taken_before(l - 1, "out") + k + 1)
                if k >= 3:
                    act.wait_ge(sq_used[l], k - 2)
                fn(sq[:, k % 2, 0:n] if k else sq_sum[:, 0:n], act_t[:, k, 0:n], ACT.Square).then_inc(sq_ready[l], 1)

            def roots(l, n):
                for c, (t0, t1) in enumerate(norm_parts(n)):
                    act.wait_ge(ms_ready, 2 * l + c + 1)
                    fn(rstd[:, t0:t1], rstd[:, t0:t1], ACT.Sqrt).then_inc(std_ready, 1)

            def upper_part(j):
                act.wait_ge(slot_in[SPLIT[j] % RING], 16 * (SPLIT[j] // RING + 1))
                if j >= 2:
                    act.wait_ge(block_done, SPLIT[j - 2] + 1)
                fn(w_hi[:, j % 2], ring[:, SPLIT[j] % RING], ACT.Copy).then_inc(hi_made, 1)

            def attention(l):
                tiles = q_tiles(l)
                base, _, _ = before[l]
                nu = 2 * len(tiles)
                with act.Fori(0, 3) as pr:
                    u0 = pr * nu + base

                    def exps(k):
                        n = CTX + tiles[k // 2][6] * P
                        act.wait_ge(neg_ready, u0 + (k + 1))
                        if k >= 2:
                            act.wait_ge(pt_ready, u0 + (k - 1))
                        fn(p_sb[:, k % 2, 0:n], s_sb[:, k % 2, 0:n], ACT.Exp, bias=stat[:, k % 2:k % 2 + 1],
                           accum_out=stat[:, 8 + k % 4:9 + k % 4]).then_inc(p_ready, 1)
                        if tiles[k // 2][0] == "C":
                            fn(stat[:, 12 + k % 4:13 + k % 4], sink[:, l, bass.ds(pr * 2 + k % 2, 1)], ACT.Exp,
                               bias=stat[:, k % 2:k % 2 + 1]).then_inc(es_ready, 1)

                    def take_pt(k):
                        cs = len(chunks(tiles[k // 2]))
                        half = (cs + 1) // 2
                        act.wait_ge(pt_ready, u0 + (k + 1))
                        if k >= 2:
                            act.wait_ge(o_ready, u0 + (k - 1))
                        fn(pt_sb[:, k % 2, half * P:cs * P], ps[:, 5, 0:(cs - half) * P], ACT.Copy).then_inc(pt_act, 1)

                    exps(0)
                    for k in range(nu):
                        take_pt(k)
                        if k + 1 < nu:
                            exps(k + 1)

            def hidden(l, layer, isctx, n):
                act.wait_ge(arg_ready[l], 2 * isctx + layer + 1)
                fn((hid if layer else mlp[2])[:, 0:n], mlp[0][:, 0:n], ACT.Sin).then_inc(hid_ready[l], 1)

            def gate_filler(l):
                parts, done = gate_parts(l), [0]

                def fill(n):
                    for _ in range(min(n, len(parts) - done[0])):
                        c = done[0]
                        b, t, w = parts[c]
                        if t + w == ntok(l):
                            act.wait_ge(block_done, done_at(l, "g") + b + 1)
                        else:
                            act.wait_ge(g_mm[l], c - b + 1)
                        if c >= 2:
                            act.wait_ge(g_stored[l][c % 2], 16 * (c // 2))
                        elif l:
                            act.wait_ge(g_stored[0][c], 16 * (len(gate_parts(0)) // 2))
                        fn(g_st[:, c % 2, 0:w], ps[:, 6 + c % 2, 0:w], ACT.Silu).then_inc(g_taken[l], 1)
                        act.wait_ge(g_taken[l], c + 1)
                        if l and c == 0:
                            act.wait_ge(mix_gated[0], N_G)
                        act.dma_start(A["gates"][b, :, t:t + w], g_st[:, c % 2, 0:w]).then_inc(g_stored[l][c % 2], 16)
                        done[0] += 1
                return fill

            act.dma_start(condT[:], A["cond"]).then_inc(cond_in, 16)
            act.wait_ge(cond_in, 16)
            fn(silu_c[:], condT[:], ACT.Silu).then_inc(silu_ready, 1)
            for l in L2:
                n = ntok(l)
                if l == 0:
                    for k in range(KC):
                        square(l, TOK, k)
                roots(l, TOK)
                if l == 0:
                    act.wait_ge(consts_in, 16 * 6)
                act.wait_ge(ada_ready, 3 if l else 1)
                for k in range(KC):
                    for c, (t0, t1) in enumerate(((0, SEQ), (SEQ, TOK))):
                        act.wait_ge(scaled[l], 2 * k + c + 1)
                        fn(act_t[:, k, t0:t1], act_t[:, k, t0:t1], ACT.Identity,
                           bias=ada[:, l, k, c:c + 1]).then_inc(h_ready[l], 1)

                hidden(l, 0, False, SEQ)

                act.wait_ge(pads_set, 6 * (l + 1))

                def pad_block(b):
                    act.wait_ge(block_done, done_at(l, "pb") + b + 1)
                    if b >= 2:
                        act.wait_ge(conv_ready[l], b - 1)
                    src = ps[:, 3 * (b % 2):3 * (b % 2) + 3].rearrange("p a b -> p (a b)")
                    fn(pc_in[:, b % 2, 1:1 + SEQ], src[:, 0:SEQ], ACT.Copy).then_inc(pc_ready[l], 1)
                    if l == 0:
                        fn(pc_in[:, b % 2, SEQ + 3:SEQ + 3 + CTX], src[:, SEQ:TOK], ACT.Copy).then_inc(pc_ready[l], 1)

                def take_tiles(b):
                    dst = z_tm if b < 2 else x1_tm
                    for gi, (t0, w) in enumerate(time_tiles(l)):
                        c = b * len(time_tiles(l)) + gi
                        act.wait_ge(tp_ready[l], c + 1)
                        fn(dst[:, t0:t0 + w, (b % 2) * P:(b % 2 + 1) * P],
                           ps[:, 6 + c % 2, 0:w * P].rearrange("p (a b) -> p a b", b=P), ACT.Copy).then_inc(tp_taken[l], 1)

                pad_block(0)
                for b in range(1, N_PB):
                    pad_block(b)
                    if b <= 4:
                        take_tiles(b - 1)

                taps = wn = 0
                fill = gate_filler(l)
                for ji, (isctx, o, ns, nt) in enumerate(jobs(l)):
                    at_start, at_taps, at_signal, at_slot, at_end = FILLS[l][ji]
                    if o == 0:
                        if isctx:
                            hidden(l, 0, isctx, nt * P)
                        else:
                            act.wait_ge(conv_ready[l], N_PB)
                            act.wait_ge(tp_ready[l], 4 * len(time_tiles(l)))
                        hidden(l, 1, isctx, nt * P)
                    fill(at_start)
                    for i in range(nt):
                        act.wait_ge(tap_ready[l], taps + i + 1)
                        if i >= 2:
                            act.wait_ge(tsq_used[l], taps + i - 1)
                        fn(sq_t(i), room[:, 2 * i:2 * i + 2].rearrange("p a b -> p (a b)"), ACT.Square).then_inc(tsq_ready[l], 1)
                    taps += nt
                    act.wait_ge(en_ready[l], ji + 1)
                    fn(k_rt, k_rt, ACT.Sqrt).then_inc(rt_ready[l], 1)
                    fill(at_taps)
                    fill(at_signal)
                    for s in range(ns):
                        act.wait_ge(w_mm[l], wn + 1)
                        w = CH if s < 2 else 2 * CH
                        fn(spec[:, s].rearrange("p a c -> p (a c)")[:, 0:w], ps[:, 2 + wn % 2, 0:w], ACT.Copy
                           ).then_inc(w_taken[l], 1)
                        wn += 1
                        if s in (2, 5):
                            fill(at_slot)
                    fill(at_end)
                fill(len(gate_parts(l)))

                act.wait_ge(hyena_done[l], 1)
                for k in range(KC):
                    if k % 2 == 0:
                        pos = STREAM_AT[l, "v", k // 2]
                        act.wait_ge(slot_in[pos % RING], 16 * (pos // RING + 1))
                        fn(v_hi[:, k:k + 2].rearrange("p k m -> p (k m)"), ring[:, pos % RING].rearrange("p k m -> p (k m)"),
                           ACT.Copy).then_inc(v_hi_made[l], 1)
                    fn(h_hi[:, k], act_t[:, k], ACT.Copy).then_inc(h_hi_made[l], 1)
                for b in range(2):
                    act.wait_ge(g_stored[l][b], 16 * (len(gate_parts(l)) // 2))

                first = split_before(l, "k")
                for t in range(NT + NTC):
                    if t == NT:
                        upper_part(first)
                        upper_part(first + 1)
                    act.wait_ge(v_mm[l], t + 1)
                    fn(v_tm[:, t], ps[:, 6 + t % 2], ACT.Copy).then_inc(v_taken[l], 1)
                for j in range(2, N_K + N_Q):
                    upper_part(first + j)

                attention(l)

                first = split_before(l, "out")
                upper_part(first)
                upper_part(first + 1)
                act.wait_ge(ot_taken, before[l + 1][0] // 2)
                for k in range(KC):
                    act.wait_ge(mix_gated[l], k + 1)
                    fn(mix_hi(k)[:, 0:n], mix[:, k, 0:n], ACT.Copy).then_inc(mix_hi_made[l], 1)
                for j in range(2, N_OUT):
                    upper_part(first + j)
                    square(l + 1, n, j - 2)
                for k in range(N_OUT - 2, KC):
                    square(l + 1, n, k)

            roots(DEPTH, SEQ)

        @block.vector
        def _(dve):
            v = nc.vector
            step = Steps(dve)

            def tt(out, a, op, b, sem=None):
                step(v.tensor_tensor(out, a, b, op), sem)

            def stt(out, a, c, op, b, sem=None):
                step(v.scalar_tensor_tensor(out=out, in0=a, scalar=c, in1=b, op0=ALU.mult, op1=op), sem)

            def mul(out, a, c, sem=None):
                step(v.tensor_scalar(out, a, c, None, ALU.mult), sem)

            add, sub, mult = ALU.add, ALU.subtract, ALU.mult

            def add_squares(l, n, k):
                dve.wait_ge(sq_ready[l], k + 1)
                tt(sq_sum[:, 0:n], sq_sum[:, 0:n], add, sq[:, k % 2, 0:n], sq_used[l])
                step.join()

            def norm(l, n):
                dve.wait_ge(ms_mm, l + 1)
                src = ps[:, 0:3].rearrange("p a b -> p (a b)")
                for t0, t1 in norm_parts(n):
                    step(v.tensor_scalar(rstd[:, t0:t1], src[:, t0:t1], 1.0 / D, EPS, mult, add), ms_ready)
                for c, (t0, t1) in enumerate(norm_parts(n)):
                    dve.wait_ge(std_ready, 2 * l + c + 1)
                    step(v.reciprocal(rstd[:, t0:t1], rstd[:, t0:t1]))
                step.join()

            def reduce_arg(n, bank, b, f):
                src = ps[:, bank:bank + 2].rearrange("p a b -> p (a b)")[:, 0:n]
                a, k = mlp[0][:, 0:n], mlp[1][:, 0:n]
                step(v.tensor_scalar(a, src, b, f, add, mult))
                step.join()
                step(v.tensor_scalar(k, a, 1.0 / (2 * math.pi), ROUND, mult, add))
                step.join()
                step(v.tensor_scalar(k, k, ROUND, None, sub))
                for part in (TWO_PI_A, TWO_PI_B, TWO_PI_C):
                    step.join()
                    stt(a, k, -part, add, a)
                step.join()

            def even(src, z):
                tb, tc, te, td = room[:, 0:4], room[:, 4:8], room[:, 24:26], room[:, 26:28]
                tt(tb, src[:, 0:4], add, src[:, 4:8])
                tt(tc, src[:, 0:4], sub, src[:, 4:8])
                step.join()
                tt(te, tb[:, 0:2], add, tb[:, 2:4])
                tt(z[:, 2, 0], tb[:, 0], sub, tb[:, 2])
                tt(td[:, 0], tc[:, 1], sub, tc[:, 3])
                tt(td[:, 1], tc[:, 1], add, tc[:, 3])
                step.join()
                tt(z[:, 0, 0], te[:, 0], add, te[:, 1], bf)
                tt(z[:, 1, 0], te[:, 0], sub, te[:, 1], bf)
                tt(z[:, 2, 1], tb[:, 3], sub, tb[:, 1], bf)
                stt(z[:, 3, 0], td[:, 0], SQ5, add, tc[:, 0])
                stt(z[:, 3, 1], td[:, 1], -SQ5, sub, tc[:, 2], bf)
                stt(z[:, 4, 0], td[:, 0], -SQ5, add, tc[:, 0])
                stt(z[:, 4, 1], td[:, 1], -SQ5, add, tc[:, 2], bf)
                step.join()

            def odd(src, z):
                tp, tm, te = room[:, 0:3], room[:, 3:6], room[:, 6:8]
                tf, to, tg = room[:, 24:26], room[:, 26:28], room[:, 28:30]
                tt(tp, src[:, 1:4], sub, src[:, 7:4:-1])
                tt(tm, src[:, 1:4], add, src[:, 7:4:-1])
                step.join()
                stt(te[:, 0], tp[:, 1], SQ5, add, src[:, 0])
                stt(te[:, 1], tp[:, 1], -SQ5, add, src[:, 0])
                stt(tf[:, 0], tm[:, 1], SQ5, add, src[:, 4])
                stt(tf[:, 1], tm[:, 1], SQ5, sub, src[:, 4])
                mul(to[:, 0], tp[:, 0], C1)
                mul(to[:, 1], tp[:, 0], S1)
                mul(tg[:, 0], tm[:, 0], -S1)
                mul(tg[:, 1], tm[:, 0], -C1)
                step.join()
                stt(to[:, 0], tp[:, 2], S1, add, to[:, 0])
                stt(to[:, 1], tp[:, 2], -C1, add, to[:, 1])
                stt(tg[:, 0], tm[:, 2], -C1, add, tg[:, 0])
                stt(tg[:, 1], tm[:, 2], S1, add, tg[:, 1])
                step.join()
                for i in range(2):
                    tt(z[:, 5 + i, 0], te[:, i], add, to[:, i])
                    tt(z[:, 5 + i, 1], tg[:, i], sub, tf[:, i], bf)
                for i in range(2):
                    tt(z[:, 7 + i, 0], te[:, i], sub, to[:, i])
                    tt(z[:, 7 + i, 1], tg[:, i], add, tf[:, i], bf)
                step.join()

            def few(kc, kn, z):
                tt(z[:, 0, 0], kc[:, 0], add, kc[:, 1], bf)
                tt(z[:, 1, 0], kc[:, 0], sub, kc[:, 1], bf)
                mul(z[:, 2, 0], kn[:, 0], 1.0)
                mul(z[:, 2, 1], kn[:, 1], -1.0, bf)
                step.join()

            def back(y):
                r = room
                tt(r[:, 0:4].rearrange("p (a b) c -> p a b c", b=2), spec[:, 5:7], add, spec[:, 7:9])
                tt(r[:, 4:8].rearrange("p (a b) c -> p a b c", b=2), spec[:, 5:7], sub, spec[:, 7:9])
                tt(r[:, 8], spec[:, 0, 0], add, spec[:, 1, 0])
                tt(r[:, 9], spec[:, 0, 0], sub, spec[:, 1, 0])
                tt(r[:, 10:12], spec[:, 3], add, spec[:, 4])
                tt(r[:, 12:14], spec[:, 3], sub, spec[:, 4])
                step.join()
                tt(r[:, 14], r[:, 8], add, spec[:, 2, 0])
                tt(r[:, 15], r[:, 9], sub, spec[:, 2, 1])
                tt(r[:, 16], r[:, 8], sub, spec[:, 2, 0])
                tt(r[:, 17], r[:, 9], add, spec[:, 2, 1])
                tt(r[:, 18], r[:, 12], sub, r[:, 11])
                tt(r[:, 19], r[:, 12], add, r[:, 11])
                step.join()
                e = r[:, 20:28]
                tt(e[:, 0], r[:, 14], add, r[:, 10])
                tt(e[:, 4], r[:, 14], sub, r[:, 10])
                tt(e[:, 2], r[:, 16], sub, r[:, 13])
                tt(e[:, 6], r[:, 16], add, r[:, 13])
                stt(e[:, 1], r[:, 18], SQ5, add, r[:, 15])
                stt(e[:, 5], r[:, 18], -SQ5, add, r[:, 15])
                stt(e[:, 3], r[:, 19], -SQ5, add, r[:, 17])
                stt(e[:, 7], r[:, 19], SQ5, add, r[:, 17])
                step.join()
                pp, qp, rp, tp_ = (r[:, i] for i in range(4))
                pm, qm, rm, tm = (r[:, i] for i in range(4, 8))
                tt(r[:, 8], pp, add, rp)
                tt(r[:, 9], tm, sub, qm)
                tt(r[:, 10], pp, sub, rp)
                tt(r[:, 11], qm, add, tm)
                mul(r[:, 12], pm, C1)
                mul(r[:, 13], pm, S1)
                mul(r[:, 14], qp, S1)
                mul(r[:, 15], qp, C1)
                step.join()
                stt(r[:, 12], rm, S1, add, r[:, 12])
                stt(r[:, 13], rm, -C1, add, r[:, 13])
                stt(r[:, 14], tp_, C1, add, r[:, 14])
                stt(r[:, 15], tp_, -S1, add, r[:, 15])
                tt(r[:, 16], r[:, 10], sub, r[:, 11])
                tt(r[:, 17], r[:, 10], add, r[:, 11])
                step.join()
                tt(r[:, 18], r[:, 12], sub, r[:, 14])
                tt(r[:, 19], r[:, 12], add, r[:, 14])
                tt(r[:, 28], r[:, 13], sub, r[:, 15])
                tt(r[:, 29], r[:, 13], add, r[:, 15])
                tt(y[:, 0], e[:, 0], add, r[:, 8])
                tt(y[:, 4], e[:, 4], add, r[:, 9])
                stt(y[:, 2], r[:, 16], SQ5, add, e[:, 2])
                stt(y[:, 6], r[:, 17], -SQ5, add, e[:, 6])
                step.join()
                tt(y[:, 1], e[:, 1], add, r[:, 18])
                tt(y[:, 7], e[:, 7], sub, r[:, 19])
                tt(y[:, 3], e[:, 3], add, r[:, 28])
                tt(y[:, 5], e[:, 5], sub, r[:, 29])
                step.join()

            def network(l, layer, isctx, bank, n):
                dve.wait_ge(mlp_mm[l], 2 * isctx + layer + 1)
                if layer:
                    dve.wait_ge(hid_ready[l], 2 * isctx + 1)
                reduce_arg(n, bank, f_small[:, l, 2 * layer:2 * layer + 1], f_small[:, l, 2 * layer + 1:2 * layer + 2])
                a = mlp[0][:, 0:n]
                step(v.tensor_scalar(a, a, 3.1415925, -3.1415925, ALU.min, ALU.max), arg_ready[l])
                step.join()

            def hyena(l):
                nonlocal bf
                bf = bf_ready[l]
                taps = xn = wn = conv_n = back_n = 0
                for ji, (isctx, o, ns, nt) in enumerate(jobs(l)):
                    if o == 0 and isctx:
                        for layer in range(2):
                            network(l, layer, isctx, 2 * layer, nt * P)
                    dve.wait_ge(dec_in[l], 16 * (ji + 1))
                    for i in range(nt):
                        dve.wait_ge(tap_mm[l], taps + i + 1)
                        tt(room[:, 2 * i:2 * i + 2], ps[:, 4 + (taps + i) % 2].rearrange("p (a b) -> p a b", b=CH), mult,
                           decay[:, 2 * i:2 * i + 2], tap_ready[l])
                    taps += nt
                    dve.wait_ge(tsq_used[l], taps)
                    step(v.tensor_copy(k_rt, ps[:, 1, 0:CH]))
                    step.join()
                    tt(k_rt, k_rt, add, ps[:, 1, CH:2 * CH])
                    step.join()
                    step(v.tensor_scalar(k_rt, k_rt, 1e-6, None, add), en_ready[l])
                    dve.wait_ge(rt_ready[l], ji + 1)
                    dve.wait_ge(drow_in[l], 16 * (ji + 1))
                    step(v.reciprocal(k_s, k_rt))
                    tt(d_row[0:1], d_row[0:1], mult, k_rt[0:1])
                    step.join()
                    tt(room[0:1, 0], room[0:1, 0], add, d_row[0:1])
                    if isctx:
                        mul(k_s, k_s, 4.0)
                    step.join()
                    kc, kn = room[:, 16:16 + nt], room[:, nt:2 * nt]
                    tt(kc, room[:, 0:nt], add, room[:, nt:2 * nt])
                    step.join()
                    tt(kn, room[:, 0:nt], sub, room[:, nt:2 * nt])
                    step.join()
                    if isctx:
                        few(kc, kn, spec)
                    else:
                        even(kc, spec)
                        odd(kn, spec)
                    for s in range(ns):
                        dve.wait_ge(x_mm[l], xn + 1)
                        tt(khat[:, s], ps[:, xn % 2].rearrange("p (a b) -> p a b", b=CH), mult,
                           k_s.unsqueeze(1).broadcast_to([P, 2, CH]), x_taken[l])
                        xn += 1
                    step.join()
                    u = z_tm[:, NT:NT + NTC] if isctx else z_tm[:, 0:NT]
                    if ji == 0:
                        dve.wait_ge(tp_taken[l], 4 * len(time_tiles(l)))
                    if isctx:
                        few(u, u, spec)
                    else:
                        even(u, spec)
                        odd(u, spec)
                    for s in range(ns):
                        dve.wait_ge(x_mm[l], xn + 1)
                        if conv_n >= 2:
                            dve.wait_ge(y_part[l], 2 * (conv_n - 1))
                        x = ps[:, xn % 2].rearrange("p (a b) -> p a b", b=CH)
                        for part, sm in ((0, prod_ready[l]), (1, x_taken[l])):
                            tt(prod[:, conv_n % 2, part].rearrange("p (a b) -> p a b", b=CH), x, mult,
                               khat[:, s, part].unsqueeze(1).broadcast_to([P, 2, CH]), sm)
                        xn += 1
                        conv_n += 1
                    wn += ns
                    dve.wait_ge(w_taken[l], wn)
                    if isctx:
                        r = room
                        tt(r[:, 0], spec[:, 0, 0], add, spec[:, 1, 0])
                        tt(r[:, 1], spec[:, 0, 0], sub, spec[:, 1, 0])
                        step.join()
                        tt(u[:, 0], r[:, 0], add, spec[:, 2, 0])
                        tt(u[:, 1], r[:, 1], sub, spec[:, 2, 1])
                        step.join()
                    else:
                        back(u)
                    if o == 0:
                        x1 = x1_tm[:, NT:NT + NTC] if isctx else x1_tm[:, 0:NT]
                        tt(u, u, mult, x1)
                        step.join()
                    else:
                        step(v.memset(stat_h[:, 0:1], 0.0), yt_ready[l])
                        for gi, (b, t0, w) in enumerate(back_tiles(isctx)):
                            dve.wait_ge(yt_mm[l], back_n + 1)
                            dst = mix[:, b, t0 * P:(t0 + w) * P]
                            tt(dst, dst, mult, ps[:, 4 + gi % 2, 0:w * P], yt_taken[l])
                            back_n += 1
                step.join()
                step(v.memset(stat_h[:, 0:1], 0.0), hyena_done[l])
                step.join()

            def take_ada(l, first, n, bank, col):
                tt(ada[:, l, first:first + n], ps[:, bank, 2 * col:2 * (col + n)].rearrange("p (a b) -> p a b", b=2), add,
                   b_ada[:, l, first:first + n].unsqueeze(2).broadcast_to([P, n, 2]), ada_ready)
                step.join()



            def rope(l, blk, signal=None):
                dve.wait_ge(rope_in[l], 16)
                step(v.stream_shuffle(rope_t[:, 0], blk, [i ^ 16 for i in range(32)]))
                step.join()
                tt(rope_t[:, 1], rope_t[:, 0], mult, rope_cs[:, 1])
                tt(blk, blk, mult, rope_cs[:, 0])
                step.join()
                tt(blk, blk, add, rope_t[:, 1], signal)
                step.join()

            def lower_part(j):
                s = SPLIT[j] % RING
                dve.wait_ge(hi_made, j + 1)
                v.tensor_tensor(ring_r[:, s], ring[:, s], w_hi[:, j % 2], sub).then_inc(lo_made, 1)

            def attention(l):
                tiles = q_tiles(l)
                base, sinks, steps = before[l]
                nw = len(tiles)
                nu, per = 2 * nw, steps_of(tiles)

                def has_sink(k):
                    return tiles[k // 2][0] == "C"
                with dve.Fori(0, 3) as pr:
                    u0 = pr * nu + base
                    w0 = pr * nw + base // 2
                    own = [0]

                    def chain(ins):
                        ins.then_inc(unit_step, 1)
                        own[0] += 1

                    def join():
                        dve.wait_ge(unit_step, pr * per + (steps + own[0]))

                    def sinks_made(units):
                        dve.wait_ge(es_ready, pr * sinks_of(tiles, nu) + (sinks + sinks_of(tiles, units)))

                    def q_block(w):
                        _, qb, _, _, j, _, _ = tiles[w]
                        return mix[:, bass.ds(pr + qb, 1), j * P:(j + 1) * P].rearrange("p a b -> p (a b)")

                    def stage_q(w):
                        if w >= 2:
                            dve.wait_ge(s_ready, u0 + (2 * w - 2))
                        for par in range(2):
                            v.tensor_scalar(q_st[64 * par:64 * par + 64, w % 2, par], q_block(w)[64 * par:64 * par + 64],
                                            QSCALE, None, mult).then_inc(qst_ready, 1)

                    def softmax_in(k):
                        kind, _, _, _, j, first, n = tiles[k // 2]
                        par = k % 2
                        dve.wait_ge(s_ready, u0 + (k + 1))
                        if k >= 2:
                            dve.wait_ge(p_ready, u0 + (k - 1))
                            if has_sink(k - 2):
                                sinks_made(k - 1)
                        bank = 2 * (k % 2)
                        lo = sink[:, l, bass.ds(pr * 2 + par, 1)] if has_sink(k) else LOWEST
                        chain(v.tensor_scalar(s_sb[:, k % 2, 0:CTX], ps[:, bank + 1, P:P + CTX], 1.0, lo, mult, ALU.max,
                                              accum_out=stat[:, 2 + k % 2:3 + k % 2]))
                        c, m = stat[:, 2 + k % 2:3 + k % 2], stat[:, 4 + k % 2:5 + k % 2]
                        if n:
                            if kind == "A":
                                bias = t_inner[:, par] if n == 5 else \
                                    t_edge[:, par, (2 * (first - j) + 6) * GRID:(2 * (first - j) + 6) * GRID + n * P]
                            else:
                                bias = m_win[:, (first - j + 1) * P:(first - j + 1 + n) * P]
                            src = ps[:, bank:bank + 2].rearrange("p a b -> p (a b)")[:, 0:n * P]
                            chain(v.tensor_tensor_reduce(out=s_sb[:, k % 2, CTX:CTX + n * P], in0=src, in1=bias, scale=1.0,
                                                         scalar=LOWEST, op0=add, op1=ALU.max, accum_out=m))
                            join()
                            v.tensor_scalar(stat[:, k % 2:k % 2 + 1], m, c, -1.0, ALU.max, mult).then_inc(neg_ready, 1)
                        else:
                            join()
                            v.tensor_scalar(stat[:, k % 2:k % 2 + 1], c, -1.0, None, mult).then_inc(neg_ready, 1)

                    def take_pt(k):
                        half = (len(chunks(tiles[k // 2])) + 1) // 2
                        dve.wait_ge(pt_ready, u0 + (k + 1))
                        if k >= 2:
                            dve.wait_ge(o_ready, u0 + (k - 1))
                        v.tensor_copy(pt_sb[:, k % 2, 0:half * P], ps[:, 4, 0:half * P]).then_inc(pt_dve, 1)

                    def divide(w):
                        dve.wait_ge(o_ready, u0 + (2 * w + 2))
                        if w >= 2:
                            dve.wait_ge(ot_ready, w0 + (w - 1))
                        cols = slice(8 + (2 * w) % 4, 10 + (2 * w) % 4)
                        total = stat[:, cols]
                        if has_sink(2 * w):
                            sinks_made(2 * w + 2)
                            chain(v.tensor_tensor(stat[:, 16:18], total, stat[:, cols.start + 4:cols.stop + 4], add))
                            total = stat[:, 16:18]
                            join()
                        chain(v.reciprocal(stat[:, 18:20], total))
                        join()
                        for par in range(2):
                            v.tensor_scalar(o_sb[:, w % 2, par * HD:(par + 1) * HD], ps[:, 6 + w % 2, par * HD:(par + 1) * HD],
                                            stat[:, 18 + par:19 + par], None, mult).then_inc(on_ready, 1)

                    def take_o(w):
                        dve.wait_ge(ot_ready, w0 + (w + 1))
                        v.tensor_scalar(q_block(w), ps[:, 6 + w % 2, P:2 * P], 1.0, None, mult).then_inc(ot_taken, 1)

                    stage_q(0)
                    stage_q(1)
                    raw = t_raw[:, bass.ds(pr * 2, 2)].rearrange("p h a b -> p (h a) b")
                    chain(v.tensor_tensor(t_edge.rearrange("p h (a b) -> p (h a) b", b=GRID), raw,
                                          m_cols.unsqueeze(1).broadcast_to([P, 28, GRID]), add))
                    join()
                    softmax_in(0)
                    softmax_in(1)
                    chain(v.tensor_tensor(t_inner, t_edge[:, :, 128:768], m_rows.unsqueeze(1).broadcast_to([P, 2, 640]), add))
                    for k in range(nu):
                        if 1 < k + 1 < nu:
                            softmax_in(k + 1)
                        take_pt(k)
                        if k % 2 and k // 2 + 2 < nw:
                            stage_q(k // 2 + 2)
                        if k >= 2 and k % 2 == 0:
                            divide(k // 2 - 1)
                        if k >= 3 and k % 2:
                            take_o(k // 2 - 1)
                    divide(nw - 1)
                    take_o(nw - 1)
                    assert own[0] == per

            bf = None
            for l in L2:
                n = ntok(l)
                if l == 0:
                    for k in range(1, KC):
                        add_squares(l, n, k)
                    dve.wait_ge(consts_in, 16 * 6)
                    dve.wait_ge(early_done, KC)
                    take_ada(0, 0, N_EARLY, 5, 0)
                step(v.scalar_tensor_tensor(out=mod_a[:], in0=ada[:, l, KC:2 * KC], scalar=1.0,
                                            in1=norm_g[:, l].unsqueeze(2).broadcast_to([P, KC, 2]), op0=add, op1=mult))
                norm(l, TOK)
                if l:
                    dve.wait_ge(x_stored, 16 * KC)
                for k in range(KC):
                    for c, (t0, t1) in enumerate(((0, SEQ), (SEQ, TOK))):
                        stt(act_t[:, k, t0:t1], act_t[:, k, t0:t1], mod_a[:, k, c:c + 1], mult, rstd[:, t0:t1], scaled[l])
                step.join()

                for layer in range(2):
                    network(l, layer, False, 6, SEQ)

                w = TOK + 2 if l == 0 else SEQ
                step.at[block_taken.name] = taken_before(l, "pb")
                for b in range(N_PB):
                    dve.wait_ge(pc_ready[l], (b + 1) * (2 if l == 0 else 1))
                    if b >= 2:
                        dve.wait_ge(tp_ready[l], len(time_tiles(l)) * min(b - 1, 4))
                    x, y = pc_in[:, b % 2], pc_out[:, b % 2]
                    cw = [conv_w[:, l, b, i:i + 1] for i in range(4)]
                    step(v.tensor_scalar(y[:, 1:1 + w], x[:, 1:1 + w], cw[1], cw[3], mult, add), block_taken)
                    step.join()
                    stt(y[:, 1:1 + w], x[:, 0:w], cw[0], add, y[:, 1:1 + w])
                    step.join()
                    if b < 4:
                        stt(y[:, 1:1 + w], x[:, 2:2 + w], cw[2], add, y[:, 1:1 + w], conv_ready[l])
                    else:
                        if l == 0:
                            stt(mix[:, b - 4, SEQ:TOK], x[:, SEQ + 4:SEQ + 4 + CTX], cw[2], add, y[:, SEQ + 3:SEQ + 3 + CTX])
                        stt(mix[:, b - 4, 0:SEQ], x[:, 2:2 + SEQ], cw[2], add, y[:, 1:1 + SEQ], conv_ready[l])
                    step.join()

                hyena(l)

                dve.wait_ge(block_done, STREAM_AT[l, "v", 0])
                for k in range(KC):
                    if k % 2 == 0:
                        dve.wait_ge(v_hi_made[l], k // 2 + 1)
                        both = slice(k, k + 2)
                        v.tensor_tensor(v_lo[:, both].rearrange("p k m -> p (k m)"),
                                        ring[:, STREAM_AT[l, "v", k // 2] % RING].rearrange("p k m -> p (k m)"),
                                        v_hi[:, both].rearrange("p k m -> p (k m)"), sub).then_inc(block_done, 1)
                    dve.wait_ge(h_hi_made[l], k + 1)
                    tt(act_r[:, k], act_t[:, k], sub, h_hi[:, k], h_split[l])

                first, blocks = split_before(l, "k"), [("k", b) for b in range(N_K)] + [("q", b) for b in range(N_Q)]
                lower_part(first)
                lower_part(first + 1)
                for j, (stage, b) in enumerate(blocks):
                    dve.wait_ge(block_done, STREAM_AT[l, stage, b] + 1)
                    dst = k_fm[:, b] if stage == "k" else mix[:, MIX_C + b if b < 3 else MIX_A + b - 3]
                    width = TOK if stage == "k" else n
                    src = ps[:, 3 * (j % 2):3 * (j % 2) + 3].rearrange("p a b -> p (a b)")
                    v.tensor_scalar(dst[:, 0:width], src[:, 0:width], 1.0, None, mult).then_inc(block_taken, 1)
                    if j + 2 < len(blocks):
                        lower_part(first + j + 2)
                    if (stage, b) == ("k", N_K - 1) or stage == "q" and b < 3:
                        dve.wait_ge(block_taken, taken_before(l, "k") + j + 1)
                        rope(l, dst[:, 0:SEQ], rope_done[l] if (stage, b) == ("q", 2) else None)
                dve.wait_ge(block_done, STREAM_AT[l, "out", 0])
                if l == 0:
                    take_ada(0, N_EARLY, N_ADA - N_EARLY, 7, 0)
                    take_ada(1, 0, N_EARLY, 7, N_ADA - N_EARLY)
                else:
                    take_ada(1, N_EARLY, N_ADA - N_EARLY, 7, 0)
                dve.wait_ge(block_taken, taken_before(l, "out"))
                dve.wait_ge(masks_in[l], 16 * 3)
                dve.wait_ge(traw_in[l], 16 * 12)
                dve.wait_ge(qst_zero, l + 1)
                attention(l)

                first = split_before(l, "out")
                lower_part(first)
                for k in range(KC):
                    dve.wait_ge(mix_hi_made[l], k + 1)
                    tt(mix_r[:, k, 0:n], mix[:, k, 0:n], sub, mix_hi(k)[:, 0:n], mix_split[l])
                    if k == 0:
                        lower_part(first + 1)
                for m in range(KC):
                    dve.wait_ge(block_done, done_at(l, "out") + m + 1)
                    dve.wait_ge(xin_in[l][m % 2], 16 * (m // 2 + 1))
                    src = ps[:, 3 * (m % 2):3 * (m % 2) + 3].rearrange("p a b -> p (a b)")
                    if l == 0:
                        stt(act_t[:, m, SEQ:TOK], src[:, SEQ:TOK], ada[:, l, 2 * KC + m, 1:2], add, x_in[:, m % 2, SEQ:TOK])
                    v.scalar_tensor_tensor(out=act_t[:, m, 0:SEQ], in0=src[:, 0:SEQ], scalar=ada[:, l, 2 * KC + m, 0:1],
                                           in1=x_in[:, m % 2, 0:SEQ], op0=mult, op1=add).then_inc(block_taken, 1)
                    if m + 2 < N_OUT:
                        lower_part(first + m + 2)
                    if m > 1:
                        add_squares(l + 1, n, m - 1)
                add_squares(l + 1, n, KC - 1)
            norm(DEPTH, SEQ)
            for m in range(KC):
                if m >= 2:
                    dve.wait_ge(fin_out[m % 2], 16 * (m // 2))
                stt(fin[:, m % 2], act_t[:, m, 0:SEQ], norm_g[:, DEPTH, m:m + 1], mult, rstd[:, 0:SEQ], fin_ready)


def lay_out(i):
    f = np.float32
    i = {k: np.asarray(v, f) for k, v in i.items()}
    o = {}
    blocks = lambda w, cols: [w[:, c].reshape(KC, P, P).transpose(1, 0, 2).reshape(P, KC * P) for c in cols]
    rng = lambda a, n: [np.arange(a + P * b, a + P * b + P) for b in range(n)]
    heads = lambda a: [np.concatenate([np.arange(a + HD * h, a + HD * h + HD) for h in C_HEAD_ORDER[p:p + 2]])
                       for p in (0, 2, 4)]
    per = []
    rows = np.concatenate(rng(384, 2) + rng(0, 3) + heads(640))
    columns = {"ada": rng(0, N_ADA), "pb": rng(1536, 6), "q": heads(2560) + rng(0, 3), "k": rng(384, 3) + rng(2944, 1),
               "g": rng(2304, 2) + rng(1152, 3) + heads(3200), "out": rng(0, 8)}
    for l, name, b in STREAM:
        if name == "v":
            w = i["w_in"][l]
            wv = np.concatenate([w[:, 768:1152], w[:, 3072:3200]], 1).reshape(KC, P, 512).transpose(1, 0, 2)
            per.append(wv[:, 2 * b:2 * b + 2].reshape(P, 1024))
        else:
            w = i["w_ada"][l] if name == "ada" else i["w_out"][l][rows] if name == "out" else i["w_in"][l]
            per += blocks(w, [columns[name][b]])
    o["early"] = np.stack(blocks(i["w_ada"][0], columns["ada"][:N_EARLY])).reshape(KC, 2, P, KC * P).transpose(0, 2, 1, 3
                                                                                                             ).reshape(KC, P, 2 * KC * P)
    o["weights"] = np.stack(per)
    col = lambda a, n: a.reshape(n, P).T
    x = np.concatenate([i["x"][0], i["ctx"][0]], 0).T
    o["x_blocks"] = x.reshape(KC, P, TOK)
    o["cond"] = np.stack([col(i["c"][0], KC), col(i["c_ctx"], KC)], 2)
    o["norm_g"] = np.stack([col(i["norm_g"][l], KC) for l in range(DEPTH)] + [col(i["final_g"], KC)], 1)
    o["b_ada"] = np.stack([col(i["b_ada"][l], N_ADA) for l in range(DEPTH)], 1)
    o["conv_w"] = np.stack([np.stack([col(i["hy_conv_w"][l, t], 6) for t in range(3)] + [col(i["hy_conv_b"][l], 6)], 2)
                            for l in range(DEPTH)], 1)
    two = lambda a: np.concatenate([a, a])
    o["f_small"] = np.stack([np.stack([two(i[n][l]) for n in ("hy_b1", "hy_freq1", "hy_b2", "hy_freq2")], 1)
                             for l in range(DEPTH)], 1)
    o["sink"] = np.broadcast_to(i["sink"][None][:, :, list(C_HEAD_ORDER)], (P, DEPTH, 6))
    w12 = np.zeros((DEPTH, P, 2, P), f)
    w3 = np.zeros((DEPTH, 2, P, 512), f)
    for l in range(DEPTH):
        for e in range(2):
            w12[l, 33 * e:33 * e + 33, 0, 64 * e:64 * e + 64] = i["hy_w1"][l]
            w12[l, 64 * e:64 * e + 64, 1, 64 * e:64 * e + 64] = i["hy_w2"][l]
            w3[l, e, 64 * e:64 * e + 64] = i["hy_w3"][l][:, 512 * e:512 * e + 512]
    o["w12"], o["w3"] = w12, w3
    o["hy_d"] = i["hy_d"]
    rel = np.arange(GRID)[None, :] - np.arange(GRID)[:, None] + 15
    padded = np.concatenate([i["na_rpb"], np.zeros(i["na_rpb"].shape[:3] + (1,), f)], 3)
    rel = np.where((rel < 0) | (rel > 30), 31, rel)
    o["rpb"] = padded[:, :, :, rel].transpose(0, 1, 3, 2, 4)
    o["ident"] = np.eye(P, dtype=f)
    o["dft_f"], o["dft_i"] = dft_tables()
    o["rope"] = np.stack(rope_tables(), 1)
    o["m_cols"], o["m_rows"], o["m_win"] = attention_masks()
    o["feats"], o["decay"] = filter_tables(SEQ)
    o["feats_ctx"], o["decay_ctx"] = filter_tables(CTX)
    return {k: np.ascontiguousarray(v, f) for k, v in o.items()}


def kernel(**inputs):
    import concourse.bacc as bacc
    from concourse.bass_utils import run_bass_kernel_spmd

    arrays = lay_out(inputs)
    nc = bacc.Bacc("TRN2", target_bir_lowering=False, num_devices=1)
    aps = {k: nc.dram_tensor(f"in_{k}", v.shape, F32, kind="ExternalInput").ap() for k, v in arrays.items()}
    aps["x_mid"] = nc.dram_tensor("x_mid", (KC, P, TOK), F32, kind="Internal").ap()
    aps["gates"] = nc.dram_tensor("gates", (N_G, P, TOK), F32, kind="Internal").ap()
    aps["out"] = nc.dram_tensor("out_fm", (KC, P, SEQ), F32, kind="ExternalOutput").ap()
    build(nc, aps)
    r = run_bass_kernel_spmd(nc, [{f"in_{k}": v for k, v in arrays.items()}], core_ids=[0])
    return np.ascontiguousarray(r.results[0]["out_fm"].reshape(D, SEQ).T)[None]
```

```python
import math
from contextlib import ExitStack

import numpy as np

import concourse.bass as bass
from concourse import mybir

F32, F32R = mybir.dt.float32, mybir.dt.float32r
ALU = mybir.AluOpType
ACT = mybir.ActivationFunctionType

P = 128
D = 1024
KC = D // P
SEQ, CTX = 1024, 256
TOK = SEQ + CTX
NT, NTC = SEQ // P, CTX // P
DEPTH = 2
GRID = 64
CH = 256
HD = 64
QSCALE = HD ** -0.5
EPS = 1e-6
NEG = -1e30
LOWEST = -3.0e38

N_ADA, N_PB, N_Q, N_K, N_V, N_G, N_OUT = 24, 6, 6, 4, 4, 8, 8
RING = 4
N_EARLY = 2 * KC
LATE = ([(0, "ada", b) for b in range(N_EARLY, N_ADA)] + [(1, "ada", b) for b in range(N_EARLY)],
        [(1, "ada", b) for b in range(N_EARLY, N_ADA)])
LATE_PER = [len(late) // N_G for late in LATE]


def stream():
    stage = lambda l, name, n: [(l, name, b) for b in range(n)]
    out = []
    for l in range(DEPTH):
        out += stage(l, "pb", N_PB)
        for b in range(N_G):
            out += [(l, "g", b)] + LATE[l][b * LATE_PER[l]:(b + 1) * LATE_PER[l]]
        out += stage(l, "v", N_V) + stage(l, "k", N_K) + stage(l, "q", N_Q) + stage(l, "out", N_OUT)
    return out


STREAM = stream()
STREAM_AT = {block: i for i, block in enumerate(STREAM)}
assert len(STREAM) % RING == 0
assert all(STREAM_AT[l, name, 0] % 2 == 0 for l in range(DEPTH) for name in ("pb", "k", "q", "out"))

MIX_A, MIX_C = 2, 5
C_HEAD_ORDER = (0, 3, 1, 4, 2, 5)

SLOT_R = (0, 8, 4, 2, 6, 1, 3, 7, 5)
NS_MAIN, NS_CTX = 9, 3
DFT_START = [0, 2, 4, 7, 10, 13, 16, 19, 22]
N_DFT = 25
SQ5, C1, S1 = math.sqrt(0.5), math.cos(math.pi / 8), math.sin(math.pi / 8)

TWO_PI_A, TWO_PI_B = 6.28125, 0.0019340515136718750
TWO_PI_C = 2 * math.pi - TWO_PI_A - TWO_PI_B
ROUND = 12582912.0


def dft_tables():
    p = np.arange(P, dtype=np.float64)
    fwd, inv = [], []
    for slot, r in enumerate(SLOT_R):
        theta = 2 * np.pi * (p[:, None] * r / 2048 + p[:, None] * p[None, :] / P)
        c, s = np.cos(theta), np.sin(theta)
        g = (1.0 if r in (0, 8) else 2.0) / 2048
        fwd += [c, -s] if slot < 2 else [c, s, -s]
        inv += [g * c.T, -g * s.T] if slot < 2 else [g * c.T, g * s.T, -g * s.T]
    pack = lambda m: np.stack(m, 1).astype(np.float32)
    return pack(fwd), pack(inv)


def rope_tables():
    pos = np.arange(SEQ)
    row, col = pos // GRID, pos % GRID
    inv = 10000.0 ** (-np.arange(16) / 16.0)
    cos, sin = np.zeros((P, SEQ)), np.zeros((P, SEQ))
    for d in range(P):
        e = d % HD
        ang = (row if e < 32 else col) * inv[e % 16]
        cos[d] = np.cos(ang)
        sin[d] = np.sin(ang) * (-1 if e % 32 < 16 else 1)
    return cos.astype(np.float32), sin.astype(np.float32)


def attention_masks():
    c = np.arange(GRID)
    c0 = np.clip(c - 8, 0, GRID - 16)
    ok = (c[None, :] >= c0[:, None]) & (c[None, :] < c0[:, None] + 16)
    cols = np.where(ok, 0, NEG)
    cols = np.concatenate([cols, cols]).astype(np.float32)
    rows = np.zeros((P, 10, GRID), np.float32)
    for par in range(2):
        for i in range(10):
            dr = i - 4 - par
            if not -4 <= dr <= 3:
                rows[64 * par:64 * par + 64, i] = NEG
    q, k = np.arange(P)[:, None], np.arange(3 * P)[None, :] - P
    window = np.where(np.abs(q - k) <= 128, 0, NEG).astype(np.float32)
    return cols, rows.reshape(P, 640), window


def filter_tables(L):
    t = np.linspace(0.0, 1.0, L, dtype=np.float32)
    w = (np.float32(2.0 * math.pi / L) * np.arange(L, dtype=np.float32)).astype(np.float32)
    f = np.linspace(1e-4, 15, 16, dtype=np.float32)
    a = (f[:, None] * w[None, :]).astype(np.float32).astype(np.float64)
    z = np.concatenate([t[None].astype(np.float64), np.cos(a), -np.sin(a)], 0)
    back = (L - np.arange(L)) % L
    feats = np.concatenate([z, z[:, back]], 0).astype(np.float32)
    lo, hi = math.log(1e-2) / 1.5, math.log(1e-2) / 0.3
    deltas = np.abs(np.linspace(lo, hi, CH, dtype=np.float32)).astype(np.float64)
    dec = np.exp(-t.astype(np.float64)[:, None] * deltas[None])
    late = dec[back]
    late[0] = 0.0
    both = np.concatenate([dec, late], 0).reshape(2 * L // P, P, CH)
    return feats, both.transpose(1, 0, 2).astype(np.float32)


def build(nc, A):
    ctx = ExitStack()
    with ctx:
        def sb(name, shape):
            return ctx.enter_context(nc.sbuf_tensor(name, shape, F32))

        R_SIZE, H_HI_AT = 26000, 15616
        with ExitStack() as places:
            def sb_r(name, shape):
                return places.enter_context(nc.sbuf_tensor(name, shape, F32R))
            act_r, mix_r, ring_r = sb_r("act_r", [P, KC, TOK]), sb_r("mix_r", [P, KC, TOK]), sb_r("ring_r", [P, RING, KC, P])
            low_r, high_r = sb_r("low_r", [P, H_HI_AT]), sb_r("high_r", [P, R_SIZE - H_HI_AT])
            w_hi = sb_r("w_hi", [P, 2, KC, P])
        act_t = sb("act_t", [P, KC, TOK])
        mix = sb("mix", [P, KC, TOK])
        ring = sb("ring", [P, RING, KC, P])
        region = sb("region", [P, R_SIZE])
        g_st = sb("g_st", [P, 2, 512])
        w12 = sb("w12", [P, 2, P])
        sb("w_hi_rest", [P, 2 * KC * P - 2 * 512 - 2 * P])
        ident = sb("ident", [P, P])
        ones = sb("ones", [P, P])
        condT = sb("condT", [P, KC, 2])
        silu_c = sb("silu_c", [P, KC, 2])
        norm_g = sb("norm_g", [P, DEPTH + 1, KC])
        b_ada = sb("b_ada", [P, DEPTH, N_ADA])
        ada = sb("ada", [P, DEPTH, N_ADA, 2])
        mod_a = sb("mod_a", [P, KC, 2])
        conv_w = sb("conv_w", [P, DEPTH, N_PB, 4])
        f_small = sb("f_small", [P, DEPTH, 4])
        sink = sb("sink", [P, DEPTH, 6])
        ps = ctx.enter_context(nc.psum_tensor("ps", [P, 8, 512], F32))

        def view(start, *shape):
            n = int(np.prod(shape))
            assert start + n <= R_SIZE, (start, shape)
            v = region[:, start:start + n]
            if len(shape) == 2:
                v = v.rearrange("p (a b) -> p a b", b=shape[1])
            if len(shape) == 3:
                v = v.rearrange("p (a b c) -> p a b c", b=shape[1], c=shape[2])
            return v

        sq = view(9216, 2, TOK)
        sq_sum = view(11776, TOK)
        diag = view(7424, NT + NTC, P)
        rms = view(8704, NT + NTC, 2)
        spec = view(0, NS_MAIN, 2, CH)
        khat = view(4608, NS_MAIN, 2, CH)
        decay = view(4608, 2 * NT, CH)
        z_tm = view(9216, NT + NTC, CH)
        x1_tm = view(11776, NT + NTC, CH)
        dft_f = view(14336, N_DFT, P)
        dft_i = view(17536, N_DFT, P)
        PAD = TOK + 4
        pc_in = view(20736, 2, PAD)
        pc_out = view(20736 + 2 * PAD, 2, PAD)
        hid = view(20736, SEQ)
        w3f = view(21760, 2 * CH)
        w3r = view(22272, 2 * CH)
        k_rt = view(22784, CH)
        k_s = view(23040, CH)
        prod = view(23296, 2, 2, 2 * CH)
        mlp = [view(1024 * i, SEQ) for i in range(3)]
        feats = view(3072, SEQ)
        early_w = [mix[:].rearrange("p a b -> p (a b)")[:, 2048 * i:2048 * (i + 1)] if i < 5 else
                   view(3072 + 2048 * (i - 5), 2048) for i in range(KC)]
        d_row = view(25600, CH)
        mark = view(R_SIZE - 8, 8)
        room = mix[:, 2:8, :].rearrange("p a b -> p (a b)").rearrange("p (u c) -> p u c", c=CH)
        k_fm = view(0, N_K, TOK)
        v_tm = view(5120, NT + NTC, 512)
        t_raw = view(10240, 6, 14, GRID)
        rope_cs = view(10240, 2, SEQ)
        rope_t = view(12288, 2, SEQ)
        t_edge = view(15616, 2, 896)
        t_inner = view(17408, 2, 640)
        s_sb = view(18688, 2, 896)
        p_sb = view(20480, 2, 896)
        pt_sb = view(22272, 2, 896)
        o_sb = view(24576, 2, P)
        m_cols = view(24832, GRID)
        m_rows = view(24896, 640)
        m_win = view(25536, 3 * P)
        stat = view(25920, 32)
        v_hi, v_lo = (low_r[:, at:at + N_V * KC * P].rearrange("p (k m) -> p k m", m=512) for at in (0, 10240))
        h_hi = high_r[:, 0:KC * TOK].rearrange("p (k t) -> p k t", t=TOK)

        k_hi, k_lo = act_r[:, 0:N_K], low_r[:, 0:N_K * TOK].rearrange("p (k t) -> p k t", t=TOK)
        q_hi, q_lo = (act_r[:, N_K, at:at + 4 * P].rearrange("p (a b c) -> p a b c", b=2, c=P) for at in (0, 4 * P))

        def mix_hi(k):
            return high_r[:, (k + 2) * TOK:(k + 3) * TOK] if k < 6 else low_r[:, (k - 2) * TOK:(k - 1) * TOK]
        g_in = view(15616, 2, TOK)
        x_in = view(0, 2, TOK)
        fin = view(9216, KC, SEQ)

        def sem(name):
            return ctx.enter_context(nc.semaphore(name))

        L2 = range(DEPTH)

        def per_layer(name):
            return [sem(f"{name}{l}") for l in L2]

        consts_in, consts_set, cond_in, silu_ready = sem("consts_in"), sem("consts_set"), sem("cond_in"), sem("silu_ready")
        early_in, early_done = [sem(f"early_in{b}") for b in range(2)], sem("early_done")
        x_loaded = [sem(f"x_loaded{b}") for b in range(2)]
        slot_in = [sem(f"slot_in{s}") for s in range(RING)]
        block_done = sem("block_done")
        block_taken = sem("block_taken")
        sq_ready = [sem(f"sq_ready{l}") for l in range(DEPTH + 1)]
        sq_used = [sem(f"sq_used{l}") for l in range(DEPTH + 1)]
        ms_mm, ms_ready, std_ready = sem("ms_mm"), sem("ms_ready"), sem("std_ready")
        diag_ready, rstd_mm = sem("diag_ready"), sem("rstd_mm")
        ada_ready, scaled, h_ready = sem("ada_ready"), per_layer("scaled"), per_layer("h_ready")
        pads_set, dft_in = sem("pads_set"), per_layer("dft_in")
        pc_ready, conv_ready = per_layer("pc_ready"), per_layer("conv_ready")
        tp_ready, tp_taken = per_layer("tp_ready"), per_layer("tp_taken")
        net_in = per_layer("net_in")
        fl_in, dec_in, drow_in = per_layer("fl_in"), per_layer("dec_in"), per_layer("drow_in")
        mlp_mm, arg_ready, hid_ready = per_layer("mlp_mm"), per_layer("arg_ready"), per_layer("hid_ready")
        tap_mm, tap_ready, tsq_ready, tsq_used = (per_layer(x) for x in ("tap_mm", "tap_ready", "tsq_ready", "tsq_used"))
        en_ready, rt_ready = per_layer("en_ready"), per_layer("rt_ready")
        bf_ready, x_mm, x_taken, prod_ready = (per_layer(x) for x in ("bf_ready", "x_mm", "x_taken", "prod_ready"))
        y_part, w_mm, w_taken = (per_layer(x) for x in ("y_part", "w_mm", "w_taken"))
        yt_ready, yt_mm, yt_taken, hyena_done = (per_layer(x) for x in ("yt_ready", "yt_mm", "yt_taken", "hyena_done"))
        hi_made, lo_made = sem("hi_made"), sem("lo_made")
        k_hi_made, k_split, k_rest = sem("k_hi_made"), sem("k_split"), sem("k_rest")
        v_hi_made, h_hi_made, h_split, mix_hi_made, mix_split = (
            per_layer(x) for x in ("v_hi_made", "h_hi_made", "h_split", "mix_hi_made", "mix_split"))
        v_mm, v_taken, rope_in, rope_done = (per_layer(x) for x in ("v_mm", "v_taken", "rope_in", "rope_done"))
        masks_in, traw_in, qst_zero = per_layer("masks_in"), per_layer("traw_in"), sem("qst_zero")
        qst_ready, s_ready, neg_ready, p_ready = sem("qst_ready"), sem("s_ready"), sem("neg_ready"), sem("p_ready")
        es_ready, pt_ready, pt_dve, pt_act = sem("es_ready"), sem("pt_ready"), sem("pt_dve"), sem("pt_act")
        o_ready, on_ready, ot_ready, ot_taken = sem("o_ready"), sem("on_ready"), sem("ot_ready"), sem("ot_taken")
        unit_step = sem("unit_step")
        g_mm, g_taken, mix_gated = (per_layer(x) for x in ("g_mm", "g_taken", "mix_gated"))
        g_stored = [[sem(f"g_stored{l}_{b}") for b in range(2)] for l in L2]
        g_in_in = [[sem(f"g_in_in{l}_{b}") for b in range(2)] for l in L2]
        xin_in = [[sem(f"xin_in{l}_{b}") for b in range(2)] for l in L2]
        x_stored, fin_ready = sem("x_stored"), sem("fin_ready")
        fin_out = sem("fin_out")
        vec_step = sem("vec_step")

        def back_tiles(isctx):
            return [(b, NT, NTC) for b in range(2)] if isctx else [(b, t, 4) for b in range(2) for t in (0, 4)]

        class Steps:
            def __init__(self, eng):
                self.eng, self.open, self.at = eng, {}, {}

            def __call__(self, ins, sem=None):
                s = vec_step if sem is None else sem
                self.at[s.name] = self.at.get(s.name, 0) + 1
                ins.then_inc(s, 1)
                self.open[s.name] = (s, self.at[s.name])

            def join(self):
                for s, n in self.open.values():
                    self.eng.wait_ge(s, n)
                self.open = {}

        def ntok(l):
            return TOK if l == 0 else SEQ

        def groups(n):
            return [(t, min(512, n - t)) for t in range(0, n, 512)]

        TAKEN = N_PB + N_Q + N_K + N_OUT

        def taken_before(l, stage):
            return l * TAKEN + dict(pb=0, k=N_PB, q=N_PB + N_K, out=TAKEN - N_OUT, end=TAKEN)[stage]

        SPLIT = [STREAM_AT[l, name, b] for l in L2 for name, n in (("k", N_K), ("q", N_Q), ("out", N_OUT)) for b in range(n)]

        def split_before(l, stage):
            return l * (N_K + N_Q + N_OUT) + (N_K + N_Q if stage == "out" else 0)

        def fillers(l):
            out = []
            for b in range(N_G):
                at = STREAM_AT[l, "g", b] + 1
                out += [("g", b, t, w) for t, w in groups(ntok(l))] + [("ada", at, at + LATE_PER[l])]
            return out

        def gate_parts(l):
            return [f for f in fillers(l) if f[0] == "g"]

        def done_at(l, stage):
            return STREAM_AT[l, stage, 0]

        FILLS = [[(3, 3, 4, 0, 5), (0, 3, 4, 0, 4), (0, 2, 1, 0, 1), (0, 2, 1, 0, 2)], [(2, 4, 3, 0, 4), (0, 4, 3, 0, 4)]]

        def time_tiles(l):
            return [(0, 4), (4, 4), (8, 2)] if l == 0 else [(0, 4), (4, 4)]

        def sq_t(i):
            return room[:, 16 + 2 * (i % 2):18 + 2 * (i % 2)].rearrange("p a b -> p (a b)")

        def jobs(l):
            main = [(False, o, NS_MAIN, NT) for o in range(2)]
            return main + ([(True, o, NS_CTX, NTC) for o in range(2)] if l == 0 else [])

        def q_tiles(l):
            near = {0: 0, 1: 0, 6: 4, 7: 4}
            a = [(j, near[j], 4) if j in near else (j, j - 2, 5) for j in range(NT)]
            c = [(j, max(j - 1, 0), 2 if j in (0, NT - 1) else 3) for j in range(NT)]
            x = [(NT + j, 0, 0) for j in range(NTC)] if l == 0 else []
            return [(kind, *where, *tile) for kind, tiles in (("A", a), ("A", x), ("C", c), ("C", x)) for tile in tiles
                    for where in [(MIX_A, None, 0) if kind == "A" else (MIX_C, N_K - 1, 384)]]

        def steps_of(tiles):
            return 2 + sum(2 + 2 * (2 if n else 1) + (2 if kind == "C" else 1) for kind, _, _, _, _, _, n in tiles)

        def sinks_of(tiles, units):
            return sum(tiles[k // 2][0] == "C" for k in range(units))

        before = [(0, 0, 0)]
        for l in L2:
            tiles = q_tiles(l)
            u, c, st = before[-1]
            before.append((u + 6 * len(tiles), c + 3 * sinks_of(tiles, 2 * len(tiles)), st + 3 * steps_of(tiles)))

        def chunks(tile):
            first, n = tile[5:]
            return [(i * P, NT + i) for i in range(NTC)] + [(CTX + i * P, first + i) for i in range(n)]

        block = ctx.enter_context(nc.Block())

        @block.sync
        def _(sp):
            for k in range(KC):
                if k >= 2:
                    sp.wait_ge(early_in[k % 2], 16 * (k // 2))
                sp.dma_start(early_w[k], A["early"][k]).then_inc(early_in[k % 2], 16)
            for s in range(RING):
                sp.dma_start(ring[:, s].rearrange("p k m -> p (k m)"), A["weights"][s]).then_inc(slot_in[s], 16)
            with sp.Fori(1, len(STREAM) // RING) as i:
                for s in range(RING):
                    sp.wait_ge(block_done, i * RING + (s + 1 - RING))
                    sp.dma_start(ring[:, s].rearrange("p k m -> p (k m)"),
                                 A["weights"][bass.ds(i * RING + s, 1)].rearrange("a p f -> (a p) f")
                                 ).then_inc(slot_in[s], 16)
            for m in range(KC):
                sp.wait_ge(fin_ready, m + 1)
                sp.dma_start(A["out"][m], fin[:, m]).then_inc(fin_out, 16)
            sp.wait_ge(fin_out, 16 * KC)

        @block.gpsimd
        def _(pool):
            g = nc.gpsimd
            g.memset(ones[:], 1.0).then_inc(consts_set, 1)
            for k in range(KC):
                if k >= 2:
                    pool.wait_ge(x_loaded[k % 2], 16 * (k // 2))
                pool.dma_start(act_t[:, k], A["x_blocks"][k]).then_inc(x_loaded[k % 2], 16)
            for dst, src in ((ident[:], A["ident"]), (norm_g[:], A["norm_g"]),
                             (b_ada[:], A["b_ada"]), (conv_w[:], A["conv_w"]), (f_small[:], A["f_small"]),
                             (sink[:], A["sink"])):
                pool.dma_start(dst, src).then_inc(consts_in, 16)
            for l in L2:
                if l:
                    pool.wait_ge(block_taken, taken_before(l, "pb"))
                else:
                    pool.wait_ge(early_done, KC)
                pool.dma_start(w12[:], A["w12"][l]).then_inc(net_in[l], 16)
                pool.dma_start(feats[0:66, 0:SEQ], A["feats"]).then_inc(net_in[l], 16)
                for b in range(2):
                    g.memset(pc_in[:, b, 0:1], 0.0).then_inc(pads_set, 1)
                    g.memset(pc_in[:, b, SEQ + 1:SEQ + 3], 0.0).then_inc(pads_set, 1)
                    g.memset(pc_in[:, b, PAD - 1:PAD], 0.0).then_inc(pads_set, 1)
                pool.dma_start(dft_f, A["dft_f"]).then_inc(dft_in[l], 16)
                pool.dma_start(dft_i, A["dft_i"]).then_inc(dft_in[l], 16)
                pool.wait_ge(conv_ready[l], N_PB)
                pool.wait_ge(tp_ready[l], 4 * len(time_tiles(l)))
                pool.dma_start(w3f, A["w3"][l, 0]).then_inc(fl_in[l], 16)
                pool.dma_start(w3r, A["w3"][l, 1]).then_inc(fl_in[l], 16)
                conv_n = x_n = 0
                for ji, (isctx, o, ns, nt) in enumerate(jobs(l)):
                    nm = "_ctx" if isctx else ""
                    if o == 0 and isctx:
                        pool.wait_ge(yt_ready[l], 1)
                        pool.dma_start(feats[0:66, 0:nt * P], A["feats_ctx"]).then_inc(net_in[l], 16)
                    if ji:
                        pool.wait_ge(x_taken[l], x_n)
                    pool.dma_start(decay[:, 0:2 * nt], A["decay" + nm]).then_inc(dec_in[l], 16)
                    pool.dma_start(d_row[0:1], A["hy_d"][l, o:o + 1]).then_inc(drow_in[l], 16)
                    x_n += ns
                    for s in range(ns):
                        pr_a, pr_b = prod[:, conv_n % 2, 0], prod[:, conv_n % 2, 1]
                        x_n += 1
                        conv_n += 1
                        pool.wait_ge(prod_ready[l], conv_n)
                        pool.wait_ge(x_taken[l], x_n)
                        g.tensor_tensor(spec[:, s, 0], pr_a[:, 0:CH], pr_b[:, CH:], ALU.subtract).then_inc(y_part[l], 1)
                        g.tensor_tensor(spec[:, s, 1], pr_a[:, CH:], pr_b[:, 0:CH], ALU.add).then_inc(y_part[l], 1)
                pool.wait_ge(hyena_done[l], 1)
                pool.wait_ge(block_done, STREAM_AT[l, "v", 0])
                for b in range(N_V):
                    pool.wait_ge(v_hi_made[l], b + 1)
                    both = slice(2 * b, 2 * b + 2)
                    g.tensor_tensor(v_lo[:, both].rearrange("p k m -> p (k m)"),
                                    ring[:, STREAM_AT[l, "v", b] % RING].rearrange("p k m -> p (k m)"),
                                    v_hi[:, both].rearrange("p k m -> p (k m)"), ALU.subtract).then_inc(block_done, 1)
                pool.wait_ge(v_taken[l], NT + NTC)
                pool.dma_start(rope_cs, A["rope"]).then_inc(rope_in[l], 16)
                pool.wait_ge(rope_done[l], 1)
                for h in range(6):
                    for par in range(2):
                        pool.dma_start(t_raw[64 * par:64 * par + 64, h].rearrange("p a b -> p (a b)"),
                                       A["rpb"][l, h, :, 1 - par:15 - par].rearrange("p a b -> p (a b)")
                                       ).then_inc(traw_in[l], 16)
                pool.wait_ge(block_done, STREAM_AT[l, "q", N_Q - 1] + 1)
                g.memset(act_r[:, N_K, 0:8 * P].bitcast(F32), 0.0).then_inc(qst_zero, 1)
                for dst, src in ((m_cols, "m_cols"), (m_rows, "m_rows"), (m_win, "m_win")):
                    pool.dma_start(dst, A[src]).then_inc(masks_in[l], 16)
                pool.wait_ge(rope_done[l], 1)
                for b in range(1, N_K):
                    g.tensor_copy(k_hi[:, b], k_fm[:, b]).then_inc(k_rest, 1)
                for b in range(1, N_K):
                    pool.wait_ge(k_rest, 2 * (N_K - 1) * l + b)
                    g.tensor_tensor(k_lo[:, b], k_fm[:, b], k_hi[:, b], ALU.subtract).then_inc(k_rest, 1)
                pool.wait_ge(neg_ready, before[l][0] + 4 * len(q_tiles(l)) + 2 * NT)
                for b in range(2):
                    pool.wait_ge(g_stored[l][b], 16 * (len(gate_parts(l)) // 2))

                def load_gate(m):
                    pool.dma_start(g_in[:, m % 2, 0:ntok(l)], A["gates"][m, :, 0:ntok(l)]).then_inc(g_in_in[l][m % 2], 16)
                load_gate(0)
                load_gate(1)
                tiles_before, n_tiles = before[l][0] // 2, len(q_tiles(l))
                for m in range(N_G):
                    if m == 0:
                        pool.wait_ge(ot_taken, tiles_before + 3 * n_tiles - n_tiles // 2)
                    if m == N_G - 1:
                        pool.wait_ge(ot_taken, tiles_before + 3 * n_tiles)
                    pool.wait_ge(g_in_in[l][m % 2], 16 * (m // 2 + 1))
                    g.tensor_tensor(mix[:, m, 0:ntok(l)], mix[:, m, 0:ntok(l)], g_in[:, m % 2, 0:ntok(l)],
                                    ALU.mult).then_inc(mix_gated[l], 1)
                    if m + 2 < N_G:
                        pool.wait_ge(mix_gated[l], m + 1)
                        load_gate(m + 2)
                if l:
                    pool.wait_ge(x_stored, 16 * KC)
                for m in range(KC):
                    if m >= 2:
                        pool.wait_ge(block_taken, taken_before(l, "out") + m - 1)
                    pool.dma_start(x_in[:, m % 2], A["x_mid" if l else "x_blocks"][m]).then_inc(xin_in[l][m % 2], 16)
                    if l == 0 and m >= 1:
                        pool.wait_ge(block_taken, taken_before(l, "out") + m)
                        pool.dma_start(A["x_mid"][m - 1], act_t[:, m - 1]).then_inc(x_stored, 16)
                if l == 0:
                    pool.wait_ge(block_taken, taken_before(l, "end"))
                    pool.dma_start(A["x_mid"][KC - 1], act_t[:, KC - 1]).then_inc(x_stored, 16)

        @block.tensor
        def _(pe):
            mm, tr = nc.tensor.matmul, nc.tensor.transpose
            at = [0]

            def over_blocks(n, emit):
                turns = n // RING if n // RING >= 2 else 0
                if turns:
                    with pe.Fori(0, turns) as i:
                        for b in range(RING):
                            pos = at[0] + b
                            pe.wait_ge(slot_in[pos % RING], (i + (pos // RING + 1)) * 16)
                            emit(i * RING + b, pos % RING)
                for b in range(turns * RING, n):
                    pos = at[0] + b
                    pe.wait_ge(slot_in[pos % RING], 16 * (pos // RING + 1))
                    emit(b, pos % RING)
                at[0] += n

            def project_split(hi, lo, n, first_taken, first_split, src_ready):
                def emit(idx, s):
                    parity = s % 2
                    pe.wait_ge(block_taken, idx + (first_taken - 1))
                    pe.wait_ge(lo_made, idx + (first_split + 1))
                    for k in range(KC):
                        if not isinstance(idx, int) or idx == 0:
                            pe.wait_ge(src_ready, k + 1)
                        gs = [(ps[:, 3 * parity + gi, 0:w], t, w) for gi, (t, w) in enumerate(groups(n))]
                        for out, t, w in gs:
                            mm(out, w_hi[:, parity, k], hi(k)[:, t:t + w], start=(k == 0), stop=False)
                            mm(out, w_hi[:, parity, k], lo[:, k, t:t + w], start=False, stop=False)
                        for out, t, w in gs:
                            last = mm(out, ring_r[:, s, k], hi(k)[:, t:t + w], start=False, stop=(k == KC - 1))
                    last.then_inc(block_done, 1)
                return emit

            def project(src, n, first_taken, src_ready=None, per_chunk=1):
                def emit(idx, s):
                    parity = s % 2
                    if first_taken or not isinstance(idx, int) or idx >= 2:
                        pe.wait_ge(block_taken, idx + (first_taken - 1))
                    for k in range(KC):
                        if src_ready is not None and (idx == 0 if isinstance(idx, int) else s == 0):
                            pe.wait_ge(src_ready, (k + 1) * per_chunk)
                        for gi, (t, w) in enumerate(groups(n)):
                            last = mm(ps[:, 3 * parity + gi, 0:w], ring[:, s, k], src[:, k, t:t + w],
                                      start=(k == 0), stop=(k == KC - 1))
                    last.then_inc(block_done, 1)
                return emit

            def rms_of_tokens(l, n):
                pe.wait_ge(sq_used[l], KC - 1)
                for t in range(n // P):
                    last = mm(ps[:, 0, 2 * t:2 * t + 2], sq_sum[:, t * P:(t + 1) * P], ones[:, 0:2], start=True, stop=True)
                last.then_inc(ms_mm, 1)
                pe.wait_ge(diag_ready, l + 1)
                for gi, (t, w) in enumerate(groups(n)):
                    last = mm(ps[:, 3 + gi, 0:w], ones[:], diag[:, t // P:(t + w) // P].rearrange("p a b -> p (a b)"),
                              start=True, stop=True)
                last.then_inc(rstd_mm, 1)

            def transform(mats, slot, bank, inverse):
                m0, out = DFT_START[slot], ps[:, bank]
                if slot < 2 and not inverse:
                    mm(out[:, 0:CH], mats[:, m0], spec[:, slot, 0], start=True, stop=True)
                    return mm(out[:, CH:], mats[:, m0 + 1], spec[:, slot, 0], start=True, stop=True)
                if slot < 2:
                    mm(out[:, 0:CH], mats[:, m0], spec[:, slot, 0], start=True, stop=False)
                    return mm(out[:, 0:CH], mats[:, m0 + 1], spec[:, slot, 1], start=False, stop=True)
                plus, minus = (m0 + 2, m0 + 1) if inverse else (m0 + 1, m0 + 2)
                mm(out, mats[:, m0], spec[:, slot].rearrange("p a c -> p (a c)"), start=True, stop=False,
                   skip_group_check=True)
                mm(out[:, 0:CH], mats[:, plus], spec[:, slot, 1], start=False, stop=False, skip_group_check=True)
                return mm(out[:, CH:], mats[:, minus], spec[:, slot, 0], start=False, stop=True, skip_group_check=True)

            def network(l, layer, isctx, bank, n):
                if layer == 0:
                    pe.wait_ge(net_in[l], 16 * (2 + isctx))
                else:
                    pe.wait_ge(hid_ready[l], 2 * isctx + 1)
                for gi, (t, w) in enumerate(groups(n)):
                    lhs, rhs = (w12[0:66, 0], feats[0:66, t:t + w]) if layer == 0 else (w12[:, 1], mlp[2][:, t:t + w])
                    last = mm(ps[:, bank + gi, 0:w], lhs, rhs, start=True, stop=True)
                last.then_inc(mlp_mm[l], 1)

            def hyena(l, fill):
                taps = bf = xn = wn = 0
                for ji, (isctx, o, ns, nt) in enumerate(jobs(l)):
                    at_start, at_taps, at_signal, at_slot, at_end = FILLS[l][ji]
                    fill(at_start)
                    if ji == 0:
                        pe.wait_ge(fl_in[l], 32)
                        pe.wait_ge(block_taken, taken_before(l, "k"))
                    if o == 0:
                        if isctx:
                            for layer in range(2):
                                network(l, layer, isctx, 2 * layer, nt * P)
                        pe.wait_ge(hid_ready[l], 2 * isctx + 2)
                    if isctx and o == 0:
                        pe.wait_ge(yt_taken[l], 4)
                    for i in range(nt):
                        if taps >= 2:
                            pe.wait_ge(tap_ready[l], taps - 1)
                        for e in range(2):
                            t = 2 * i + e
                            last = mm(ps[:, 4 + taps % 2, e * CH:(e + 1) * CH], hid[:, (t % nt) * P:(t % nt + 1) * P],
                                      (w3f if t < nt else w3r)[:, o * CH:(o + 1) * CH], start=True, stop=True)
                        last.then_inc(tap_mm[l], 1)
                        taps += 1
                    for i in range(nt):
                        pe.wait_ge(tsq_ready[l], taps - nt + i + 1)
                        mm(ps[:, 1], ones[:], sq_t(i), start=(i == 0), stop=(i == nt - 1)).then_inc(tsq_used[l], 1)
                    if ji == 0:
                        pe.wait_ge(dft_in[l], 32)
                    fill(at_taps)
                    for signal in range(2):
                        if signal:
                            fill(at_signal)
                        for s in range(ns + signal):
                            if s < ns:
                                pe.wait_ge(bf_ready[l], bf + s + 1)
                                if xn >= 2:
                                    pe.wait_ge(x_taken[l], xn - 1)
                                transform(dft_f, s, xn % 2, False).then_inc(x_mm[l], 1)
                                xn += 1
                            if signal and s >= 1:
                                pe.wait_ge(y_part[l], 2 * (wn + 1))
                                if wn >= 2:
                                    pe.wait_ge(w_taken[l], wn - 1)
                                transform(dft_i, s - 1, 2 + wn % 2, True).then_inc(w_mm[l], 1)
                                wn += 1
                                if s in (3, 6):
                                    fill(at_slot)
                        bf += ns
                    fill(at_end)
                    if o == 1:
                        pe.wait_ge(yt_ready[l], 1 + isctx)
                        for gi, (b, t0, w) in enumerate(back_tiles(isctx)):
                            if gi >= 2 or isctx:
                                pe.wait_ge(yt_taken[l], 4 * isctx + gi - 1 if gi >= 2 else 4)
                            for e in range(w):
                                last = tr(ps[:, 4 + gi % 2, e * P:(e + 1) * P], z_tm[:, t0 + e, b * P:(b + 1) * P], ident[:])
                            last.then_inc(yt_mm[l], 1)

            def attention(l):
                tiles = q_tiles(l)
                base, _, _ = before[l]
                nu = 2 * len(tiles)
                with pe.Fori(0, 3) as pr:
                    u0 = pr * nu + base
                    w0 = pr * (nu // 2) + base // 2

                    def times_k(out, q, kb, t0, n):
                        hi, lo = ((part[:, bass.ds(pr, 1), t0:t0 + n].rearrange("p a b -> p (a b)") if kb is None else
                                   part[:, kb, t0:t0 + n]) for part in (k_hi, k_lo))
                        mm(out, q[0], hi, start=True, stop=False)
                        mm(out, q[0], lo, start=False, stop=False)
                        return mm(out, q[1], hi, start=False, stop=True)

                    def scores(k):
                        ji, par = divmod(k, 2)
                        _, _, kb, _, _, first, n = tiles[ji]
                        if par == 0:
                            pe.wait_ge(qst_ready, u0 + (k + 2))
                        if k >= 2:
                            pe.wait_ge(neg_ready, u0 + (k - 1))
                        if kb is not None and tiles[ji - 1][2] is None:
                            pe.wait_ge(k_rest, 2 * (N_K - 1) * (l + 1))
                        bank, q = 2 * (k % 2), (q_hi[:, ji % 2, par], q_lo[:, ji % 2, par])
                        if n:
                            w = min(n, 4) * P
                            times_k(ps[:, bank, 0:w], q, kb, first * P, w)
                        if n > 4:
                            times_k(ps[:, bank + 1, 0:P], q, kb, (first + 4) * P, P)
                        times_k(ps[:, bank + 1, P:P + CTX], q, kb, SEQ, CTX).then_inc(s_ready, 1)

                    def transpose_p(k):
                        pe.wait_ge(p_ready, u0 + (k + 1))
                        if k >= 1:
                            pe.wait_ge(pt_dve, u0 + k)
                            pe.wait_ge(pt_act, u0 + k)
                        cs = chunks(tiles[k // 2])
                        half = (len(cs) + 1) // 2
                        for c, (col, _) in enumerate(cs):
                            bank, at_col = (4, c) if c < half else (5, c - half)
                            last = tr(ps[:, bank, at_col * P:(at_col + 1) * P], p_sb[:, k % 2, col:col + P], ident[:])
                        last.then_inc(pt_ready, 1)

                    def times_v(k):
                        ji, par = divmod(k, 2)
                        kb, vcol = tiles[ji][2:4]
                        pe.wait_ge(pt_dve, u0 + (k + 1))
                        pe.wait_ge(pt_act, u0 + (k + 1))
                        if par == 0 and ji >= 2:
                            pe.wait_ge(ot_taken, w0 + (ji - 1))
                        cs = chunks(tiles[ji])
                        for c, (_, t) in enumerate(cs):
                            v = v_tm[:, t, bass.ds(pr * P + par * HD, HD)] if kb is None else \
                                v_tm[:, t, vcol + par * HD:vcol + (par + 1) * HD]
                            last = mm(ps[:, 6 + ji % 2, par * HD:(par + 1) * HD], pt_sb[:, k % 2, c * P:(c + 1) * P], v,
                                      start=(c == 0), stop=(c == len(cs) - 1))
                        last.then_inc(o_ready, 1)

                    def transpose_o(w):
                        pe.wait_ge(on_ready, u0 + (2 * w + 2))
                        tr(ps[:, 6 + w % 2, P:2 * P], o_sb[:, w % 2], ident[:]).then_inc(ot_ready, 1)

                    scores(0)
                    scores(1)
                    for k in range(nu):
                        transpose_p(k)
                        if k + 2 < nu:
                            scores(k + 2)
                        times_v(k)
                        if k >= 2 and k % 2 == 0:
                            transpose_o(k // 2 - 1)
                    transpose_o(nu // 2 - 1)

            def filler(l):
                parts, done = fillers(l), [0]

                def fill(n):
                    for _ in range(min(n, len(parts) - done[0])):
                        c, part = done[0], parts[done[0]]
                        if c >= 2:
                            pe.wait_ge(g_taken[l], c - 1)
                        out = ps[:, 6 + c % 2]
                        if part[0] == "g":
                            _, b, t, w = part
                            s = at[0] % RING
                            if t == 0:
                                pe.wait_ge(slot_in[s], 16 * (at[0] // RING + 1))
                            for k in range(KC):
                                last = mm(out[:, 0:w], ring[:, s, k], act_t[:, k, t:t + w], start=(k == 0), stop=(k == KC - 1))
                            if t + w == ntok(l):
                                last.then_inc(block_done, 1)
                                at[0] += 1
                            else:
                                last.then_inc(g_mm[l], 1)
                        else:
                            for i in range(part[2] - part[1]):
                                s = at[0] % RING
                                pe.wait_ge(slot_in[s], 16 * (at[0] // RING + 1))
                                for k in range(KC):
                                    last = mm(out[:, 2 * i:2 * i + 2], ring[:, s, k], silu_c[:, k],
                                              start=(k == 0), stop=(k == KC - 1))
                                last.then_inc(block_done, 1)
                                at[0] += 1
                        done[0] += 1
                return fill

            pe.wait_ge(consts_set, 1)
            pe.wait_ge(silu_ready, 1)
            for l in L2:
                n = ntok(l)

                if l == 0:
                    for part in range(KC):
                        pe.wait_ge(early_in[part % 2], 16 * (part // 2 + 1))
                        w = early_w[part].rearrange("p (b k m) -> p b k m", b=2, k=KC)
                        for b in range(2):
                            col = 2 * (2 * part + b)
                            for k in range(KC):
                                last = mm(ps[:, 5, col:col + 2], w[:, b, k], silu_c[:, k], start=(k == 0), stop=(k == KC - 1))
                        last.then_inc(early_done, 1)
                rms_of_tokens(l, TOK)

                def to_time(b):
                    pe.wait_ge(conv_ready[l], b + 1)
                    for gi, (t0, w) in enumerate(time_tiles(l)):
                        c = b * len(time_tiles(l)) + gi
                        if c >= 2:
                            pe.wait_ge(tp_taken[l], c - 1)
                        for t in range(t0, t0 + w):
                            col = 1 + t * P + (2 if t >= NT else 0)
                            last = tr(ps[:, 6 + c % 2, (t - t0) * P:(t - t0 + 1) * P], pc_out[:, b % 2, col:col + P], ident[:])
                        last.then_inc(tp_ready[l], 1)

                if l == 0:
                    pe.wait_ge(consts_in, 16 * 6)
                if l == 0:
                    pe.wait_ge(ada_ready, 1)
                network(l, 0, False, 6, SEQ)
                emit = project(act_t, n, taken_before(l, "pb"), h_ready[l], 2)

                def pb_block(idx, s):
                    emit(idx, s)
                    if idx == 0:
                        network(l, 1, False, 6, SEQ)
                    if 1 <= idx <= 4:
                        to_time(idx - 1)
                for b in range(N_PB):
                    s = at[0] % RING
                    pe.wait_ge(slot_in[s], 16 * (at[0] // RING + 1))
                    pb_block(b, s)
                    at[0] += 1
                pe.wait_ge(tp_taken[l], 4 * len(time_tiles(l)))
                fill = filler(l)
                hyena(l, fill)
                fill(len(fillers(l)))
                pe.wait_ge(g_taken[l], len(fillers(l)))

                for t in range(NT + NTC):
                    if t >= 2:
                        pe.wait_ge(v_taken[l], t - 1)
                    for k in range(KC):
                        if t == 0:
                            pe.wait_ge(h_split[l], k + 1)
                            pe.wait_ge(block_done, STREAM_AT[l, "v", k // 2] + 1)
                        cols = slice(t * P, (t + 1) * P)
                        out = ps[:, 6 + t % 2]
                        mm(out, h_hi[:, k, cols], v_hi[:, k], start=(k == 0), stop=False)
                        mm(out, h_hi[:, k, cols], v_lo[:, k], start=False, stop=False)
                        last = mm(out, act_r[:, k, cols], v_hi[:, k], start=False, stop=(k == KC - 1))
                    last.then_inc(v_mm[l], 1)
                at[0] += N_V

                def h(n):
                    return project_split(lambda k: h_hi[:, k], act_r, n, taken_before(l, "k"), split_before(l, "k"),
                                         h_split[l])
                if l == 0:
                    over_blocks(N_K + N_Q, h(TOK))
                else:
                    over_blocks(N_K, h(TOK))
                    over_blocks(N_Q, lambda idx, s: h(n)(N_K + idx, s))
                pe.wait_ge(v_taken[l], NT + NTC)
                pe.wait_ge(rope_done[l], 1)
                pe.wait_ge(qst_zero, l + 1)
                pe.wait_ge(k_split, l + 1)
                attention(l)

                over_blocks(N_OUT, project_split(mix_hi, mix_r, n, taken_before(l, "out"), split_before(l, "out"), mix_split[l]))
            rms_of_tokens(DEPTH, SEQ)

        @block.scalar
        def _(act):
            fn = nc.scalar.activation

            def square(l, n, k):
                if l == 0:
                    act.wait_ge(x_loaded[k % 2], 16 * (k // 2 + 1))
                else:
                    act.wait_ge(block_taken, taken_before(l - 1, "out") + k + 1)
                if k >= 3:
                    act.wait_ge(sq_used[l], k - 2)
                fn(sq[:, k % 2, 0:n] if k else sq_sum[:, 0:n], act_t[:, k, 0:n], ACT.Square).then_inc(sq_ready[l], 1)

            def roots(l, n):
                act.wait_ge(ms_ready, l + 1)
                fn(rms[:, 0:n // P], rms[:, 0:n // P], ACT.Sqrt).then_inc(std_ready, 1)

            def upper_part(j):
                act.wait_ge(slot_in[SPLIT[j] % RING], 16 * (SPLIT[j] // RING + 1))
                if j >= 2:
                    act.wait_ge(block_done, SPLIT[j - 2] + 1)
                fn(w_hi[:, j % 2], ring[:, SPLIT[j] % RING], ACT.Copy).then_inc(hi_made, 1)

            def attention(l):
                tiles = q_tiles(l)
                base, _, _ = before[l]
                nu = 2 * len(tiles)
                with act.Fori(0, 3) as pr:
                    u0 = pr * nu + base

                    def exps(k):
                        n = CTX + tiles[k // 2][6] * P
                        act.wait_ge(neg_ready, u0 + (k + 1))
                        if k >= 2:
                            act.wait_ge(pt_ready, u0 + (k - 1))
                        fn(p_sb[:, k % 2, 0:n], s_sb[:, k % 2, 0:n], ACT.Exp, bias=stat[:, k % 2:k % 2 + 1],
                           accum_out=stat[:, 8 + k % 4:9 + k % 4]).then_inc(p_ready, 1)
                        if tiles[k // 2][0] == "C":
                            fn(stat[:, 12 + k % 4:13 + k % 4], sink[:, l, bass.ds(pr * 2 + k % 2, 1)], ACT.Exp,
                               bias=stat[:, k % 2:k % 2 + 1]).then_inc(es_ready, 1)

                    def take_pt(k):
                        cs = len(chunks(tiles[k // 2]))
                        half = (cs + 1) // 2
                        act.wait_ge(pt_ready, u0 + (k + 1))
                        if k >= 2:
                            act.wait_ge(o_ready, u0 + (k - 1))
                        fn(pt_sb[:, k % 2, half * P:cs * P], ps[:, 5, 0:(cs - half) * P], ACT.Copy).then_inc(pt_act, 1)

                    exps(0)
                    for k in range(nu):
                        take_pt(k)
                        if k + 1 < nu:
                            exps(k + 1)

            def hidden(l, layer, isctx, n):
                act.wait_ge(arg_ready[l], 2 * isctx + layer + 1)
                fn((hid if layer else mlp[2])[:, 0:n], mlp[0][:, 0:n], ACT.Sin).then_inc(hid_ready[l], 1)

            def filler(l):
                parts, done, gates = fillers(l), [0], [0]

                def fill(n):
                    for _ in range(min(n, len(parts) - done[0])):
                        c, gc, part = done[0], gates[0], parts[done[0]]
                        src = ps[:, 6 + c % 2]
                        done[0] += 1
                        if part[0] == "ada":
                            act.wait_ge(block_done, part[2])
                            for i, (m, _, b) in enumerate(STREAM[part[1]:part[2]]):
                                last = fn(ada[:, m, b], src[:, 2 * i:2 * i + 2], ACT.Identity, bias=b_ada[:, m, b:b + 1])
                            last.then_inc(g_taken[l], 1)
                            continue
                        _, b, t, w = part
                        if t + w == ntok(l):
                            act.wait_ge(block_done, STREAM_AT[l, "g", b] + 1)
                        else:
                            act.wait_ge(g_mm[l], gc - b + 1)
                        if gc >= 2:
                            act.wait_ge(g_stored[l][gc % 2], 16 * (gc // 2))
                        elif l:
                            act.wait_ge(g_stored[0][gc], 16 * (len(gate_parts(0)) // 2))
                        fn(g_st[:, gc % 2, 0:w], src[:, 0:w], ACT.Silu).then_inc(g_taken[l], 1)
                        act.wait_ge(g_taken[l], c + 1)
                        if l and gc == 0:
                            act.wait_ge(mix_gated[0], N_G)
                        act.dma_start(A["gates"][b, :, t:t + w], g_st[:, gc % 2, 0:w]).then_inc(g_stored[l][gc % 2], 16)
                        gates[0] += 1
                return fill

            act.dma_start(condT[:], A["cond"]).then_inc(cond_in, 16)
            act.wait_ge(cond_in, 16)
            fn(silu_c[:], condT[:], ACT.Silu).then_inc(silu_ready, 1)
            for l in L2:
                n = ntok(l)
                if l == 0:
                    for k in range(KC):
                        square(l, TOK, k)
                roots(l, TOK)
                if l == 0:
                    act.wait_ge(consts_in, 16 * 6)
                if l == 0:
                    act.wait_ge(ada_ready, 1)
                for k in range(KC):
                    for c, (t0, t1) in enumerate(((0, SEQ), (SEQ, TOK))):
                        act.wait_ge(scaled[l], 2 * k + c + 1)
                        fn(act_t[:, k, t0:t1], act_t[:, k, t0:t1], ACT.Identity,
                           bias=ada[:, l, k, c:c + 1]).then_inc(h_ready[l], 1)

                hidden(l, 0, False, SEQ)

                act.wait_ge(pads_set, 6 * (l + 1))

                def pad_block(b):
                    act.wait_ge(block_done, done_at(l, "pb") + b + 1)
                    if b >= 2:
                        act.wait_ge(conv_ready[l], b - 1)
                    src = ps[:, 3 * (b % 2):3 * (b % 2) + 3].rearrange("p a b -> p (a b)")
                    fn(pc_in[:, b % 2, 1:1 + SEQ], src[:, 0:SEQ], ACT.Copy).then_inc(pc_ready[l], 1)
                    if l == 0:
                        fn(pc_in[:, b % 2, SEQ + 3:SEQ + 3 + CTX], src[:, SEQ:TOK], ACT.Copy).then_inc(pc_ready[l], 1)

                def take_tiles(b):
                    dst = z_tm if b < 2 else x1_tm
                    for gi, (t0, w) in enumerate(time_tiles(l)):
                        c = b * len(time_tiles(l)) + gi
                        act.wait_ge(tp_ready[l], c + 1)
                        fn(dst[:, t0:t0 + w, (b % 2) * P:(b % 2 + 1) * P],
                           ps[:, 6 + c % 2, 0:w * P].rearrange("p (a b) -> p a b", b=P), ACT.Copy).then_inc(tp_taken[l], 1)

                pad_block(0)
                for b in range(1, N_PB):
                    pad_block(b)
                    if b <= 4:
                        take_tiles(b - 1)

                taps = wn = 0
                fill = filler(l)
                for ji, (isctx, o, ns, nt) in enumerate(jobs(l)):
                    at_start, at_taps, at_signal, at_slot, at_end = FILLS[l][ji]
                    if o == 0:
                        if isctx:
                            hidden(l, 0, isctx, nt * P)
                        else:
                            act.wait_ge(conv_ready[l], N_PB)
                            act.wait_ge(tp_ready[l], 4 * len(time_tiles(l)))
                        hidden(l, 1, isctx, nt * P)
                    fill(at_start)
                    for i in range(nt):
                        act.wait_ge(tap_ready[l], taps + i + 1)
                        if i >= 2:
                            act.wait_ge(tsq_used[l], taps + i - 1)
                        fn(sq_t(i), room[:, 2 * i:2 * i + 2].rearrange("p a b -> p (a b)"), ACT.Square).then_inc(tsq_ready[l], 1)
                    taps += nt
                    act.wait_ge(en_ready[l], ji + 1)
                    fn(k_rt, k_rt, ACT.Sqrt).then_inc(rt_ready[l], 1)
                    fill(at_taps)
                    fill(at_signal)
                    for s in range(ns):
                        act.wait_ge(w_mm[l], wn + 1)
                        w = CH if s < 2 else 2 * CH
                        fn(spec[:, s].rearrange("p a c -> p (a c)")[:, 0:w], ps[:, 2 + wn % 2, 0:w], ACT.Copy
                           ).then_inc(w_taken[l], 1)
                        wn += 1
                        if s in (2, 5):
                            fill(at_slot)
                    fill(at_end)
                fill(len(fillers(l)))

                act.wait_ge(hyena_done[l], 1)
                for k in range(KC):
                    if k % 2 == 0:
                        pos = STREAM_AT[l, "v", k // 2]
                        act.wait_ge(slot_in[pos % RING], 16 * (pos // RING + 1))
                        fn(v_hi[:, k:k + 2].rearrange("p k m -> p (k m)"), ring[:, pos % RING].rearrange("p k m -> p (k m)"),
                           ACT.Copy).then_inc(v_hi_made[l], 1)
                    fn(h_hi[:, k], act_t[:, k], ACT.Copy).then_inc(h_hi_made[l], 1)
                for b in range(2):
                    act.wait_ge(g_stored[l][b], 16 * (len(gate_parts(l)) // 2))

                first = split_before(l, "k")
                for t in range(NT + NTC):
                    if t == NT:
                        upper_part(first)
                        upper_part(first + 1)
                    act.wait_ge(v_mm[l], t + 1)
                    fn(v_tm[:, t], ps[:, 6 + t % 2], ACT.Copy).then_inc(v_taken[l], 1)
                for j in range(2, N_K + N_Q):
                    upper_part(first + j)
                act.wait_ge(rope_done[l], 1)
                act.wait_ge(block_done, STREAM_AT[l, "q", N_Q - 1] + 1)
                fn(k_hi[:, 0], k_fm[:, 0], ACT.Copy).then_inc(k_hi_made, 1)

                attention(l)

                first = split_before(l, "out")
                upper_part(first)
                upper_part(first + 1)
                act.wait_ge(ot_taken, before[l + 1][0] // 2)
                for k in range(KC):
                    act.wait_ge(mix_gated[l], k + 1)
                    fn(mix_hi(k)[:, 0:n], mix[:, k, 0:n], ACT.Copy).then_inc(mix_hi_made[l], 1)
                for j in range(2, N_OUT):
                    upper_part(first + j)
                    square(l + 1, n, j - 2)
                for k in range(N_OUT - 2, KC):
                    square(l + 1, n, k)

            roots(DEPTH, SEQ)

        @block.vector
        def _(dve):
            v = nc.vector
            step = Steps(dve)

            def tt(out, a, op, b, sem=None):
                step(v.tensor_tensor(out, a, b, op), sem)

            def stt(out, a, c, op, b, sem=None):
                step(v.scalar_tensor_tensor(out=out, in0=a, scalar=c, in1=b, op0=ALU.mult, op1=op), sem)

            def mul(out, a, c, sem=None):
                step(v.tensor_scalar(out, a, c, None, ALU.mult), sem)

            add, sub, mult = ALU.add, ALU.subtract, ALU.mult
            rstd = ps[:, 3:6].rearrange("p a b -> p (a b)")

            def add_squares(l, n, k):
                dve.wait_ge(sq_ready[l], k + 1)
                tt(sq_sum[:, 0:n], sq_sum[:, 0:n], add, sq[:, k % 2, 0:n], sq_used[l])
                step.join()

            def norm(l, n):
                tiles = n // P
                r = rms[:, 0:tiles]
                dve.wait_ge(ms_mm, l + 1)
                sums = ps[:, 0, 0:2 * tiles].rearrange("p (a b) -> p a b", b=2)
                step(v.tensor_scalar(r, sums, 1.0 / D, EPS, mult, add), ms_ready)
                dve.wait_ge(std_ready, l + 1)
                step(v.reciprocal(r, r))
                step.join()
                tt(diag[:, 0:tiles], ident[:].unsqueeze(1).broadcast_to([P, tiles, P]), mult,
                   rms[:, 0:tiles, 0:1].broadcast_to([P, tiles, P]), diag_ready)
                dve.wait_ge(rstd_mm, l + 1)

            def reduce_arg(n, bank, b, f):
                src = ps[:, bank:bank + 2].rearrange("p a b -> p (a b)")[:, 0:n]
                a, k = mlp[0][:, 0:n], mlp[1][:, 0:n]
                step(v.tensor_scalar(a, src, b, f, add, mult))
                step.join()
                step(v.tensor_scalar(k, a, 1.0 / (2 * math.pi), ROUND, mult, add))
                step.join()
                step(v.tensor_scalar(k, k, ROUND, None, sub))
                for part in (TWO_PI_A, TWO_PI_B, TWO_PI_C):
                    step.join()
                    stt(a, k, -part, add, a)
                step.join()

            def even(src, z):
                tb, tc, te, td = room[:, 0:4], room[:, 4:8], room[:, 24:26], room[:, 26:28]
                tt(tb, src[:, 0:4], add, src[:, 4:8])
                tt(tc, src[:, 0:4], sub, src[:, 4:8])
                step.join()
                tt(te, tb[:, 0:2], add, tb[:, 2:4])
                tt(z[:, 2, 0], tb[:, 0], sub, tb[:, 2])
                tt(td[:, 0], tc[:, 1], sub, tc[:, 3])
                tt(td[:, 1], tc[:, 1], add, tc[:, 3])
                step.join()
                tt(z[:, 0, 0], te[:, 0], add, te[:, 1], bf)
                tt(z[:, 1, 0], te[:, 0], sub, te[:, 1], bf)
                tt(z[:, 2, 1], tb[:, 3], sub, tb[:, 1], bf)
                stt(z[:, 3, 0], td[:, 0], SQ5, add, tc[:, 0])
                stt(z[:, 3, 1], td[:, 1], -SQ5, sub, tc[:, 2], bf)
                stt(z[:, 4, 0], td[:, 0], -SQ5, add, tc[:, 0])
                stt(z[:, 4, 1], td[:, 1], -SQ5, add, tc[:, 2], bf)
                step.join()

            def odd(src, z):
                tp, tm, te = room[:, 0:3], room[:, 3:6], room[:, 6:8]
                tf, to, tg = room[:, 24:26], room[:, 26:28], room[:, 28:30]
                tt(tp, src[:, 1:4], sub, src[:, 7:4:-1])
                tt(tm, src[:, 1:4], add, src[:, 7:4:-1])
                step.join()
                stt(te[:, 0], tp[:, 1], SQ5, add, src[:, 0])
                stt(te[:, 1], tp[:, 1], -SQ5, add, src[:, 0])
                stt(tf[:, 0], tm[:, 1], SQ5, add, src[:, 4])
                stt(tf[:, 1], tm[:, 1], SQ5, sub, src[:, 4])
                mul(to[:, 0], tp[:, 0], C1)
                mul(to[:, 1], tp[:, 0], S1)
                mul(tg[:, 0], tm[:, 0], -S1)
                mul(tg[:, 1], tm[:, 0], -C1)
                step.join()
                stt(to[:, 0], tp[:, 2], S1, add, to[:, 0])
                stt(to[:, 1], tp[:, 2], -C1, add, to[:, 1])
                stt(tg[:, 0], tm[:, 2], -C1, add, tg[:, 0])
                stt(tg[:, 1], tm[:, 2], S1, add, tg[:, 1])
                step.join()
                for i in range(2):
                    tt(z[:, 5 + i, 0], te[:, i], add, to[:, i])
                    tt(z[:, 5 + i, 1], tg[:, i], sub, tf[:, i], bf)
                for i in range(2):
                    tt(z[:, 7 + i, 0], te[:, i], sub, to[:, i])
                    tt(z[:, 7 + i, 1], tg[:, i], add, tf[:, i], bf)
                step.join()

            def few(kc, kn, z):
                tt(z[:, 0, 0], kc[:, 0], add, kc[:, 1], bf)
                tt(z[:, 1, 0], kc[:, 0], sub, kc[:, 1], bf)
                mul(z[:, 2, 0], kn[:, 0], 1.0)
                mul(z[:, 2, 1], kn[:, 1], -1.0, bf)
                step.join()

            def back(y):
                r = room
                tt(r[:, 0:4].rearrange("p (a b) c -> p a b c", b=2), spec[:, 5:7], add, spec[:, 7:9])
                tt(r[:, 4:8].rearrange("p (a b) c -> p a b c", b=2), spec[:, 5:7], sub, spec[:, 7:9])
                tt(r[:, 8], spec[:, 0, 0], add, spec[:, 1, 0])
                tt(r[:, 9], spec[:, 0, 0], sub, spec[:, 1, 0])
                tt(r[:, 10:12], spec[:, 3], add, spec[:, 4])
                tt(r[:, 12:14], spec[:, 3], sub, spec[:, 4])
                step.join()
                tt(r[:, 14], r[:, 8], add, spec[:, 2, 0])
                tt(r[:, 15], r[:, 9], sub, spec[:, 2, 1])
                tt(r[:, 16], r[:, 8], sub, spec[:, 2, 0])
                tt(r[:, 17], r[:, 9], add, spec[:, 2, 1])
                tt(r[:, 18], r[:, 12], sub, r[:, 11])
                tt(r[:, 19], r[:, 12], add, r[:, 11])
                step.join()
                e = r[:, 20:28]
                tt(e[:, 0], r[:, 14], add, r[:, 10])
                tt(e[:, 4], r[:, 14], sub, r[:, 10])
                tt(e[:, 2], r[:, 16], sub, r[:, 13])
                tt(e[:, 6], r[:, 16], add, r[:, 13])
                stt(e[:, 1], r[:, 18], SQ5, add, r[:, 15])
                stt(e[:, 5], r[:, 18], -SQ5, add, r[:, 15])
                stt(e[:, 3], r[:, 19], -SQ5, add, r[:, 17])
                stt(e[:, 7], r[:, 19], SQ5, add, r[:, 17])
                step.join()
                pp, qp, rp, tp_ = (r[:, i] for i in range(4))
                pm, qm, rm, tm = (r[:, i] for i in range(4, 8))
                tt(r[:, 8], pp, add, rp)
                tt(r[:, 9], tm, sub, qm)
                tt(r[:, 10], pp, sub, rp)
                tt(r[:, 11], qm, add, tm)
                mul(r[:, 12], pm, C1)
                mul(r[:, 13], pm, S1)
                mul(r[:, 14], qp, S1)
                mul(r[:, 15], qp, C1)
                step.join()
                stt(r[:, 12], rm, S1, add, r[:, 12])
                stt(r[:, 13], rm, -C1, add, r[:, 13])
                stt(r[:, 14], tp_, C1, add, r[:, 14])
                stt(r[:, 15], tp_, -S1, add, r[:, 15])
                tt(r[:, 16], r[:, 10], sub, r[:, 11])
                tt(r[:, 17], r[:, 10], add, r[:, 11])
                step.join()
                tt(r[:, 18], r[:, 12], sub, r[:, 14])
                tt(r[:, 19], r[:, 12], add, r[:, 14])
                tt(r[:, 28], r[:, 13], sub, r[:, 15])
                tt(r[:, 29], r[:, 13], add, r[:, 15])
                tt(y[:, 0], e[:, 0], add, r[:, 8])
                tt(y[:, 4], e[:, 4], add, r[:, 9])
                stt(y[:, 2], r[:, 16], SQ5, add, e[:, 2])
                stt(y[:, 6], r[:, 17], -SQ5, add, e[:, 6])
                step.join()
                tt(y[:, 1], e[:, 1], add, r[:, 18])
                tt(y[:, 7], e[:, 7], sub, r[:, 19])
                tt(y[:, 3], e[:, 3], add, r[:, 28])
                tt(y[:, 5], e[:, 5], sub, r[:, 29])
                step.join()

            def network(l, layer, isctx, bank, n):
                dve.wait_ge(mlp_mm[l], 2 * isctx + layer + 1)
                if layer:
                    dve.wait_ge(hid_ready[l], 2 * isctx + 1)
                reduce_arg(n, bank, f_small[:, l, 2 * layer:2 * layer + 1], f_small[:, l, 2 * layer + 1:2 * layer + 2])
                a = mlp[0][:, 0:n]
                step(v.tensor_scalar(a, a, 3.1415925, -3.1415925, ALU.min, ALU.max), arg_ready[l])
                step.join()

            def hyena(l):
                nonlocal bf
                bf = bf_ready[l]
                taps = xn = wn = conv_n = back_n = 0
                for ji, (isctx, o, ns, nt) in enumerate(jobs(l)):
                    if o == 0 and isctx:
                        for layer in range(2):
                            network(l, layer, isctx, 2 * layer, nt * P)
                    dve.wait_ge(dec_in[l], 16 * (ji + 1))
                    for i in range(nt):
                        dve.wait_ge(tap_mm[l], taps + i + 1)
                        tt(room[:, 2 * i:2 * i + 2], ps[:, 4 + (taps + i) % 2].rearrange("p (a b) -> p a b", b=CH), mult,
                           decay[:, 2 * i:2 * i + 2], tap_ready[l])
                    taps += nt
                    dve.wait_ge(tsq_used[l], taps)
                    step(v.tensor_copy(k_rt, ps[:, 1, 0:CH]))
                    step.join()
                    tt(k_rt, k_rt, add, ps[:, 1, CH:2 * CH])
                    step.join()
                    step(v.tensor_scalar(k_rt, k_rt, 1e-6, None, add), en_ready[l])
                    dve.wait_ge(rt_ready[l], ji + 1)
                    dve.wait_ge(drow_in[l], 16 * (ji + 1))
                    step(v.reciprocal(k_s, k_rt))
                    tt(d_row[0:1], d_row[0:1], mult, k_rt[0:1])
                    step.join()
                    tt(room[0:1, 0], room[0:1, 0], add, d_row[0:1])
                    if isctx:
                        mul(k_s, k_s, 4.0)
                    step.join()
                    kc, kn = room[:, 16:16 + nt], room[:, nt:2 * nt]
                    tt(kc, room[:, 0:nt], add, room[:, nt:2 * nt])
                    step.join()
                    tt(kn, room[:, 0:nt], sub, room[:, nt:2 * nt])
                    step.join()
                    if isctx:
                        few(kc, kn, spec)
                    else:
                        even(kc, spec)
                        odd(kn, spec)
                    for s in range(ns):
                        dve.wait_ge(x_mm[l], xn + 1)
                        tt(khat[:, s], ps[:, xn % 2].rearrange("p (a b) -> p a b", b=CH), mult,
                           k_s.unsqueeze(1).broadcast_to([P, 2, CH]), x_taken[l])
                        xn += 1
                    step.join()
                    u = z_tm[:, NT:NT + NTC] if isctx else z_tm[:, 0:NT]
                    if ji == 0:
                        dve.wait_ge(tp_taken[l], 4 * len(time_tiles(l)))
                    if isctx:
                        few(u, u, spec)
                    else:
                        even(u, spec)
                        odd(u, spec)
                    for s in range(ns):
                        dve.wait_ge(x_mm[l], xn + 1)
                        if conv_n >= 2:
                            dve.wait_ge(y_part[l], 2 * (conv_n - 1))
                        x = ps[:, xn % 2].rearrange("p (a b) -> p a b", b=CH)
                        for part, sm in ((0, prod_ready[l]), (1, x_taken[l])):
                            tt(prod[:, conv_n % 2, part].rearrange("p (a b) -> p a b", b=CH), x, mult,
                               khat[:, s, part].unsqueeze(1).broadcast_to([P, 2, CH]), sm)
                        xn += 1
                        conv_n += 1
                    wn += ns
                    dve.wait_ge(w_taken[l], wn)
                    if isctx:
                        r = room
                        tt(r[:, 0], spec[:, 0, 0], add, spec[:, 1, 0])
                        tt(r[:, 1], spec[:, 0, 0], sub, spec[:, 1, 0])
                        step.join()
                        tt(u[:, 0], r[:, 0], add, spec[:, 2, 0])
                        tt(u[:, 1], r[:, 1], sub, spec[:, 2, 1])
                        step.join()
                    else:
                        back(u)
                    if o == 0:
                        x1 = x1_tm[:, NT:NT + NTC] if isctx else x1_tm[:, 0:NT]
                        tt(u, u, mult, x1)
                        step.join()
                    else:
                        step(v.memset(mark[:, 0:1], 0.0), yt_ready[l])
                        for gi, (b, t0, w) in enumerate(back_tiles(isctx)):
                            dve.wait_ge(yt_mm[l], back_n + 1)
                            dst = mix[:, b, t0 * P:(t0 + w) * P]
                            tt(dst, dst, mult, ps[:, 4 + gi % 2, 0:w * P], yt_taken[l])
                            back_n += 1
                step.join()
                step(v.memset(mark[:, 0:1], 0.0), hyena_done[l])
                step.join()

            def take_ada():
                tt(ada[:, 0, 0:N_EARLY], ps[:, 5, 0:2 * N_EARLY].rearrange("p (a b) -> p a b", b=2), add,
                   b_ada[:, 0, 0:N_EARLY].unsqueeze(2).broadcast_to([P, N_EARLY, 2]), ada_ready)
                step.join()



            def rope(l, blk, signal=None):
                dve.wait_ge(rope_in[l], 16)
                step(v.stream_shuffle(rope_t[:, 0], blk, [i ^ 16 for i in range(32)]))
                step.join()
                tt(rope_t[:, 1], rope_t[:, 0], mult, rope_cs[:, 1])
                tt(blk, blk, mult, rope_cs[:, 0])
                step.join()
                tt(blk, blk, add, rope_t[:, 1], signal)
                step.join()

            def lower_part(j):
                s = SPLIT[j] % RING
                dve.wait_ge(hi_made, j + 1)
                v.tensor_tensor(ring_r[:, s], ring[:, s], w_hi[:, j % 2], sub).then_inc(lo_made, 1)

            def attention(l):
                tiles = q_tiles(l)
                base, sinks, steps = before[l]
                nw = len(tiles)
                nu, per = 2 * nw, steps_of(tiles)

                def has_sink(k):
                    return tiles[k // 2][0] == "C"
                with dve.Fori(0, 3) as pr:
                    u0 = pr * nu + base
                    w0 = pr * nw + base // 2
                    own = [0]

                    def chain(ins):
                        ins.then_inc(unit_step, 1)
                        own[0] += 1

                    def join():
                        dve.wait_ge(unit_step, pr * per + (steps + own[0]))

                    def sinks_made(units):
                        dve.wait_ge(es_ready, pr * sinks_of(tiles, nu) + (sinks + sinks_of(tiles, units)))

                    def q_block(w):
                        _, qb, _, _, j, _, _ = tiles[w]
                        return mix[:, bass.ds(pr + qb, 1), j * P:(j + 1) * P].rearrange("p a b -> p (a b)")

                    def stage_q(w):
                        if w >= 2:
                            dve.wait_ge(s_ready, u0 + (2 * w - 2))
                        rows = [slice(64 * par, 64 * par + 64) for par in range(2)]
                        for par, r in enumerate(rows):
                            chain(v.tensor_scalar(q_hi[r, w % 2, par], q_block(w)[r], QSCALE, None, mult))
                        join()
                        for par, r in enumerate(rows):
                            v.scalar_tensor_tensor(out=q_lo[r, w % 2, par], in0=q_block(w)[r], scalar=QSCALE,
                                                   in1=q_hi[r, w % 2, par], op0=mult, op1=sub).then_inc(qst_ready, 1)

                    def softmax_in(k):
                        kind, _, _, _, j, first, n = tiles[k // 2]
                        par = k % 2
                        dve.wait_ge(s_ready, u0 + (k + 1))
                        if k >= 2:
                            dve.wait_ge(p_ready, u0 + (k - 1))
                            if has_sink(k - 2):
                                sinks_made(k - 1)
                        bank = 2 * (k % 2)
                        lo = sink[:, l, bass.ds(pr * 2 + par, 1)] if has_sink(k) else LOWEST
                        chain(v.tensor_scalar(s_sb[:, k % 2, 0:CTX], ps[:, bank + 1, P:P + CTX], 1.0, lo, mult, ALU.max,
                                              accum_out=stat[:, 2 + k % 2:3 + k % 2]))
                        c, m = stat[:, 2 + k % 2:3 + k % 2], stat[:, 4 + k % 2:5 + k % 2]
                        if n:
                            if kind == "A":
                                bias = t_inner[:, par] if n == 5 else \
                                    t_edge[:, par, (2 * (first - j) + 6) * GRID:(2 * (first - j) + 6) * GRID + n * P]
                            else:
                                bias = m_win[:, (first - j + 1) * P:(first - j + 1 + n) * P]
                            src = ps[:, bank:bank + 2].rearrange("p a b -> p (a b)")[:, 0:n * P]
                            chain(v.tensor_tensor_reduce(out=s_sb[:, k % 2, CTX:CTX + n * P], in0=src, in1=bias, scale=1.0,
                                                         scalar=LOWEST, op0=add, op1=ALU.max, accum_out=m))
                            join()
                            v.tensor_scalar(stat[:, k % 2:k % 2 + 1], m, c, -1.0, ALU.max, mult).then_inc(neg_ready, 1)
                        else:
                            join()
                            v.tensor_scalar(stat[:, k % 2:k % 2 + 1], c, -1.0, None, mult).then_inc(neg_ready, 1)

                    def take_pt(k):
                        half = (len(chunks(tiles[k // 2])) + 1) // 2
                        dve.wait_ge(pt_ready, u0 + (k + 1))
                        if k >= 2:
                            dve.wait_ge(o_ready, u0 + (k - 1))
                        v.tensor_copy(pt_sb[:, k % 2, 0:half * P], ps[:, 4, 0:half * P]).then_inc(pt_dve, 1)

                    def divide(w):
                        dve.wait_ge(o_ready, u0 + (2 * w + 2))
                        if w >= 2:
                            dve.wait_ge(ot_ready, w0 + (w - 1))
                        cols = slice(8 + (2 * w) % 4, 10 + (2 * w) % 4)
                        total = stat[:, cols]
                        if has_sink(2 * w):
                            sinks_made(2 * w + 2)
                            chain(v.tensor_tensor(stat[:, 16:18], total, stat[:, cols.start + 4:cols.stop + 4], add))
                            total = stat[:, 16:18]
                            join()
                        chain(v.reciprocal(stat[:, 18:20], total))
                        join()
                        for par in range(2):
                            v.tensor_scalar(o_sb[:, w % 2, par * HD:(par + 1) * HD], ps[:, 6 + w % 2, par * HD:(par + 1) * HD],
                                            stat[:, 18 + par:19 + par], None, mult).then_inc(on_ready, 1)

                    def take_o(w):
                        dve.wait_ge(ot_ready, w0 + (w + 1))
                        v.tensor_scalar(q_block(w), ps[:, 6 + w % 2, P:2 * P], 1.0, None, mult).then_inc(ot_taken, 1)

                    stage_q(0)
                    stage_q(1)
                    dve.wait_ge(masks_in[l], 16 * 3)
                    dve.wait_ge(traw_in[l], 16 * 12)
                    raw = t_raw[:, bass.ds(pr * 2, 2)].rearrange("p h a b -> p (h a) b")
                    chain(v.tensor_tensor(t_edge.rearrange("p h (a b) -> p (h a) b", b=GRID), raw,
                                          m_cols.unsqueeze(1).broadcast_to([P, 28, GRID]), add))
                    join()
                    softmax_in(0)
                    softmax_in(1)
                    chain(v.tensor_tensor(t_inner, t_edge[:, :, 128:768], m_rows.unsqueeze(1).broadcast_to([P, 2, 640]), add))
                    for k in range(nu):
                        if 1 < k + 1 < nu:
                            softmax_in(k + 1)
                        take_pt(k)
                        if k % 2 and k // 2 + 2 < nw:
                            stage_q(k // 2 + 2)
                        if k >= 2 and k % 2 == 0:
                            divide(k // 2 - 1)
                        if k >= 3 and k % 2:
                            take_o(k // 2 - 1)
                    divide(nw - 1)
                    take_o(nw - 1)
                    assert own[0] == per

            bf = None
            for l in L2:
                n = ntok(l)
                if l == 0:
                    for k in range(1, KC):
                        add_squares(l, n, k)
                    dve.wait_ge(consts_in, 16 * 6)
                    dve.wait_ge(early_done, KC)
                    take_ada()
                step(v.scalar_tensor_tensor(out=mod_a[:], in0=ada[:, l, KC:2 * KC], scalar=1.0,
                                            in1=norm_g[:, l].unsqueeze(2).broadcast_to([P, KC, 2]), op0=add, op1=mult))
                norm(l, TOK)
                if l:
                    dve.wait_ge(x_stored, 16 * KC)
                for k in range(KC):
                    for c, (t0, t1) in enumerate(((0, SEQ), (SEQ, TOK))):
                        stt(act_t[:, k, t0:t1], act_t[:, k, t0:t1], mod_a[:, k, c:c + 1], mult, rstd[:, t0:t1], scaled[l])
                step.join()

                for layer in range(2):
                    network(l, layer, False, 6, SEQ)

                w = TOK + 2 if l == 0 else SEQ
                step.at[block_taken.name] = taken_before(l, "pb")
                for b in range(N_PB):
                    dve.wait_ge(pc_ready[l], (b + 1) * (2 if l == 0 else 1))
                    if b >= 2:
                        dve.wait_ge(tp_ready[l], len(time_tiles(l)) * min(b - 1, 4))
                    x, y = pc_in[:, b % 2], pc_out[:, b % 2]
                    cw = [conv_w[:, l, b, i:i + 1] for i in range(4)]
                    step(v.tensor_scalar(y[:, 1:1 + w], x[:, 1:1 + w], cw[1], cw[3], mult, add), block_taken)
                    step.join()
                    stt(y[:, 1:1 + w], x[:, 0:w], cw[0], add, y[:, 1:1 + w])
                    step.join()
                    if b < 4:
                        stt(y[:, 1:1 + w], x[:, 2:2 + w], cw[2], add, y[:, 1:1 + w], conv_ready[l])
                    else:
                        if l == 0:
                            stt(mix[:, b - 4, SEQ:TOK], x[:, SEQ + 4:SEQ + 4 + CTX], cw[2], add, y[:, SEQ + 3:SEQ + 3 + CTX])
                        stt(mix[:, b - 4, 0:SEQ], x[:, 2:2 + SEQ], cw[2], add, y[:, 1:1 + SEQ], conv_ready[l])
                    step.join()

                hyena(l)

                dve.wait_ge(g_taken[l], len(fillers(l)))
                dve.wait_ge(block_done, STREAM_AT[l, "v", 0])
                for k in range(KC):
                    dve.wait_ge(h_hi_made[l], k + 1)
                    tt(act_r[:, k], act_t[:, k], sub, h_hi[:, k], h_split[l])

                first, blocks = split_before(l, "k"), [("k", b) for b in range(N_K)] + [("q", b) for b in range(N_Q)]
                lower_part(first)
                lower_part(first + 1)
                for j, (stage, b) in enumerate(blocks):
                    dve.wait_ge(block_done, STREAM_AT[l, stage, b] + 1)
                    dst = k_fm[:, b] if stage == "k" else mix[:, MIX_C + b if b < 3 else MIX_A + b - 3]
                    width = TOK if stage == "k" else n
                    src = ps[:, 3 * (j % 2):3 * (j % 2) + 3].rearrange("p a b -> p (a b)")
                    v.tensor_scalar(dst[:, 0:width], src[:, 0:width], 1.0, None, mult).then_inc(block_taken, 1)
                    if j + 2 < len(blocks):
                        lower_part(first + j + 2)
                    if (stage, b) == ("k", N_K - 1) or stage == "q" and b < 3:
                        dve.wait_ge(block_taken, taken_before(l, "k") + j + 1)
                        rope(l, dst[:, 0:SEQ], rope_done[l] if (stage, b) == ("q", 2) else None)
                dve.wait_ge(block_taken, taken_before(l, "out"))
                dve.wait_ge(k_hi_made, l + 1)
                v.tensor_tensor(k_lo[:, 0], k_fm[:, 0], k_hi[:, 0], sub).then_inc(k_split, 1)
                dve.wait_ge(qst_zero, l + 1)
                attention(l)

                first = split_before(l, "out")
                lower_part(first)
                for k in range(KC):
                    dve.wait_ge(mix_hi_made[l], k + 1)
                    tt(mix_r[:, k, 0:n], mix[:, k, 0:n], sub, mix_hi(k)[:, 0:n], mix_split[l])
                    if k == 0:
                        lower_part(first + 1)
                for m in range(KC):
                    dve.wait_ge(block_done, STREAM_AT[l, "out", m] + 1)
                    dve.wait_ge(xin_in[l][m % 2], 16 * (m // 2 + 1))
                    src = ps[:, 3 * (m % 2):3 * (m % 2) + 3].rearrange("p a b -> p (a b)")
                    if l == 0:
                        stt(act_t[:, m, SEQ:TOK], src[:, SEQ:TOK], ada[:, l, 2 * KC + m, 1:2], add, x_in[:, m % 2, SEQ:TOK])
                    v.scalar_tensor_tensor(out=act_t[:, m, 0:SEQ], in0=src[:, 0:SEQ], scalar=ada[:, l, 2 * KC + m, 0:1],
                                           in1=x_in[:, m % 2, 0:SEQ], op0=mult, op1=add).then_inc(block_taken, 1)
                    if m + 2 < N_OUT:
                        lower_part(first + m + 2)
                    if m > 1:
                        add_squares(l + 1, n, m - 1)
                add_squares(l + 1, n, KC - 1)
            norm(DEPTH, SEQ)
            for m in range(KC):
                stt(fin[:, m], act_t[:, m, 0:SEQ], norm_g[:, DEPTH, m:m + 1], mult, rstd[:, 0:SEQ], fin_ready)


def lay_out(i):
    f = np.float32
    i = {k: np.asarray(v, f) for k, v in i.items()}
    o = {}
    blocks = lambda w, cols: [w[:, c].reshape(KC, P, P).transpose(1, 0, 2).reshape(P, KC * P) for c in cols]
    rng = lambda a, n: [np.arange(a + P * b, a + P * b + P) for b in range(n)]
    heads = lambda a: [np.concatenate([np.arange(a + HD * h, a + HD * h + HD) for h in C_HEAD_ORDER[p:p + 2]])
                       for p in (0, 2, 4)]
    per = []
    rows = np.concatenate(rng(384, 2) + rng(0, 3) + heads(640))
    columns = {"ada": rng(0, N_ADA), "pb": rng(1536, 6), "q": heads(2560) + rng(0, 3), "k": rng(384, 3) + rng(2944, 1),
               "g": rng(2304, 2) + rng(1152, 3) + heads(3200), "out": rng(0, 8)}
    for l, name, b in STREAM:
        if name == "v":
            w = i["w_in"][l]
            wv = np.concatenate([w[:, 768:1152], w[:, 3072:3200]], 1).reshape(KC, P, 512).transpose(1, 0, 2)
            per.append(wv[:, 2 * b:2 * b + 2].reshape(P, 1024))
        else:
            w = i["w_ada"][l] if name == "ada" else i["w_out"][l][rows] if name == "out" else i["w_in"][l]
            per += blocks(w, [columns[name][b]])
    early = np.stack(blocks(i["w_ada"][0], columns["ada"][:N_EARLY])).reshape(KC, 2, P, KC * P)
    o["early"] = early.transpose(0, 2, 1, 3).reshape(KC, P, 2 * KC * P)
    o["weights"] = np.stack(per)
    col = lambda a, n: a.reshape(n, P).T
    x = np.concatenate([i["x"][0], i["ctx"][0]], 0).T
    o["x_blocks"] = x.reshape(KC, P, TOK)
    o["cond"] = np.stack([col(i["c"][0], KC), col(i["c_ctx"], KC)], 2)
    o["norm_g"] = np.stack([col(i["norm_g"][l], KC) for l in range(DEPTH)] + [col(i["final_g"], KC)], 1)
    o["b_ada"] = np.stack([col(i["b_ada"][l], N_ADA) for l in range(DEPTH)], 1)
    o["conv_w"] = np.stack([np.stack([col(i["hy_conv_w"][l, t], 6) for t in range(3)] + [col(i["hy_conv_b"][l], 6)], 2)
                            for l in range(DEPTH)], 1)
    two = lambda a: np.concatenate([a, a])
    o["f_small"] = np.stack([np.stack([two(i[n][l]) for n in ("hy_b1", "hy_freq1", "hy_b2", "hy_freq2")], 1)
                             for l in range(DEPTH)], 1)
    o["sink"] = np.broadcast_to(i["sink"][None][:, :, list(C_HEAD_ORDER)], (P, DEPTH, 6))
    w12 = np.zeros((DEPTH, P, 2, P), f)
    w3 = np.zeros((DEPTH, 2, P, 512), f)
    for l in range(DEPTH):
        for e in range(2):
            w12[l, 33 * e:33 * e + 33, 0, 64 * e:64 * e + 64] = i["hy_w1"][l]
            w12[l, 64 * e:64 * e + 64, 1, 64 * e:64 * e + 64] = i["hy_w2"][l]
            w3[l, e, 64 * e:64 * e + 64] = i["hy_w3"][l][:, 512 * e:512 * e + 512]
    o["w12"], o["w3"] = w12, w3
    o["hy_d"] = i["hy_d"]
    rel = np.arange(GRID)[None, :] - np.arange(GRID)[:, None] + 15
    padded = np.concatenate([i["na_rpb"], np.zeros(i["na_rpb"].shape[:3] + (1,), f)], 3)
    rel = np.where((rel < 0) | (rel > 30), 31, rel)
    o["rpb"] = padded[:, :, :, rel].transpose(0, 1, 3, 2, 4)
    o["ident"] = np.eye(P, dtype=f)
    o["dft_f"], o["dft_i"] = dft_tables()
    o["rope"] = np.stack(rope_tables(), 1)
    o["m_cols"], o["m_rows"], o["m_win"] = attention_masks()
    o["feats"], o["decay"] = filter_tables(SEQ)
    o["feats_ctx"], o["decay_ctx"] = filter_tables(CTX)
    return {k: np.ascontiguousarray(v, f) for k, v in o.items()}


def kernel(**inputs):
    import concourse.bacc as bacc
    from concourse.bass_utils import run_bass_kernel_spmd

    arrays = lay_out(inputs)
    nc = bacc.Bacc("TRN2", target_bir_lowering=False, num_devices=1)
    aps = {k: nc.dram_tensor(f"in_{k}", v.shape, F32, kind="ExternalInput").ap() for k, v in arrays.items()}
    aps["x_mid"] = nc.dram_tensor("x_mid", (KC, P, TOK), F32, kind="Internal").ap()
    aps["gates"] = nc.dram_tensor("gates", (N_G, P, TOK), F32, kind="Internal").ap()
    aps["out"] = nc.dram_tensor("out_fm", (KC, P, SEQ), F32, kind="ExternalOutput").ap()
    build(nc, aps)
    r = run_bass_kernel_spmd(nc, [{f"in_{k}": v for k, v in arrays.items()}], core_ids=[0])
    return np.ascontiguousarray(r.results[0]["out_fm"].reshape(D, SEQ).T)[None]
```
